# Optimizing a Trainium2 kernel written in Bass

```python
import jax, jax.numpy as jnp
from jax import lax
import numpy as np

D_MODEL = 2048
BATCH = 1
SEQ = 256
DEPTH = 1
DEC_BATCH = 8
DEC_SEQ = 16
PAST_LEN = 128

CHUNK = 64
Q_BLOCK = 128
NORM_EPS = 1e-6

RWKV_HEAD = 64
RWKV_HEADS = 16
RWKV_WIDTH = RWKV_HEADS * RWKV_HEAD
DECAY_LORA = 96
AAA_LORA = 96
GATE_LORA = 256
GN_EPS = 64e-5
RWKV_PROJ = 3 * RWKV_WIDTH + DECAY_LORA + AAA_LORA + GATE_LORA

MLA_HEADS = 8
QK_NOPE = 128
QK_ROPE = 64
V_HEAD = 128
KV_LORA = 512
ROPE_THETA = 10000.0
MLA_Q_WIDTH = MLA_HEADS * (QK_NOPE + QK_ROPE)
MLA_PROJ = MLA_Q_WIDTH + KV_LORA + QK_ROPE
MLA_WIDTH = MLA_HEADS * V_HEAD
SOFTMAX_SCALE = (QK_NOPE + QK_ROPE) ** -0.5
NEG_INF = -1e30

GATE_PROJ = 2 * D_MODEL
IN_PROJ = RWKV_PROJ + MLA_PROJ + GATE_PROJ

D_FF = 5632
CONV_W = 3

kernel_name = 'rwkv7_mla_convglu_streaming_step'

def rmsnorm(x, g):
    xf = x.astype(jnp.float32)
    y = xf * lax.rsqrt(jnp.mean(xf * xf, axis=-1, keepdims=True) + NORM_EPS)
    return (y * g.astype(jnp.float32)).astype(x.dtype)

def rope(x, pos):
    half = QK_ROPE // 2
    inv = ROPE_THETA ** (-jnp.arange(half, dtype=jnp.float32) / half)
    ang = pos.astype(jnp.float32)[:, None] * inv[None, :]
    shp = (pos.shape[0],) + (1,) * (x.ndim - 3) + (half,)
    cos, sin = jnp.cos(ang).reshape(shp), jnp.sin(ang).reshape(shp)
    xf = x.astype(jnp.float32)
    x1, x2 = xf[..., :half], xf[..., half:]
    return jnp.concatenate([x1 * cos - x2 * sin, x1 * sin + x2 * cos], axis=-1).astype(x.dtype)

def rwkv7_mix(p_a, prev_row, wkv0, mu_shift, w0, w2, a0, a2, g2, k_k, k_a, r_k, lnx_g, lnx_b, w_o_a):
    B, T, _ = p_a.shape
    H, N, W = RWKV_HEADS, RWKV_HEAD, RWKV_WIDTH
    f32 = jnp.float32
    p_prev = jnp.concatenate([prev_row.astype(p_a.dtype), p_a[:, :-1]], axis=1)
    z = p_a + mu_shift * (p_prev - p_a)
    r, k, v, zw, za, zg = jnp.split(z, [W, 2 * W, 3 * W, 3 * W + DECAY_LORA, 3 * W + DECAY_LORA + AAA_LORA], axis=-1)
    w_raw = (w0 + jnp.tanh(zw) @ w2).astype(f32)
    decay = jnp.exp(-jnp.exp(-jax.nn.softplus(-w_raw) - 0.5))
    a = jax.nn.sigmoid((a0 + za @ a2).astype(f32))
    g = jax.nn.sigmoid(zg) @ g2
    r, k, v = r.astype(f32), k.astype(f32), v.astype(f32)
    kk = (k * k_k).reshape(B, T, H, N)
    kk = kk * lax.rsqrt(jnp.maximum(jnp.sum(kk * kk, axis=-1, keepdims=True), 1e-12))
    k = k * (1.0 + (a - 1.0) * k_a)
    heads = lambda t: t.reshape(B, T, H, N)
    r, k, v, decay, a = heads(r), heads(k), heads(v), heads(decay), heads(a)

    def step(S, inp):
        r_t, w_t, k_t, v_t, kk_t, a_t = inp
        sa = jnp.einsum('bhvk,bhk->bhv', S, kk_t)
        S = (S * w_t[:, :, None, :] + v_t[..., None] * k_t[:, :, None, :]
             - sa[..., None] * (kk_t * a_t)[:, :, None, :])
        return S, jnp.einsum('bhvk,bhk->bhv', S, r_t)

    seq_first = lambda t: jnp.swapaxes(t, 0, 1)
    S_T, y = lax.scan(step, wkv0.astype(f32), (seq_first(r), seq_first(decay), seq_first(k),
                                                seq_first(v), seq_first(kk), seq_first(a)))
    y = seq_first(y)
    mu = jnp.mean(y, axis=-1, keepdims=True)
    var = jnp.mean(jnp.square(y - mu), axis=-1, keepdims=True)
    y = ((y - mu) * lax.rsqrt(var + GN_EPS)).reshape(B, T, W) * lnx_g + lnx_b
    bonus = jnp.sum(r * k * r_k, axis=-1, keepdims=True) * v
    y = (y + bonus.reshape(B, T, W)) * g
    return y.astype(p_a.dtype) @ w_o_a, S_T, p_a[:, -1:]

def mla_project(p_b, pos, g_kv):
    B, T, _ = p_b.shape
    q, c_kv, k_r = jnp.split(p_b, [MLA_Q_WIDTH, MLA_Q_WIDTH + KV_LORA], axis=-1)
    q = q.reshape(B, T, MLA_HEADS, QK_NOPE + QK_ROPE)
    return q[..., :QK_NOPE], rope(q[..., QK_NOPE:], pos), rmsnorm(c_kv, g_kv), rope(k_r, pos)

def mla_expand(c_kv, w_ukv):
    B, S, _ = c_kv.shape
    kv = (c_kv @ w_ukv).reshape(B, S, MLA_HEADS, QK_NOPE + V_HEAD)
    return kv[..., :QK_NOPE], kv[..., QK_NOPE:]

def attend(q_nope, q_rope, k_nope, k_rope, v, mask):
    s = jnp.einsum('bqhd,bkhd->bhqk', q_nope, k_nope) + jnp.einsum('bqhr,bkr->bhqk', q_rope, k_rope)
    s = s.astype(jnp.float32) * SOFTMAX_SCALE
    if mask is not None:
        s = jnp.where(mask[None, None], s, NEG_INF)
    p = jax.nn.softmax(s, axis=-1).astype(v.dtype)
    return jnp.einsum('bhqk,bkhd->bqhd', p, v)

def mla_prompt_attention(q_nope, q_rope, k_nope, k_rope, v):
    T = q_nope.shape[1]
    outs = []
    for start in range(0, T, Q_BLOCK):
        stop = start + Q_BLOCK
        q_chunk = (start + jnp.arange(Q_BLOCK)) // CHUNK
        k_chunk = jnp.arange(stop) // CHUNK
        mask = k_chunk[None, :] <= q_chunk[:, None]
        outs.append(attend(q_nope[:, start:stop], q_rope[:, start:stop],
                           k_nope[:, :stop], k_rope[:, :stop], v[:, :stop], mask))
    return jnp.concatenate(outs, axis=1)

def hybrid_layer(x, pos, shift_prev, wkv0, conv_prev, past_latent, past_krope, lp):
    B, T, _ = x.shape
    xn = rmsnorm(x, lp['g_mix'])
    proj = xn @ lp['w_in']
    p_a, p_b, p_g = jnp.split(proj, [RWKV_PROJ, RWKV_PROJ + MLA_PROJ], axis=-1)
    y_a, wkv_new, shift_new = rwkv7_mix(p_a, shift_prev, wkv0, lp['mu_shift'], lp['w0'], lp['w2'],
                                        lp['a0'], lp['a2'], lp['g2'], lp['k_k'], lp['k_a'], lp['r_k'],
                                        lp['lnx_g'], lp['lnx_b'], lp['w_o_a'])
    q_nope, q_rope, c_kv, k_rope = mla_project(p_b, pos, lp['g_kv'])
    if past_latent is None:
        k_nope, v = mla_expand(c_kv, lp['w_ukv'])
        o = mla_prompt_attention(q_nope, q_rope, k_nope, k_rope, v)
    else:
        lat = jnp.concatenate([past_latent.astype(c_kv.dtype), c_kv], axis=1)
        kr = jnp.concatenate([past_krope.astype(k_rope.dtype), k_rope], axis=1)
        k_nope, v = mla_expand(lat, lp['w_ukv'])
        o = attend(q_nope, q_rope, k_nope, kr, v, None)
    y_b = o.reshape(B, T, MLA_WIDTH) @ lp['w_o_b']
    gate_a, gate_b = jnp.split(jax.nn.sigmoid(p_g), 2, axis=-1)
    h = x + (gate_a * y_a + gate_b * y_b) @ lp['w_out']
    hn = rmsnorm(h, lp['g_ffn'])
    gate, up = jnp.split(hn @ lp['w_ffn_in'], 2, axis=-1)
    gate_ext = jnp.concatenate([conv_prev.astype(gate.dtype), gate], axis=1)
    cw = lp['conv_w']
    gate_c = sum(gate_ext[:, j:j + T] * cw[j] for j in range(CONV_W)) + lp['conv_b']
    h = h + (jax.nn.silu(gate_c) * up) @ lp['w_ffn_down']
    return h, c_kv, k_rope, wkv_new, shift_new, gate_ext[:, T:]

def setup_inputs(seed: int = 0) -> dict:
    key = jax.random.key(seed)
    ks = iter(jax.random.split(key, 40))
    nrm = lambda shape, scale: jax.random.normal(next(ks), shape, jnp.float32) * scale
    L, W, H, N = DEPTH, RWKV_WIDTH, RWKV_HEADS, RWKV_HEAD
    return {
        'x_prompt': nrm((BATCH, SEQ, D_MODEL), 1.0),
        'x_sample': nrm((DEC_BATCH, DEC_SEQ, D_MODEL), 1.0),
        'cache_mla_latent': nrm((L, DEC_BATCH, PAST_LEN, KV_LORA), 1.0),
        'cache_mla_krope': nrm((L, DEC_BATCH, PAST_LEN, QK_ROPE), 1.0),
        'state_rwkv_wkv': nrm((L, DEC_BATCH, H, N, N), 0.3),
        'state_rwkv_shift': nrm((L, DEC_BATCH, 1, RWKV_PROJ), 1.0),
        'state_ffn_conv': nrm((L, DEC_BATCH, CONV_W - 1, D_FF), 1.0),
        'g_mix': 1.0 + nrm((L, D_MODEL), 0.02),
        'w_in': nrm((L, D_MODEL, IN_PROJ), D_MODEL ** -0.5),
        'mu_shift': jax.random.uniform(next(ks), (L, RWKV_PROJ), jnp.float32),
        'w0': jax.random.uniform(next(ks), (L, W), jnp.float32, -5.0, 1.0),
        'w2': nrm((L, DECAY_LORA, W), DECAY_LORA ** -0.5),
        'a0': nrm((L, W), 0.3),
        'a2': nrm((L, AAA_LORA, W), AAA_LORA ** -0.5),
        'g2': nrm((L, GATE_LORA, W), GATE_LORA ** -0.5),
        'k_k': 0.85 + nrm((L, W), 0.05),
        'k_a': 1.0 + nrm((L, W), 0.05),
        'r_k': nrm((L, H, N), 0.1),
        'lnx_g': 1.0 + nrm((L, W), 0.02),
        'lnx_b': nrm((L, W), 0.02),
        'w_o_a': nrm((L, W, D_MODEL), W ** -0.5),
        'g_kv': 1.0 + nrm((L, KV_LORA), 0.02),
        'w_ukv': nrm((L, KV_LORA, MLA_HEADS * (QK_NOPE + V_HEAD)), KV_LORA ** -0.5),
        'w_o_b': nrm((L, MLA_WIDTH, D_MODEL), MLA_WIDTH ** -0.5),
        'w_out': nrm((L, D_MODEL, D_MODEL), D_MODEL ** -0.5),
        'g_ffn': 1.0 + nrm((L, D_MODEL), 0.02),
        'w_ffn_in': nrm((L, D_MODEL, 2 * D_FF), D_MODEL ** -0.5),
        'conv_w': nrm((L, CONV_W, D_FF), CONV_W ** -0.5),
        'conv_b': nrm((L, D_FF), 0.02),
        'w_ffn_down': nrm((L, D_FF, D_MODEL), D_FF ** -0.5),
        'g_final': 1.0 + nrm((D_MODEL,), 0.02),
    }

def reference(x_prompt, x_sample, cache_mla_latent, cache_mla_krope, state_rwkv_wkv, state_rwkv_shift,
              state_ffn_conv, g_mix, w_in, mu_shift, w0, w2, a0, a2, g2, k_k, k_a, r_k, lnx_g, lnx_b,
              w_o_a, g_kv, w_ukv, w_o_b, w_out, g_ffn, w_ffn_in, conv_w, conv_b, w_ffn_down, g_final):
    B, T, _ = x_prompt.shape
    Ts = x_sample.shape[1]
    past = cache_mla_latent.shape[2]
    pos_p = jnp.arange(T)
    pos_s = past + jnp.arange(Ts)
    dt = x_prompt.dtype
    h_p, h_s = x_prompt, x_sample
    st_p, st_s = [], []
    for l in range(DEPTH):
        lp = dict(g_mix=g_mix[l], w_in=w_in[l], mu_shift=mu_shift[l], w0=w0[l], w2=w2[l], a0=a0[l],
                  a2=a2[l], g2=g2[l], k_k=k_k[l], k_a=k_a[l], r_k=r_k[l], lnx_g=lnx_g[l], lnx_b=lnx_b[l],
                  w_o_a=w_o_a[l], g_kv=g_kv[l], w_ukv=w_ukv[l], w_o_b=w_o_b[l], w_out=w_out[l],
                  g_ffn=g_ffn[l], w_ffn_in=w_ffn_in[l], conv_w=conv_w[l], conv_b=conv_b[l],
                  w_ffn_down=w_ffn_down[l])
        zero_shift = jnp.zeros((B, 1, RWKV_PROJ), dt)
        zero_wkv = jnp.zeros((B, RWKV_HEADS, RWKV_HEAD, RWKV_HEAD), jnp.float32)
        zero_conv = jnp.zeros((B, CONV_W - 1, D_FF), dt)
        h_p, *sp = hybrid_layer(h_p, pos_p, zero_shift, zero_wkv, zero_conv, None, None, lp)
        h_s, *ss = hybrid_layer(h_s, pos_s, state_rwkv_shift[l], state_rwkv_wkv[l], state_ffn_conv[l],
                                cache_mla_latent[l], cache_mla_krope[l], lp)
        st_p.append(sp)
        st_s.append(ss)
    y_prompt = rmsnorm(h_p, g_final)
    y_sample = rmsnorm(h_s, g_final)
    stk = lambda outs, i: jnp.stack([o[i] for o in outs]).astype(dt)
    return (y_prompt, y_sample,
            stk(st_p, 0), stk(st_p, 1), stk(st_p, 2), stk(st_p, 3), stk(st_p, 4),
            stk(st_s, 0), stk(st_s, 1), stk(st_s, 2), stk(st_s, 3), stk(st_s, 4))


_drawn_inputs = setup_inputs


def setup_inputs(seed=0):
    import zlib

    import numpy as np

    out = dict(_drawn_inputs(seed))
    spreads = {}
    factors = {'lnx_g': 8.0,
     'lnx_b': 8.0,
     'g_kv': 2.941,
     'g_ffn': 2.737,
     'conv_b': 5.719,
     'g_final': 2.771}
    for name, (base, spread) in spreads.items():
        noise = np.random.default_rng([zlib.crc32(name.encode()), seed]).standard_normal(out[name].shape)
        drawn = base * np.exp(spread * noise) if base else spread * noise
        out[name] = __import__('jax').numpy.asarray(drawn.astype(out[name].dtype))
    for name, factor in factors.items():
        out[name] = (out[name] * factor).astype(out[name].dtype)
    return out
```

```python
from contextlib import ExitStack, contextmanager

import concourse.bass as bass
from concourse import mybir

F32 = mybir.dt.float32
F32R = mybir.dt.float32r
ALU = mybir.AluOpType
ACT = mybir.ActivationFunctionType
AX = mybir.AxisListType.X

P = 128
D = 2048
NT = 384
NP_ = 256
NB, TS = 8, 16
KD = D // P
W = 1024
FT = W // P
RW = 3520
Q0 = RW
CKV0 = Q0 + 1536
KR0 = CKV0 + 512
G0 = RW + 2112
DFF = 5632
NJ = DFF // P
HJ = NJ // 2
PAST = 128
LAT = 512
SCALE = 192.0 ** -0.5
EPS = 1e-6
GN_EPS = 64e-5
CDEC = 0.6065306597126334
PAD = 257 + NB * 17

C1 = ["ident", "ones"]
C2 = ["bones", "st64", "in64", "st16", "in16", "nl1", "nl1t", "lv2", "lv4", "lv8", "lv16", "lv32"]
C3 = ["rot"]
NC1 = len(C1) * P
NC2 = len(C2) * P + NT + 8
NC3 = P + 3 * NT

T_LORA = 0
T_FT = 4
T_MLA = T_FT + 4 * FT
T_MIX = T_MLA + 9
T_OUT = T_MIX + 3 * KD
T_FFN = T_OUT + KD
T_HALF = 2 * HJ + HJ
T_END = T_FFN + 2 * T_HALF


def constants():
    import numpy as np
    f = np.float32
    s, t = np.arange(P)[:, None], np.arange(P)[None, :]
    m = {"ident": s == t, "ones": s >= 0 * t, "bones": s // 64 == t // 64}
    for c in (64, 16):
        same = s // c == t // c
        m[f"st{c}"], m[f"in{c}"] = same & (s < t), same & (s <= t)
    level = lambda n: (s // (2 * n) == t // (2 * n)) & (s % (2 * n) < n) & (t % (2 * n) >= n)
    m["nl1"] = -level(1).astype(f)
    m["nl1t"] = m["nl1"].T
    for n in (2, 4, 8, 16, 32):
        m[f"lv{n}"] = level(n)
    rot = np.zeros((P, P), f)
    for b in (0, 64):
        for j in range(32):
            rot[b + j + 32, b + j] = -1
            rot[b + j, b + j + 32] = 1
    m["rot"] = rot
    cat = lambda names: [np.broadcast_to(m[n], (P, P)).astype(f) for n in names]
    tok = np.arange(NT)
    first = np.where(tok < NP_, tok % 64 == 0, tok % 16 == 0)
    reset = np.broadcast_to(1 - first.astype(f), (P, NT))
    bm = (s // 16 == np.arange(8)[None]).astype(f)
    half = 32
    inv = (f(10000.0) ** (-np.arange(half, dtype=f) / f(half))).astype(f)
    pos = np.where(tok < NP_, tok, PAST + tok % 16).astype(f)
    ang = (pos[None, :] * inv[np.arange(P) % half][:, None]).astype(f)
    key = np.concatenate([np.arange(128), np.arange(256)])[None]
    q = np.where(np.arange(NT)[None] < 128, s, 128 + s)
    amask = np.where(key // 64 <= q // 64, 0, -1e30)
    out = cat(C1) + cat(C2) + [reset, bm] + cat(C3) + [np.cos(ang), np.sin(ang), amask]
    return np.ascontiguousarray(np.concatenate([np.asarray(a, f) for a in out], 1))


class Chain:

    def __init__(self, eng, sem):
        self.eng, self.sem, self.base, self.k = eng, sem, 0, 0

    def link(self, ins):
        ins.then_inc(self.sem, 1)
        self.k += 1
        self.eng.wait_ge(self.sem, self.base + self.k)

    @contextmanager
    def loop(self, count, steps):
        base, k = self.base, self.k
        with self.eng.Fori(0, count) as i:
            self.base, self.k = i * steps + (base + k), 0
            yield i
            assert self.k == steps, f"the body links {self.k} times"
        self.base, self.k = base, k + count * steps


def build(nc, a, consts, outs):
    (y_prompt, y_sample, lat_p, kr_p, wkv_p, shift_p, conv_p,
     lat_s, kr_s, wkv_s, shift_s, conv_s) = outs
    ctx = ExitStack()
    sems = {}

    def sem(name):
        if name not in sems:
            sems[name] = ctx.enter_context(nc.semaphore(name))
        return sems[name]

    BASE = 16512
    top = [BASE]

    def at(name, shape, off, dt=F32):
        size = 4
        for n in shape[1:]:
            size *= n
        assert off % 32 == 0 and off + size <= 229368, (name, off, size)
        return nc.alloc_sbuf_tensor_at(name, shape, dt, offset=off)

    def region(name, shape, dt=F32):
        off = top[0]
        size = 4
        for n in shape[1:]:
            size *= n
        top[0] = off + (size + 31) // 32 * 32
        return at(name, shape, off, dt)

    with ctx:
        raw = region("w_raw", [P, 2, 8, P])
        hi = region("w_hi", [P, 2, 8, P], F32R)
        lo = region("w_lo", [P, 2, 8, P], F32R)
        xh = region("x_hi", [P, KD, NT], F32R)
        xl = region("x_lo", [P, KD, NT], F32R)
        c1 = region("consts_all", [P, NC1])
        prm = region("params", [P, 120])
        cprm = region("conv_params", [P, 4, NJ])
        cprev = region("conv_prev", [P, NB, 2, NJ])
        shm = region("shift_rkv", [P, NB, 24])
        shl = region("shift_lora", [P, 4, NB])
        stat = region("row_stats", [P, 8])
        tail = region("proj_last_rkv", [P, 9, 24])
        taill = region("proj_last_lora", [P, 4, 9])
        ctail = region("conv_last", [P, 9, 2, NJ])
        area = top[0]
        ident, ones = c1[:, 0:P], c1[:, P:2 * P]

        qn = region("q_nope", [P, FT, NT])
        oa = region("rwkv_out", [P, FT, NT])
        phase = top[0]
        c2 = region("consts_rwkv", [P, NC2])
        cm = {n: c2[:, i * P:(i + 1) * P] for i, n in enumerate(C2)}
        reset = c2[:, len(C2) * P:len(C2) * P + NT]
        bmask = c2[:, len(C2) * P + NT:NC2]
        pb = region("proj_pad", [P, 3, PAD])
        db_off = top[0]
        db = region("proj_diff", [P, 3, PAD])
        vx = at("v_by_sequence", [P, 2, NB, 64], db_off)
        z = region("z", [P, 3, NT])
        wl = region("lora_w2a2", [P, 2, P])
        wg = region("lora_g2", [P, 2, P])
        za = region("z_lora", [P, 4, NT])
        pf = region("params_ft", [P, 10])
        mid = region("decay_mid", [P, 4, 2])
        emid = region("decay_mid_exp", [P, 4, 2])
        sw, aa, gg, cu, dx, e1, e2, e3, kk0, sq, rn, t1, k2, kka, rk = [
            region(n, [P, NT]) for n in ("sig_w", "a_gate", "g_gate", "cum_decay", "cum_excl", "exp_inc", "exp_inv",
                                         "exp_excl", "kk_raw", "square", "norm", "k_scale", "k_mod", "kk_a",
                                         "bonus")]
        al = region("alpha_pad", [P, 2, NT])
        rh = region("rho_pad", [P, 2, NT])
        be = region("beta", [P, NT])
        kp_ = region("kappa", [P, NT])
        n_t, t_x, t_y, t_g, m_t, c_k, c_b = [
            region(n, [P, 6, P]) for n in ("n_t", "t_x", "t_y", "t_g", "m_t", "c_k", "c_b")]
        tok = region("tok_major", [P, 3, 3, P])
        rr = region("r_rhs", [P, 2, P])
        un = region("u_neg", [P, 2, P])
        asd = region("alpha_s0", [P, P])
        s0l = region("s0_load", [64, NB, P])
        s0t = region("s0_t", [P, NB, 64])
        so = region("s_out", [64, NB, P])
        st = region("state", [P, 3, 64])
        sto = region("state_rows", [64, P])
        assert top[0] <= 229368, top[0]
        yb, yc = cu, dx
        x_off = (229368 - 4 * 3 * D) // 32 * 32
        xt = at("x_rows", [P, 3, D], x_off)
        rows = at("param_rows", [P, 14, P], area)
        junk = at("square_junk", [P, D], area + 12288)

        top[0] = phase
        obh = region("mla_out_hi", [P, FT, NT], F32R)
        obl = region("mla_out_lo", [P, FT, NT], F32R)
        after_ob = top[0]
        c3 = region("consts_mla", [P, NC3])
        rot, cos, sin, amask = c3[:, 0:P], c3[:, P:P + NT], c3[:, P + NT:P + 2 * NT], c3[:, P + 2 * NT:NC3]
        qrp = region("q_rope", [P, 4, NT])
        cc_off = top[0]
        cc = region("c_kv", [P, 4, NT])
        csq = region("c_square", [P, 4, NT])
        latt = region("latent_t", [P, 4, NT])
        kr2 = region("k_rope_t", [P, NT])
        rt_off = top[0]
        rtmp = region("rope_tmp", [P, 5, NT])
        crs = region("c_rstd", [P, NT])
        ltok = region("latent_rows", [P, 3, LAT])
        qld = region("q_latent_sample", [P, 4, 8, P])
        qrz = region("q_rope_sample", [P, 8, P])
        wuk = region("w_ukv_head", [P, 2, 4, 256])
        qlp = region("q_latent", [P, 4, NP_])
        msum = region("softmax_stats", [P, 8])
        lp = at("past_latent", [P, 2, LAT], cc_off)
        kpast = at("past_krope", [P, 2, 2, 64], cc_off + 4096)
        lnew = at("new_latent_rows", [16, 2, LAT], cc_off + 5120)
        wkt = at("w_uk_t", [P, LAT], cc_off + 9216)
        qrs = at("q_rope_pair", [P, NP_], cc_off + 11264)
        krt = at("k_rope_rows", [P, 3, 64], rt_off + 7200)
        top_mla = top[0]
        top[0] = rt_off
        pp = region("probs", [P, NT])
        ptt = region("probs_t", [P, 3, P])
        ol = region("o_latent", [P, 4, NP_])
        top[0] = rt_off
        lpt = region("past_latent_t", [P, 4, P])
        kpt = region("past_krope_t", [P, P])
        qb = region("q_sequence", [P, 5, P])
        pd = region("probs_sample", [P, 144])
        pdt = region("probs_sample_t", [P, P])
        pdn = region("probs_new_t", [16, P])
        dsum = region("softmax_stats_sample", [P, 4])
        assert top[0] <= rt_off + 7200

        oah = at("rwkv_out_hi", [P, FT, NT], after_ob, F32R)
        oal = at("rwkv_out_lo", [P, FT, NT], after_ob + 12288, F32R)
        mh = at("mix_hi", [P, KD, NT], area, F32R)
        ml = at("mix_lo", [P, KD, NT], after_ob + 24576, F32R)
        top[0] = after_ob + 49152
        gab = region("gates", [P, 2, NT])
        mm = region("mixed", [P, 2, NT])
        assert top[0] <= 229368
        ht = at("h_rows", [P, 3, D], phase)
        hn = at("h_normed", [P, 3, D], phase + 24576)
        ach = at("act_hi", [P, HJ, NT], phase + 24576, F32R)
        acl = at("act_lo", [P, HJ, NT], phase + 24576 + 33792, F32R)
        gp = at("gate_pad", [P, 2 + NP_ + NB * 18], area)
        cv = at("conv", [P, 402], area + 2048)
        sg = at("silu", [P, 402], area + 4096)
        rowt = at("proj_rows", [72, 4, P], area + 20992)
        af = at("act", [P, NT], area + 6144)
        ctr = at("conv_rows", [88, 9, P], area + 8192)
        gf = at("g_final_all", [P, D], area)
        jk2 = at("square_junk2", [P, D], area + 12800)

        ps = ctx.enter_context(nc.psum_tensor("banks", [P, 8, 512], F32))
        pair = lambda b: ps[:, b:b + 2, :].rearrange("p a n -> p (a n)")[:, 0:6 * P]
        unit = lambda b, u: ps[:, b + u // 4, (u % 4) * P:(u % 4 + 1) * P]
        PARAM_ROWS = [(120, prm[:, :]), (88, cprm[:, 0:2, :]), (88, cprm[:, 2:4, :])]
        PARAM_ROWS += [(88, cprev[:, b]) for b in range(NB)]
        PARAM_ROWS += [(96, shm[:, 0:4, :]), (96, shm[:, 4:8, :]), (32, shl[:, :, :])]
        n_params = [0]
        seq18 = lambda t: t.rearrange("p (b t) -> p b t", t=18)
        BON, M_I, M_S = cm["bones"], {0: cm["in64"], 1: cm["in16"]}, {0: cm["st64"], 1: cm["st16"]}
        
        raw_full = [sem("weights_loaded_0"), sem("weights_loaded_1")]
        hi_done, lo_done, blk_used = sem("hi_done"), sem("lo_done"), sem("blocks_used")
        proj_taken, stores = sem("proj_taken"), sem("stores")
        n_stores = [0]

        def store(eng, dst, src):
            eng.dma_start(dst, src).then_inc(stores, 16)
            n_stores[0] += 16

        def transpose(out, in_):
            n = in_.shape[0]
            return nc.tensor.transpose(out, in_, ident[0:n, 0:n])

        w_in = a["w_in"][0].rearrange("(h k p) c -> h p k c", h=2, p=P)
        w_ffn = a["w_ffn_in"][0].rearrange("(h k p) c -> h p k c", h=2, p=P)
        w_oab = [a["w_o_a"][0].rearrange("(k p) c -> p k c", p=P), a["w_o_b"][0].rearrange("(k p) c -> p k c", p=P)]
        w_out = a["w_out"][0].rearrange("(k p) (h c) -> k p h c", p=P, h=2)
        w_dn = a["w_ffn_down"][0].rearrange("(k p) (h c) -> k p h c", p=P, h=2)
        xp = a["x_prompt"][0].rearrange("(t p) c -> p t c", p=P)
        xs = a["x_sample"].rearrange("b s c -> (b s) c")
        vec = lambda n, lo_=0, n_=None: a[n][0][lo_:(lo_ + n_ if n_ else a[n].shape[1])].rearrange("(t p) -> t p", p=P)

        block = ctx.enter_context(nc.Block())

        E = sem
        LEVELS = ("lv2", "lv4", "lv8", "lv16", "lv32")
        units = lambda lv: range(6) if lv < 3 else range(4)
        unit_tok = lambda u: slice(256, 384) if u >= 4 else slice(128 * (u % 2), 128 * (u % 2) + 128)
        unit_tile = lambda u: 2 if u >= 4 else u % 2
        unit_head = lambda u: u - 4 if u >= 4 else u // 2
        heads = lambda i: slice(64 * i, 64 * i + 64)
        seq17 = lambda t: t.rearrange("p (b t) -> p b t", t=17)
        seq16 = lambda t: t.rearrange("p (b t) -> p b t", t=TS)
        bc = lambda m, n: m.unsqueeze(1).to_broadcast([P, n, P])

        def pe_rwkv(f, cut):
            pe, mm_, wait = nc.tensor, nc.tensor.matmul, nc.tensor.wait_ge
            cut(0)
            wait(E("y_out_done"), f)
            wait(E("lora_w_in"), f * 48 + 48)
            mm_(ps[:, 2, 0:NT], wl[0:96, 0, :], za[0:96, 0, :], start=True, stop=True)
            mm_(ps[:, 3, 0:NT], wl[0:96, 1, :], za[0:96, 1, :], start=True, stop=True)
            for k in range(2):
                last = mm_(ps[:, 4, 0:NT], wg[:, k, :], za[:, 2 + k, :], start=k == 0, stop=k == 1)
            last.then_inc(E("lora_ps"), 1)
            wait(E("kk_sq_done"), f + 1)
            mm_(ps[:, 5, 0:NT], BON, sq[:, :], start=True, stop=True).then_inc(E("kk_sum_ps"), 1)
            cut(1)
            wait(E("s0_in"), f * 32 + 32)
            wait(E("rk_done"), f + 1)
            mm_(ps[:, 6, 0:NT], BON, rk[:, :], start=True, stop=True).then_inc(E("rk_sum_ps"), 1)
            for b in range(NB):
                last = transpose(ps[:, 7, 64 * b:64 * b + 64], s0l[:, b, :])
            last.then_inc(E("s0_ps"), 1)
            cut(2)
            wait(E("gates_done"), f + 1)
            wait(E("abkr_done"), f + 1)
            for i, src in enumerate((kp_, be)):
                for t in range(3):
                    transpose(ps[:, 2 + i, t * P:t * P + P], src[:, t * P:t * P + P])
            for t in range(3):
                last = transpose(ps[:, 4, t * P:t * P + P], z[:, 2, t * P:t * P + P])
            last.then_inc(E("tok_ps"), 1)
            wait(E("s0_done"), f + 1)
            for i in range(2):
                for b in range(NB):
                    last = mm_(ps[heads(i), 5, 16 * b:16 * b + 16], s0t[:, b, :],
                               al[:, i, 256 + 16 * b:272 + 16 * b], start=True, stop=True)
            last.then_inc(E("as_ps"), 1)
            cut(3)
            wait(E("bonus_done"), f + 1)
            for u in range(6):
                last = mm_(unit(6, u), be[:, unit_tok(u)], al[:, unit_head(u), unit_tok(u)], start=True, stop=True)
            last.then_inc(E("nt_ps"), 1)
            wait(E("tok_done"), f + 1)
            for u in range(6):
                last = mm_(unit(2, u), al[:, unit_head(u), unit_tok(u)], be[:, unit_tok(u)], start=True, stop=True)
            last.then_inc(E("n_ps"), 1)
            wait(E("as_done"), f + 1)
            for u in range(6):
                last = mm_(unit(4, u), kp_[:, unit_tok(u)], al[:, unit_head(u), unit_tok(u)], start=True, stop=True)
            last.then_inc(E("mt_ps"), 1)
            cut(4)
            for lv in range(5):
                wait(E("n_level_done"), f * 5 + (lv + 1))
                if lv == 0:
                    wait(E("t_first_done"), f + 1)
                    wait(E("mt_done"), f + 1)
                else:
                    wait(E("t_done"), f * 5 + lv)
                for u in units(lv):
                    last = mm_(unit(4, u), (c_k, c_b)[lv % 2][:, u, :], t_x[:, u, :], start=True, stop=True)
                last.then_inc(E("g_ps"), 1)
                if lv in (0, 1, 2):
                    cut(5 + lv)
                wait(E("g_done"), f * 5 + (lv + 1))
                if lv < 4:
                    for u in units(lv):
                        last = mm_(unit(6, u), t_y[:, u, :], t_g[:, u, :], start=True, stop=True)
                for u in units(lv):
                    last = mm_(unit(2, u), t_g[:, u, :], t_y[:, u, :], start=True, stop=True)
                last.then_inc(E("dt_ps"), 1)
            wait(E("t_done"), f * 5 + 5)
            for b, src in ((4, kp_), (6, be)):
                for u in range(6):
                    last = mm_(unit(b, u), src[:, unit_tok(u)], rh[:, unit_head(u), unit_tok(u)],
                               start=True, stop=True)
                last.then_inc(E("c_ps"), 1)
            wait(E("c_done"), f * 2 + 2)

            v = tok[:, 2]
            for c in range(4):
                t, r0, cs = c // 2, 64 * (c % 2), slice(64 * (c % 2), 64 * (c % 2) + 64)
                cols = slice(64 * c, 64 * c + 64)
                if c:
                    wait(E("state_done"), f * 4 + c)
                for i in range(2):
                    last = mm_(ps[r0:r0 + 64, 2, heads(i)], m_t[:, 2 * i + t, cs], v[:, t, heads(i)],
                               start=True, stop=c == 0)
                    if c:
                        last = mm_(ps[r0:r0 + 64, 2, heads(i)], al[:, i, cols], st[:, 1, :], start=False, stop=True)
                last.then_inc(E("r_ps"), 1)
                if c == 0:
                    for i in range(2):
                        mm_(ps[:, 6, heads(i)], m_t[:, 4 + i, :], v[:, 2, heads(i)], start=True, stop=False)
                        last = mm_(ps[:, 6, heads(i)], asd[:, :], ident[:, heads(i)], start=False, stop=True)
                    last.then_inc(E("rd_ps"), 1)
                wait(E("r_done"), f * 4 + (c + 1))
                for i in range(2):
                    last = mm_(ps[r0:r0 + 64, 3, heads(i)], t_y[:, 2 * i + t, cs], rr[:, 0, heads(i)],
                               start=True, stop=True)
                last.then_inc(E("u_ps"), 1)
                if c == 0:
                    wait(E("rd_done"), f + 1)
                    for i in range(2):
                        last = mm_(ps[:, 7, heads(i)], t_y[:, 4 + i, :], rr[:, 1, heads(i)], start=True, stop=True)
                    last.then_inc(E("ud_ps"), 1)
                gain = [ps[heads(i), 4, 0:64] for i in range(2)]
                yo = [ps[heads(i), 5, cols] for i in range(2)]
                for i in range(2):
                    mm_(gain[i], tok[r0:r0 + 64, 0, t, heads(i)], v[r0:r0 + 64, t, heads(i)], start=True, stop=False)
                    mm_(yo[i], v[:, t, heads(i)], c_k[:, 2 * i + t, cs], start=True, stop=False)
                    if c:
                        mm_(yo[i], st[:, 1, :], rh[:, i, cols], start=False, stop=False)
                wait(E("u_done"), f * 4 + (c + 1))
                mm_(yo[0], un[:, 0, heads(0)], c_b[:, t, cs], start=False, stop=True)
                for i in range(2):
                    last = mm_(gain[i], tok[r0:r0 + 64, 1, t, heads(i)], un[r0:r0 + 64, 0, heads(i)],
                               start=False, stop=True)
                last.then_inc(E("state_ps"), 1)
                mm_(yo[1], un[:, 0, heads(1)], c_b[:, 2 + t, cs], start=False, stop=True).then_inc(E("y_ps"), 1)
                if c == 0:
                    wait(E("ud_done"), f + 1)
                    for i in range(2):
                        o = ps[heads(i), 5, 256:384]
                        mm_(o, v[:, 2, heads(i)], c_k[:, 4 + i, :], start=True, stop=False, skip_group_check=True)
                        mm_(o, un[:, 1, heads(i)], c_b[:, 4 + i, :], start=False, stop=False, skip_group_check=True)
                        for b in range(NB):
                            last = mm_(ps[heads(i), 5, 256 + 16 * b:272 + 16 * b], s0t[:, b, :],
                                       rh[:, i, 256 + 16 * b:272 + 16 * b], start=False, stop=b == NB - 1,
                                       skip_group_check=True)
                    last.then_inc(E("yd_ps"), 1)
                if c in (1, 2):
                    wait(E("vx_done"), f * 2 + c)
                    for i in range(2):
                        last = mm_(ps[heads(i), 6 + (c - 1), :], tok[:, c - 1, 2, heads(i)],
                                   vx[:, i].rearrange("p b v -> p (b v)"), start=True, stop=True)
                    last.then_inc(E("sd_ps"), 1)
            wait(E("state_done"), f * 4 + 4)
            wait(E("y_raw_done"), f + 1)
            mm_(ps[:, 3, 0:NT], BON, yb[:, :], start=True, stop=True).then_inc(E("mean_ps"), 1)
            transpose(ps[0:64, 2, 0:P], st[:, 0, :]).then_inc(E("sp_t_ps"), 1)
            wait(E("sd_done"), f + 1)
            wait(E("y_sq_done"), f + 1)
            mm_(ps[:, 4, 0:NT], BON, sq[:, :], start=True, stop=True).then_inc(E("var_ps"), 1)
            for b in range(NB):
                last = transpose(ps[0:64, 6 + b // 4, (b % 4) * P:(b % 4 + 1) * P], s0t[:, b, :])
            last.then_inc(E("sd_t_ps"), 1)

        def act_rwkv(f, cut, ch):
            act, wait, fn = nc.scalar, nc.scalar.wait_ge, nc.scalar.activation
            cut(0)
            wait(E("lora_ps"), f + 1)
            wait(E("pf_done"), f + 1)
            fn(sw[:, :], ps[:, 2, 0:NT], ACT.Sigmoid, bias=pf[:, 3:4])
            fn(aa[:, :], ps[:, 3, 0:NT], ACT.Sigmoid, bias=pf[:, 4:5])
            fn(gg[:, :], ps[:, 4, 0:NT], ACT.Copy).then_inc(E("gates_done"), 1)
            wait(E("kk_raw_done"), f + 1)
            fn(sq[:, :], kk0[:, :], ACT.Square).then_inc(E("kk_sq_done"), 1)
            cut(1)
            wait(E("kk_clamped"), f + 1)
            ch.link(fn(rn[:, :], rn[:, :], ACT.Ln))
            ch.link(fn(rn[:, :], rn[:, :], ACT.Exp, scale=-0.5))
            wait(E("decay_sums_done"), f + 1)
            fn(e1[:, :], cu[:, :], ACT.Exp, scale=-CDEC)
            fn(e2[:, :], cu[:, :], ACT.Exp, scale=CDEC)
            fn(e3[:, :], dx[:, :], ACT.Exp, scale=-CDEC)
            fn(emid[:, :, :], mid[:, :, :], ACT.Exp, scale=-CDEC).then_inc(E("exps_done"), 1)
            wait(E("s0_ps"), f + 1)
            fn(s0t[:, :, :], ps[:, 7, :].rearrange("p (b v) -> p b v", b=NB), ACT.Copy).then_inc(E("s0_done"), 1)
            cut(2)
            wait(E("tok_ps"), f + 1)
            fn(tok[:, :, :, :].rearrange("p a t c -> p a (t c)"), ps[:, 2:5, 0:NT], ACT.Copy)\
                .then_inc(E("tok_done"), 1)
            wait(E("as_ps"), f + 1)
            fn(asd[:, :], ps[:, 5, 0:P], ACT.Copy).then_inc(E("as_done"), 1)
            cut(3)
            cut(4)
            for lv in range(5):
                wait(E("g_ps"), f * 5 + (lv + 1))
                n = len(units(lv))
                fn(t_g[:, 0:n, :], pair(4).rearrange("p (u c) -> p u c", u=6)[:, 0:n, :], ACT.Copy)\
                    .then_inc(E("g_done"), 1)
                if lv in (0, 1, 2):
                    cut(5 + lv)
            wait(E("rd_ps"), f + 1)
            fn(rr[:, 1, :], ps[:, 6, 0:P], ACT.Copy).then_inc(E("rd_done"), 1)
            wait(E("ud_ps"), f + 1)
            fn(un[:, 1, :], ps[:, 7, 0:P], ACT.Copy, scale=-1.0).then_inc(E("ud_done"), 1)
            wait(E("yd_ps"), f + 1)
            wait(E("y_ps"), f * 4 + 4)
            fn(yb[:, :], ps[:, 5, 0:NT], ACT.Copy).then_inc(E("y_raw_done"), 1)
            wait(E("sp_t_ps"), f + 1)
            wait(E("state_stores"), f * 48)
            fn(sto[:, :], ps[0:64, 2, 0:P], ACT.Copy).then_inc(E("s_out"), 1)
            wait(E("y_centred"), f + 1)
            fn(sq[:, :], yc[:, :], ACT.Square).then_inc(E("y_sq_done"), 1)
            wait(E("sd_t_ps"), f + 1)
            fn(so[:, :, :].rearrange("v (h b) c -> v h (b c)", h=2), ps[0:64, 6:8, :], ACT.Copy)\
                .then_inc(E("so_done"), 1)
            wait(E("var_ps"), f + 1)
            ch.link(fn(rn[:, :], ps[:, 4, 0:NT], ACT.Ln, scale=1.0 / 64, bias=gneps))
            fn(rn[:, :], rn[:, :], ACT.Exp, scale=-0.5).then_inc(E("y_rstd_done"), 1)

        def dve_rwkv(f, cut, ch):
            dve, wait = nc.vector, nc.vector.wait_ge
            tt, stt3, cp = nc.vector.tensor_tensor, nc.vector.scalar_tensor_tensor, nc.vector.tensor_copy
            M, A, S = ALU.mult, ALU.add, ALU.subtract
            link = ch.link
            cp(pf[:, :], prm[:, 0:80].rearrange("p (g f) -> p g f", f=FT)[:, :, bass.ds(f, 1)].squeeze(2))\
                .then_inc(E("pf_done"), 1)
            link(cp(pb[:, :, 257:PAD:17],
                    shm[:, :, :].rearrange("p b (i f) -> p i f b", f=FT)[:, :, bass.ds(f, 1), :].squeeze(2)))
            wait(E("pf_done"), f + 1)
            wait(proj_taken, f * 4 + (T_FT + 3))
            wait(E("sd_ps"), f * 2)
            link(tt(db[:, :, 0:PAD - 1], pb[:, :, 0:PAD - 1], pb[:, :, 1:PAD], S))
            for i in range(3):
                stt3(z[:, i, 0:NP_], db[:, i, 0:NP_], pf[:, i:i + 1], pb[:, i, 1:257], M, A)
                stt3(seq16(z[:, i, NP_:NT]), seq17(db[:, i, 257:PAD])[:, :, 0:TS], pf[:, i:i + 1],
                     seq17(pb[:, i, 257:PAD])[:, :, 1:17], M, A)
            col = lambda q, n: tail[:, q:q + n, :].rearrange("p q (i f) -> p q i f", f=FT)[:, :, :, bass.ds(f, 1)]
            cp(col(0, 1).squeeze(3).squeeze(1), pb[:, :, 256])
            cp(col(1, 8).squeeze(3), pb[:, :, 273:PAD:17].rearrange("p i b -> p b i")).then_inc(E("z_done"), 1)
            wait(E("z_done"), f + 1)
            zr, zk, zv = z[:, 0, :], z[:, 1, :], z[:, 2, :]
            nc.vector.tensor_scalar(kk0[:, :], zk, pf[:, 5:6], None, M).then_inc(E("kk_raw_done"), 1)
            cut(0)
            wait(E("gates_done"), f + 1)
            link(nc.vector.tensor_tensor_scan(cu[:, :], reset, sw[:, :], 0.0, M, A))
            c4 = cu[:, 0:NP_].rearrange("p (c t) -> p c t", c=4)
            link(cp(mid[:, :, :], c4[:, :, 31:64:32]))
            link(tt(c4, c4, mid[:, :, 0:1].to_broadcast([P, 4, 64]), S))
            tt(dx[:, :], cu[:, :], sw[:, :], S).then_inc(E("decay_sums_done"), 1)
            wait(E("kk_sum_ps"), f + 1)
            nc.vector.tensor_scalar(rn[:, :], ps[:, 5, 0:NT], 1e-12, None, ALU.max).then_inc(E("kk_clamped"), 1)
            cut(1)
            link(nc.vector.tensor_scalar(t1[:, :], aa[:, :], -1.0, pf[:, 6:7], A, M))
            link(stt3(k2[:, :], t1[:, :], 1.0, zk, A, M))
            stt3(rk[:, :], zr, pf[:, 7:8], k2[:, :], M, M).then_inc(E("rk_done"), 1)
            wait(E("exps_done"), f + 1)
            tt(kp_[:, :], k2[:, :], e2[:, :], M)
            link(tt(rn[:, :], kk0[:, :], rn[:, :], M))
            for i in range(2):
                h = heads(i)
                tt(al[h, i, :], rn[h, :], e3[h, :], M)
                tt(rh[h, i, :], z[h, 0, :], e1[h, :], M)
            link(tt(kka[:, :], rn[:, :], aa[:, :], M))
            tt(be[:, :], kka[:, :], e2[:, :], M).then_inc(E("abkr_done"), 1)
            wait(E("rk_sum_ps"), f + 1)
            tt(rk[:, :], ps[:, 6, 0:NT], zv, M).then_inc(E("bonus_done"), 1)
            cut(2)
            cut(3)
            u6 = lambda b, lo_, n: ps[:, b + lo_ // 4, 0:n * P].rearrange("p (u c) -> p u c", u=n)

            def masked(dst, b, masks):
                tt(dst[:, 0:4, :], u6(b, 0, 4), bc(masks[0], 4), M)
                return tt(dst[:, 4:6, :], u6(b, 4, 2), bc(masks[1], 2), M)
            wait(E("nt_ps"), f + 1)
            masked(n_t, 6, M_S).then_inc(E("nt_done"), 1)
            wait(E("nt_done"), f + 1)
            link(tt(t_y[:, :, :], n_t[:, :, :], bc(cm["nl1"], 6), M))
            link(tt(t_y[:, :, :], t_y[:, :, :], bc(ident, 6), A))
            wait(E("n_ps"), f + 1)
            link(masked(t_x, 2, {0: cm["nl1t"], 1: cm["nl1t"]}))
            tt(t_x[:, :, :], t_x[:, :, :], bc(ident, 6), A).then_inc(E("t_first_done"), 1)
            wait(E("t_first_done"), f + 1)
            wait(E("mt_ps"), f + 1)
            masked(m_t, 4, M_S).then_inc(E("mt_done"), 1)
            cut(4)
            for lv in range(5):
                if lv in (0, 1, 2):
                    cut(5 + lv)
                wait(E("dt_ps"), f * 5 + (lv + 1))
                for lo_, n in ((0, 4), (4, 2)) if lv < 3 else ((0, 4),):
                    if lv < 4:
                        tt(t_x[:, lo_:lo_ + n, :], t_x[:, lo_:lo_ + n, :], u6(6, lo_, n), S)
                    last = tt(t_y[:, lo_:lo_ + n, :], t_y[:, lo_:lo_ + n, :], u6(2, lo_, n), S)
                last.then_inc(E("t_done"), 1)
                wait(E("t_done"), f * 5 + (lv + 1))
            for j, (dst, b) in enumerate(((c_k, 4), (c_b, 6))):
                wait(E("c_ps"), f * 2 + (j + 1))
                masked(dst, b, M_I).then_inc(E("c_done"), 1)
            for c in range(4):
                r = slice(64 * (c % 2), 64 * (c % 2) + 64)
                wait(E("r_ps"), f * 4 + (c + 1))
                cp(rr[r, 0, :], ps[r, 2, 0:P]).then_inc(E("r_done"), 1)
                wait(E("u_ps"), f * 4 + (c + 1))
                nc.vector.tensor_scalar(un[r, 0, :], ps[r, 3, 0:P], -1.0, None, M).then_inc(E("u_done"), 1)
                wait(E("state_ps"), f * 4 + (c + 1))
                e_last = e1[:, 64 * c + 63:64 * c + 64]
                if c == 0:
                    link(nc.vector.tensor_scalar(st[:, 0, :], ps[:, 4, 0:64], e_last, None, M))
                elif c < 3:
                    link(stt3(st[:, 0, :], ps[:, 4, 0:64], e_last, st[:, 2, :], M, A))
                else:
                    stt3(st[:, 0, :], ps[:, 4, 0:64], e_last, st[:, 2, :], M, A).then_inc(E("state_done"), 1)
                if c < 3:
                    wait(E("y_ps"), f * 4 + (c + 1))
                    nc.vector.tensor_scalar(st[:, 2, :], st[:, 0, :], emid_tot(c + 1), None, M)
                    nc.vector.tensor_scalar(st[:, 1, :], st[:, 0, :], emid[:, c + 1, 0:1], None, M)\
                        .then_inc(E("state_done"), 1)
                    wait(E("state_done"), f * 4 + (c + 1))
                if c < 2:
                    if c == 0:
                        wait(E("tok_done"), f + 1)
                    else:
                        wait(E("ud_done"), f + 1)
                        wait(E("sd_ps"), f * 2 + 1)
                    src = tok[:, 2, 2, :] if c == 0 else un[:, 1, :]
                    for i in range(2):
                        last = tt(vx[:, i], src[:, heads(i)].unsqueeze(1).to_broadcast([P, NB, 64]),
                                  bmask.unsqueeze(2).to_broadcast([P, NB, 64]), M)
                    last.then_inc(E("vx_done"), 1)
            wait(E("yd_ps"), f + 1)
            wait(E("sd_ps"), f * 2 + 2)
            p3 = lambda b: ps[:, b, :].rearrange("p (b v) -> p b v", b=NB)
            link(tt(s0t[:, :, :], s0t[:, :, :], p3(6), A))
            link(tt(s0t[:, :, :], s0t[:, :, :], p3(7), A))
            tt(s0t[:, :, :], s0t[:, :, :],
               e1[:, 256 + TS - 1:NT:TS].unsqueeze(2).to_broadcast([P, NB, 64]), M).then_inc(E("sd_done"), 1)
            wait(E("mean_ps"), f + 1)
            stt3(yc[:, :], ps[:, 3, 0:NT], -1.0 / 64, yb[:, :], M, A).then_inc(E("y_centred"), 1)
            wait(E("y_rstd_done"), f + 1)
            wait(E("y_centred"), f + 1)
            link(tt(yc[:, :], yc[:, :], rn[:, :], M))
            link(nc.vector.tensor_scalar(yc[:, :], yc[:, :], pf[:, 8:9], pf[:, 9:10], M, A))
            link(tt(yc[:, :], yc[:, :], rk[:, :], A))
            tt(oa[:, bass.ds(f, 1), :].squeeze(1), yc[:, :], gg[:, :], M).then_inc(E("y_out_done"), 1)
            wait(E("y_out_done"), f + 1)

        emid_tot = lambda c: emid[:, c, 1:2]
        def full(t):
            return 16 * t + 16 + 16 * min(max(t - (T_MLA + 3), 0), 5)

        def act_hi(t, s, cnt=None):
            nc.scalar.wait_ge(raw_full[s], full(t) if cnt is None else cnt)
            if not (isinstance(t, int) and t == 0):
                nc.scalar.wait_ge(blk_used, t * 2 + (s - 1))
            nc.scalar.activation(hi[:, s], raw[:, s], ACT.Copy).then_inc(hi_done, 1)

        def dve_lo(t, s):
            nc.vector.wait_ge(hi_done, t * 2 + (s + 1))
            nc.vector.tensor_tensor(lo[:, s], raw[:, s], hi[:, s].bitcast(F32), ALU.subtract).then_inc(lo_done, 1)

        def pe_block(t, s, out):
            nc.tensor.wait_ge(lo_done, t * 2 + (s + 1))
            for k in range(8):
                kt = 8 * s + k
                nc.tensor.matmul(out, hi[:, s, k, :], xh[:, kt, :], start=kt == 0, stop=False)
                nc.tensor.matmul(out, hi[:, s, k, :], xl[:, kt, :], start=False, stop=False)
                last = nc.tensor.matmul(out, lo[:, s, k, :], xh[:, kt, :], start=False, stop=kt == 15)
            last.then_inc(blk_used, 1)

        def pe_proj(t, p):
            if p >= 2:
                nc.tensor.wait_ge(proj_taken, p - 1)
            for s in range(2):
                pe_block(t, s, ps[:, p % 2, 0:NT])

        def act_next(t, end=False):
            static = isinstance(t, int)
            act_hi(t, 1, full(t) if static else t * 16 + 96)
            if not end:
                act_hi(t + 1, 0, full(t + 1) if static else t * 16 + 112)

        def dve_next(t, end=False):
            dve_lo(t, 1)
            if not end:
                dve_lo(t + 1, 0)

        def pe_norm(src, first, ready, taken):
            for kt in range(KD):
                bank = 2 + kt % 6
                if kt == 0:
                    nc.tensor.wait_ge(ready, 3)
                if kt >= 6:
                    nc.tensor.wait_ge(taken, first * KD + kt - 5)
                for t in range(3):
                    last = transpose(ps[:, bank, t * P:t * P + P], src[:, t, kt * P:kt * P + P])
                last.then_inc(E("norm_ps"), 1)

        def act_norm_stats(src, sq_out, arrived, ch):
            for t in range(3):
                arrived(t)
                nc.scalar.activation(sq_out, src[:, t, :], ACT.Square, accum_out=stat[:, t:t + 1])\
                    .then_inc(E("sum_sq"), 1)
                nc.scalar.wait_ge(E("sum_sq"), sumsq[0] + t + 1)
            sumsq[0] += 3
            ch.link(nc.scalar.activation(stat[:, 3:6], stat[:, 0:3], ACT.Ln, scale=1.0 / D, bias=epsb))
            nc.scalar.activation(stat[:, 0:3], stat[:, 3:6], ACT.Exp, scale=-0.5).then_inc(E("rstd_done"), 1)
        sumsq = [0]
        epsb, gneps = EPS, GN_EPS

        def act_norm(first, gcol):
            for kt in range(KD):
                nc.scalar.wait_ge(E("norm_ps"), first * KD + kt + 1)
                nc.scalar.activation(xh[:, kt, :], ps[:, 2 + kt % 6, 0:NT], ACT.Identity,
                                     scale=prm[:, gcol + kt:gcol + kt + 1]).then_inc(E("xh_done"), 1)

        def dve_norm(first, gcol):
            for kt in range(KD):
                nc.vector.wait_ge(E("xh_done"), first * KD + kt + 1)
                nc.vector.scalar_tensor_tensor(xl[:, kt, :], ps[:, 2 + kt % 6, 0:NT], prm[:, gcol + kt:gcol + kt + 1],
                                               xh[:, kt, :].bitcast(F32), ALU.mult, ALU.subtract)\
                    .then_inc(E("xt_lo"), 1)

        @block.sync
        def _(sp):
            def block_in(t, s, dst, src):
                sp.dma_start(dst, src).then_inc(raw_full[s], 16)

            def free(t, s):
                if not (isinstance(t, int) and t == 0):
                    sp.wait_ge(lo_done, t * 2 + (s - 1))

            def tile_in(t, src):
                for s in range(2):
                    free(t, s)
                    block_in(t, s, raw[:, s], src(s))

            sp.dma_start(c1[:, :], consts[:, 0:NC1]).then_inc(sem("c1_in"), 16)
            for t in range(3):
                sp.dma_start(xt[:, t, :], xp[:, t, :] if t < 2 else xs).then_inc(sem(f"x_in{t}"), 16)
            for j, c in enumerate((3072, 3168, 3264, 3392)):
                tile_in(T_LORA + j, lambda s: w_in[s][:, :, c:c + P])
            with sp.Fori(0, FT) as f:
                for q, (c, w) in enumerate(((0, P), (W, P), (2 * W, P), (Q0, 192))):
                    tile_in(T_FT + q + f * 4, lambda s: w_in[s][:, :, bass.ds(f * w + c, P)])
            for j in range(9):
                t = T_MLA + j
                for s in range(2):
                    free(t, s)
                    if j < 4:
                        c = CKV0 + j * P
                        block_in(t, s, raw[:, s], w_in[s][:, :, c:c + P])
                    else:
                        g0 = Q0 + 384 * (j - 4)
                        cols = (g0 + 128, g0 + 320) if j < 8 else (KR0, KR0)
                        for g, c in enumerate(cols):
                            block_in(t, s, raw[:, s, :, 64 * g:64 * g + 64], w_in[s][:, :, c:c + 64])
            with sp.Fori(1, KD + 1) as j1:
                for q in range(2):
                    tile_in(j1 * 3 + (T_MIX + q - 3), lambda s: w_in[s][:, :, bass.ds(j1 * P + (G0 - P + q * D), P)])
                tile_in(j1 * 3 + (T_MIX - 1), lambda s: w_oab[s][:, :, bass.ds(j1 * P - P, P)])

            def wide_tiles(t0, ch, count, w, row0):
                with sp.Fori(0, count) as i:
                    t = i + t0
                    for s in range(2):
                        free(t, s)
                        src = w[bass.ds(i * 2 + (row0 + s), 1), :, bass.ds(ch, 1), :].squeeze(2).squeeze(0)
                        sp.dma_start(raw[:, s].rearrange("p k c -> p (k c)"), src).then_inc(raw_full[s], 16)

            with sp.Fori(0, 2) as ch:
                wide_tiles(ch * 8 + T_OUT, ch, 8, w_out, 0)
            with sp.Fori(0, 2) as hf:
                with sp.Fori(0, HJ) as j:
                    for q in range(2):
                        tile_in(hf * T_HALF + j * 2 + (T_FFN + q),
                                lambda s: w_ffn[s][:, :, bass.ds(hf * (HJ * P) + j * P + q * DFF, P)])
                with sp.Fori(0, 2) as ch:
                    wide_tiles(hf * T_HALF + ch * 11 + (T_FFN + 2 * HJ), ch, 11, w_dn, hf * HJ)

        @block.gpsimd
        def _(pool):
            seen = sem("params_in")
            n = [0]

            def load(dst, src):
                pool.dma_start(dst, src).then_inc(seen, 16)
                n[0] += 16
            load(rows[0:24, 0, :], vec("mu_shift", 0, 3072))
            for i, nm in enumerate(("w0", "a0", "k_k", "k_a")):
                load(rows[24 + 8 * i:32 + 8 * i, 0, :], vec(nm))
            load(rows[56:64, 0, :], a["r_k"][0].rearrange("(t h) n -> t (h n)", h=2))
            load(rows[64:72, 0, :], vec("lnx_g"))
            load(rows[72:80, 0, :], vec("lnx_b"))
            load(rows[80:96, 0, :], vec("g_mix"))
            load(rows[96:112, 0, :], vec("g_ffn"))
            for i, c in enumerate((3072, 3168, 3264, 3392)):
                load(rows[112 + i:113 + i, 0, :], vec("mu_shift", c, P))
                load(rows[8 * i:8 * i + 8, 13, :], a["state_rwkv_shift"][0, :, 0, c:c + P])
            load(rows[116:120, 0, :], vec("g_kv"))
            load(rows[0:88, 1, :], a["conv_w"][0, 0:2, :].rearrange("j (t p) -> (j t) p", p=P))
            load(rows[0:44, 2, :], a["conv_w"][0, 2, :].rearrange("(t p) -> t p", p=P))
            load(rows[44:88, 2, :], vec("conv_b"))
            for b in range(NB):
                load(rows[0:88, 3 + b, :], a["state_ffn_conv"][0, b].rearrange("r (t p) -> (r t) p", p=P))
                load(rows[24 * (b % 4):24 * (b % 4) + 24, 11 + b // 4, :],
                     a["state_rwkv_shift"][0, b, 0, 0:3072].rearrange("(t p) -> t p", p=P))
            n_params[0] = n[0]
            pool.dma_start(c2[:, :], consts[:, NC1:NC1 + NC2]).then_inc(sem("c2_in"), 16)

            def lora_in(f):
                for i, nm in enumerate(("w2", "a2")):
                    pool.dma_start(wl[0:96, i, :], a[nm][0][:, bass.ds(f * P, P)]).then_inc(sem("lora_w_in"), 16)
                pool.dma_start(wg[:, :, :], a["g2"][0].rearrange("(k p) c -> p k c", p=P)[:, :, bass.ds(f * P, P)])\
                    .then_inc(sem("lora_w_in"), 16)

            def s0_in(f):
                for i in range(2):
                    src = a["state_rwkv_wkv"][0].rearrange("b (f i) v k -> i f v b k", i=2)[i][bass.ds(f, 1)]
                    pool.dma_start(s0l[:, :, 64 * i:64 * i + 64], src.squeeze(0)).then_inc(sem("s0_in"), 16)

            pool.wait_ge(sem("xt_lo"), KD)
            lora_in(0)
            s0_in(0)

            def rwkv(f, last):
                pool.wait_ge(sem("nt_done"), f + 1)
                for lv, name in enumerate(LEVELS):
                    if lv >= 2:
                        pool.wait_ge(sem("g_ps"), f * 5 + (lv - 1))
                    n_u = len(units(lv))
                    nc.gpsimd.tensor_tensor((c_k, c_b)[lv % 2][:, 0:n_u, :], n_t[:, 0:n_u, :], bc(cm[name], n_u),
                                            ALU.mult).then_inc(sem("n_level_done"), 1)
                if not last:
                    pool.wait_ge(sem("gates_done"), f + 1)
                    lora_in(f + 1)
                    pool.wait_ge(sem("s0_done"), f + 1)
                    s0_in(f + 1)
                pool.wait_ge(sem("s_out"), f + 1)
                pool.wait_ge(sem("so_done"), f + 1)
                dst = wkv_s[0].rearrange("b (f i) v k -> i f v b k", i=2)
                dp = wkv_p[0, 0].rearrange("(f i) v k -> f v i k", i=2)
                one = lambda ap: ap[f] if last else ap[bass.ds(f, 1)].squeeze(0)
                for i in range(2):
                    pool.dma_start(one(dst[i]), so[:, :, 64 * i:64 * i + 64]).then_inc(sem("state_stores"), 16)
                pool.dma_start(one(dp), sto[:, :].rearrange("v (i k) -> v i k", i=2))\
                    .then_inc(sem("state_stores"), 16)

            pool.wait_ge(sem("c2_in"), 16)
            with pool.Fori(0, FT - 1) as f:
                rwkv(f, False)
            rwkv(FT - 1, True)
            pool.wait_ge(sem("state_stores"), FT * 48)

            pool.wait_ge(sem("y_out_done"), FT)
            pool.dma_start(c3[:, :], consts[:, NC1 + NC2:NC1 + NC2 + NC3]).then_inc(sem("c3_in"), 16)
            w_ukv = a["w_ukv"][0].rearrange("(k p) c -> p k c", p=P)

            def head_in(i, hh):
                pool.dma_start(wuk[:, hh], w_ukv[:, :, bass.ds(i * 512 + 256 * hh, 256)])\
                    .then_inc(sem(f"wuk_in{hh}"), 16)

            def past_in(i, bb):
                b = i * 2 + bb
                one = lambda ap: ap[bass.ds(b, 1)].squeeze(0)
                pool.dma_start(lp[:, bb, :], one(a["cache_mla_latent"][0])).then_inc(sem(f"past_in{bb}"), 16)
                pool.dma_start(kpast[:, bb], one(a["cache_mla_krope"][0]).unsqueeze(1).to_broadcast([P, 2, 64]))\
                    .then_inc(sem(f"past_in{bb}"), 16)
                pool.dma_start(lnew[0:TS, bb, :], one(lat_s[0])).then_inc(sem(f"past_in{bb}"), 16)

            for hh in range(2):
                head_in(0, hh)
            pool.wait_ge(sem("latent_rows_done"), 1)
            store(pool, lat_p[0, 0].rearrange("(t p) c -> p t c", p=P), ltok[:, 0:2, :])
            pool.dma_start(lat_s[0].rearrange("b s c -> (b s) c"), ltok[:, 2, :]).then_inc(sem("new_latent_stored"), 16)
            store(pool, kr_p[0, 0].rearrange("(t p) c -> p t c", p=P), krt[:, 0:2, :])
            store(pool, kr_s[0].rearrange("b s c -> (b s) c"), krt[:, 2, :])
            pool.wait_ge(sem("new_latent_stored"), 16)
            pool.wait_ge(sem("latent_done"), 1)
            for bb in range(2):
                past_in(0, bb)
            with pool.Fori(0, 3) as i:
                for hh in range(2):
                    pool.wait_ge(sem("oh_ps"), i * 2 + (hh + 1))
                    head_in(i + 1, hh)
            for hh in range(2):
                pool.wait_ge(sem("oh_ps"), 7 + hh)
                head_in(0, hh)
            with pool.Fori(0, 3) as i:
                for bb in range(2):
                    pool.wait_ge(sem("old_ps"), i * 2 + (bb + 1))
                    past_in(i + 1, bb)
            with pool.Fori(0, 3) as i:
                for hh in range(2):
                    pool.wait_ge(sem("ohd_ps"), i * 2 + (hh + 1))
                    head_in(i + 1, hh)
            pool.wait_ge(blk_used, 2 * T_OUT)
            for t in range(3):
                pool.dma_start(ht[:, t, :], xp[:, t, :] if t < 2 else xs).then_inc(sem("h_in"), 16)
            pool.wait_ge(sem("act_done"), 2 * HJ)
            pool.dma_start(gf[:, :], a["g_final"].partition_broadcast(P)).then_inc(sem("gf_in"), 16)
            for t in range(3):
                pool.wait_ge(sem("y_ready"), t + 1)
                store(pool, y_prompt[0].rearrange("(t p) c -> p t c", p=P)[:, t, :] if t < 2
                      else y_sample.rearrange("b s c -> (b s) c"), hn[:, t, :])
            pool.wait_ge(sem("tails_done"), 1)
            for q in range(9):
                dst = conv_p[0, 0] if q == 0 else conv_s[0, q - 1]
                store(pool, dst.rearrange("r (t p) -> (r t) p", p=P), ctr[:, q, :])
            pool.wait_ge(sem("rkv_tails_done"), 1)
            shp, shs = shift_p[0, 0], shift_s[0, :, 0]
            for q in range(9):
                dst = (shp[0] if q == 0 else shs[q - 1])[0:3072].rearrange("(t p) -> t p", p=P)
                store(pool, dst, rowt[24 * (q % 3):24 * (q % 3) + 24, q // 3, :])
            for l, (c, w) in enumerate(((3072, 96), (3168, 96), (3264, P), (3392, P))):
                store(pool, shp[:, c:c + w], rowt[9 * l:9 * l + 1, 3, 0:w])
                store(pool, shs[:, c:c + w], rowt[9 * l + 1:9 * l + 9, 3, 0:w])
            pool.wait_ge(stores, n_stores[0])

        @block.tensor
        def _(pe):
            mm_, wait = nc.tensor.matmul, nc.tensor.wait_ge
            wait(E("c1_in"), 16)
            wait(E("params_in"), n_params[0])
            for i, (r, bank) in enumerate(PARAM_ROWS):
                last = transpose(ps[:, 2 + i // 4, (i % 4) * P:(i % 4) * P + r], rows[0:r, i, :])
            last.then_inc(E("params_ps"), 1)
            wait(E("params_done"), 1)
            pe_norm(xt, 0, E("x_scaled"), E("xt_lo"))
            wait(E("xt_lo"), KD)
            for t in range(4):
                pe_proj(T_LORA + t, t)
            wait(E("c2_in"), 16)
            for q in range(4):
                pe_proj(T_FT + q, 4 + q)
            wait(E("z_lora_done"), 4)
            wait(E("zeroed"), 1)

            with pe.Fori(0, FT - 1) as f:
                def cut(k):
                    q, s = divmod(k, 2)
                    if s == 0:
                        wait(proj_taken, f * 4 + (8 + q - 1))
                    pe_block(f * 4 + (T_FT + 4 + q), s, ps[:, q % 2, 0:NT])
                pe_rwkv(f, cut)
            pe_rwkv(FT - 1, lambda k: None)

            for j in range(9):
                pe_proj(T_MLA + j, T_MLA + j)
            wait(E("c3_in"), 16)
            wait(E("y_out_done"), FT)
            wait(E("c_sq_done"), 1)
            for j in range(4):
                last = mm_(ps[:, 7, 0:NT], ones, csq[:, j, :], start=j == 0, stop=j == 3)
            last.then_inc(E("c_sum_ps"), 1)
            wait(proj_taken, T_MIX)
            for j in range(5):
                last = mm_(ps[:, 2 + j, 0:NT], rot, (kr2 if j == 4 else qrp[:, j])[:, :], start=True, stop=True)
            last.then_inc(E("rot_ps"), 1)
            wait(E("rope_done"), 1)
            wait(E("latent_done"), 1)
            for t in range(3):
                for j in range(4):
                    transpose(ps[:, 2 + t, j * P:j * P + P], latt[:, j, t * P:t * P + P])
                last = transpose(ps[:, 5, t * P:t * P + P], kr2[:, t * P:t * P + P])
            last.then_inc(E("latent_rows_ps"), 1)

            def prompt_head(i, hh):
                e = i * 2 + hh
                w = wuk[:, hh]
                wait(E(f"wuk_in{hh}"), i * 16 + 16)
                for kc in range(4):
                    last = transpose(ps[:, 2, kc * P:kc * P + P], w[:, kc, 0:P])
                last.then_inc(E("wk_ps"), 1)
                wait(E("wk_done"), e + 1)
                wait(E("ol_done"), e)
                for kc in range(4):
                    last = mm_(ps[:, 3 + kc, 0:NT], wkt[:, kc * P:kc * P + P],
                               qn[:, bass.ds(e, 1), :].squeeze(1), start=True, stop=True)
                last.then_inc(E("ql_ps"), 1)
                wait(E("ql_done"), e + 1)
                h = heads(hh)
                for t, (c0, n) in enumerate(((0, P), (P, 2 * P))):
                    for kc in range(4):
                        mm_(ps[:, 7, c0:c0 + n], qlp[:, kc, t * P:t * P + P], latt[:, kc, 0:n],
                            start=kc == 0, stop=False)
                    last = mm_(ps[:, 7, c0:c0 + n], qrs[h, t * P:t * P + P], kr2[h, 0:n], start=False, stop=True)
                last.then_inc(E("s_ps"), 1)
                wait(E("p_done"), e + 1)
                for j in range(3):
                    last = transpose(ps[:, 2, j * P:j * P + P], pp[:, j * P:j * P + P])
                last.then_inc(E("pt_ps"), 1)
                wait(E("pt_done"), e + 1)
                o = ps[:, 3:5, :].rearrange("p a (k t) -> p (a k) t", k=2)
                for kc in range(4):
                    mm_(o[:, kc, 0:P], ltok[:, 0, kc * P:kc * P + P], ptt[:, 0, :], start=True, stop=True)
                    mm_(o[:, kc, P:2 * P], ltok[:, 0, kc * P:kc * P + P], ptt[:, 1, :], start=True, stop=False)
                    last = mm_(o[:, kc, P:2 * P], ltok[:, 1, kc * P:kc * P + P], ptt[:, 2, :], start=False, stop=True)
                last.then_inc(E("ol_ps"), 1)
                wait(E("ol_done"), e + 1)
                for kc in range(4):
                    last = mm_(ps[:, 5, 0:NP_], w[:, kc, P:2 * P], ol[:, kc, :], start=kc == 0, stop=kc == 3)
                last.then_inc(E("oh_ps"), 1)
                wait(E("oh_done"), e + 1)

            wait(E("latent_rows_done"), 1)
            with pe.Fori(0, 4) as i:
                for hh in range(2):
                    prompt_head(i, hh)

            with pe.Fori(0, 4) as i:
                for bb in range(2):
                    b = i * 2 + bb
                    wait(E(f"past_in{bb}"), i * 48 + 48)
                    for kc in range(4):
                        transpose(ps[:, 2, kc * P:kc * P + P], lp[:, bb, kc * P:kc * P + P])
                    transpose(ps[:, 3, 0:P], kpast[:, bb].rearrange("p r c -> p (r c)")).then_inc(E("lpt_ps"), 1)
                    wait(E("lpt_done"), b + 1)
                    for kc in range(5):
                        k_ = lpt[:, kc, :] if kc < 4 else kpt[:, :]
                        mm_(ps[:, 4, 0:P], qb[:, kc, :], k_, start=kc == 0, stop=kc == 4)
                    for kc in range(5):
                        k_ = (latt[:, kc, :] if kc < 4 else kr2[:, :])[:, bass.ds(b * TS + NP_, TS)]
                        last = mm_(ps[:, 4, P:P + TS], qb[:, kc, :], k_, start=kc == 0, stop=kc == 4)
                    last.then_inc(E("sd_scores_ps"), 1)
                    wait(E("pd_done"), b + 1)
                    transpose(ps[:, 5, 0:P], pd[:, 0:P])
                    transpose(ps[0:TS, 5, P:2 * P], pd[:, P:P + TS]).then_inc(E("pdt_ps"), 1)
                    wait(E("pdt_done"), b + 1)
                    for kc in range(4):
                        mm_(ps[:, 6, kc * P:kc * P + P], lp[:, bb, kc * P:kc * P + P], pdt[:, :], start=True, stop=False)
                        last = mm_(ps[:, 6, kc * P:kc * P + P], lnew[0:TS, bb, kc * P:kc * P + P], pdn[0:TS, :],
                                   start=False, stop=True)
                    last.then_inc(E("old_ps"), 1)
                    wait(E("old_done"), b + 1)
            with pe.Fori(0, 4) as i:
                for hh in range(2):
                    e = i * 2 + hh
                    wait(E(f"wuk_in{hh}"), i * 16 + 80)
                    wait(E("ohd_done"), e)
                    for kc in range(4):
                        last = mm_(ps[:, 7, 0:P], wuk[:, hh, kc, P:2 * P],
                                   qld[:, kc, bass.ds(e, 1), :].squeeze(1), start=kc == 0, stop=kc == 3)
                    last.then_inc(E("ohd_ps"), 1)

            wait(E("oa_split"), FT)
            wait(E("ohd_done"), FT)
            with pe.Fori(0, KD) as j:
                for q in range(2):
                    wait(proj_taken, j * 2 + (T_MIX + q - 1))
                    for s in range(2):
                        pe_block(j * 3 + (T_MIX + q), s, ps[:, (T_MIX + q) % 2, 0:NT])
                wait(E("ab_taken"), j)
                for s, (xh_, xl_) in enumerate(((oah, oal), (obh, obl))):
                    wait(lo_done, j * 6 + (2 * T_MIX + 4 + s + 1))
                    o = ps[:, 2 + s, 0:NT]
                    for k in range(8):
                        mm_(o, hi[:, s, k, :], xh_[:, k, :], start=k == 0, stop=False)
                        mm_(o, hi[:, s, k, :], xl_[:, k, :], start=False, stop=False)
                        last = mm_(o, lo[:, s, k, :], xh_[:, k, :], start=False, stop=k == 7)
                    last.then_inc(blk_used, 1)

            def wide(t0, ch_no, kts, lh, ll):
                wait(E("acc_taken"), ch_no)
                for kt in range(kts):
                    s = kt % 2
                    wait(lo_done, t0 * 2 + (kt + 1))
                    wh, wlo = (x[:, s].rearrange("p k c -> p (k c)") for x in (hi, lo))
                    for t in range(3):
                        l_h, l_l = lh[:, kt, t * P:t * P + P], ll[:, kt, t * P:t * P + P]
                        for n, (l_, w_) in enumerate(((l_h, wh), (l_h, wlo), (l_l, wh))):
                            for cb in range(2):
                                last = mm_(ps[:, 2 + 2 * t + cb, :], l_, w_[:, 512 * cb:512 * cb + 512],
                                           start=kt == 0 and n == 0, stop=kt == kts - 1 and n == 2)
                    last.then_inc(blk_used, 1)

            wait(E("mix_done"), KD)
            with pe.Fori(0, 2) as ch:
                wide(ch * 8 + T_OUT, ch, 16, mh, ml)
            wait(E("acc_taken"), 2)
            pe_norm(hn, 1, E("h_scaled"), E("xt_lo"))
            wait(E("xt_lo"), 2 * KD)
            for hf in range(2):
                with pe.Fori(0, HJ) as j:
                    for q in range(2):
                        t = j * 2 + (hf * T_HALF + T_FFN + q)
                        wait(E(("gate_taken", "up_taken")[q]), j + hf * HJ)
                        for s in range(2):
                            pe_block(t, s, ps[:, q, 0:NT])
                wait(E("act_done"), hf * HJ + HJ)
                with pe.Fori(0, 2) as ch:
                    wide(ch * 11 + (hf * T_HALF + T_FFN + 2 * HJ), ch + (hf * 2 + 2), HJ, ach, acl)
            wait(E("acc_taken"), 6)
            for q in range(9):
                last = transpose(ps[0:88, 2 + q // 4, (q % 4) * P:(q % 4 + 1) * P],
                                 ctail[:, q].rearrange("p r j -> p (r j)"))
            for g in range(3):
                last = transpose(ps[0:72, 5, g * P:g * P + P], tail[:, 3 * g:3 * g + 3, :].rearrange("p q t -> p (q t)"))
            last = transpose(ps[0:36, 6, 0:P], taill[:, :, :].rearrange("p l q -> p (l q)"))
            last.then_inc(E("tails_ps"), 1)

        @block.scalar
        def _(act):
            wait, fn = nc.scalar.wait_ge, nc.scalar.activation
            ch = Chain(nc.scalar, E("act_chain"))
            act_norm_stats(xt, junk[:, :], lambda t: wait(E(f"x_in{t}"), 16), ch)
            wait(E("params_ps"), 1)
            for i, (r, dst) in enumerate(PARAM_ROWS):
                last = fn(dst, ps[:, 2 + i // 4, (i % 4) * P:(i % 4) * P + r].rearrange(
                    "p (a c) -> p a c", a=dst.shape[1]) if len(dst.shape) == 3 else
                    ps[:, 2 + i // 4, (i % 4) * P:(i % 4) * P + r], ACT.Copy)
            last.then_inc(E("params_done"), 1)
            wait(E("params_done"), 1)
            act_norm(0, 80)
            act_hi(0, 0)

            def taken(t, p, dst, sem_=proj_taken):
                wait(blk_used, t * 2 + 2)
                fn(dst, ps[:, p % 2, 0:NT], ACT.Copy).then_inc(sem_, 1)

            def taken_pad(t, p, i):
                wait(blk_used, t * 2 + 2)
                fn(pb[:, i, 1:257], ps[:, p % 2, 0:NP_], ACT.Copy)
                fn(seq17(pb[:, i, 257:PAD])[:, :, 1:17], seq16(ps[:, p % 2, NP_:NT]), ACT.Copy)\
                    .then_inc(proj_taken, 1)

            for t in range(4):
                act_next(t)
                if t >= 2:
                    wait(E("z_lora_done"), t - 1)
                taken_pad(t, t, t % 2)
                if t == 2:
                    wait(E("z_lora_done"), 1)
                    fn(za[0:96, 0, :], za[0:96, 0, :], ACT.Tanh)
            wait(E("z_lora_done"), 4)
            ch.link(fn(za[:, 2:4, :], za[:, 2:4, :], ACT.Sigmoid))
            for q in range(4):
                act_next(T_FT + q)
                if q < 3:
                    taken_pad(T_FT + q, q, q)

            def act_cut(f):
                def cut(k):
                    q, s = divmod(k, 2)
                    t = f * 4 + (T_FT + 4 + q)
                    if s == 0:
                        if q == 0:
                            taken(t - 1, 1, qn[:, bass.ds(f, 1), :].squeeze(1))
                        else:
                            if q == 1:
                                wait(E("z_done"), f + 1)
                            taken_pad(t - 1, q - 1, q - 1)
                    if s == 0:
                        act_hi(t, 1, t * 16 + 16)
                    else:
                        act_hi(t + 1, 0, t * 16 + 32)
                return cut
            wait(E("zeroed"), 1)
            with ch.loop(FT - 1, LINKS["act_rwkv"]) as f:
                act_rwkv(f, act_cut(f), ch)

            def last_cut(k):
                if k == 0:
                    taken(T_FT + 4 * FT - 1, 1, qn[:, FT - 1, :])
            act_rwkv(FT - 1, last_cut, ch)

            wait(E("y_out_done"), FT)
            wait(E("state_stores"), FT * 48)
            for j in range(9):
                t = T_MLA + j
                act_next(t)
                taken(t, t, cc[:, j] if j < 4 else qrp[:, j - 4] if j < 8 else kr2[:, :])
                if j == 3:
                    wait(proj_taken, t + 1)
                    fn(csq[:, :, :], cc[:, :, :], ACT.Square).then_inc(E("c_sq_done"), 1)
            wait(E("c_sum_ps"), 1)
            ch.link(fn(crs[:, :], ps[:, 7, 0:NT], ACT.Ln, scale=1.0 / LAT, bias=epsb))
            fn(crs[:, :], crs[:, :], ACT.Exp, scale=-0.5).then_inc(E("c_rstd_done"), 1)
            wait(E("latent_rows_ps"), 1)
            fn(ltok[:, :, :], ps[:, 2:5, :], ACT.Copy)
            fn(krt[:, :, :], ps[:, 5, 0:NT].rearrange("p (t c) -> p t c", t=3)[:, :, 0:64], ACT.Copy)\
                .then_inc(E("latent_rows_done"), 1)

            with ch.loop(4, 0) as i:
                for hh in range(2):
                    e = i * 2 + hh
                    wait(E("wk_ps"), e + 1)
                    fn(wkt[:, :], ps[:, 2, :], ACT.Copy).then_inc(E("wk_done"), 1)
                    if hh == 0:
                        wait(E("s_ps"), e)
                        fn(qrs[:, :], qrp[:, bass.ds(i, 1), 0:NP_].squeeze(1), ACT.Copy)
                    wait(E("ql_ps"), e + 1)
                    wait(E("qlp_done"), e + 1)
                    fn(qld[:, :, bass.ds(e, 1), :].squeeze(2), ps[:, 3:7, NP_:NT], ACT.Copy).then_inc(E("ql_done"), 1)
                    wait(E("mx_done"), e + 1)
                    for t, (c0, n) in enumerate(((0, P), (P, 2 * P))):
                        last = fn(pp[:, c0:c0 + n], pp[:, c0:c0 + n], ACT.Exp, bias=msum[:, 2 + t:3 + t],
                                  accum_out=msum[:, 4 + t:5 + t])
                    last.then_inc(E("ex_done"), 1)
                    wait(E("pt_ps"), e + 1)
                    fn(ptt[:, :, :], ps[:, 2, 0:NT].rearrange("p (j c) -> p j c", j=3), ACT.Copy)\
                        .then_inc(E("pt_done"), 1)
                    wait(E("oh_ps"), e + 1)
                    fn(obh[:, bass.ds(e, 1), 0:NP_].squeeze(1), ps[:, 5, 0:NP_], ACT.Copy).then_inc(E("obh_done"), 1)
            with ch.loop(4, 0) as i:
                for bb in range(2):
                    b = i * 2 + bb
                    wait(E("lpt_ps"), b + 1)
                    fn(lpt[:, :, :].rearrange("p k c -> p (k c)"), ps[:, 2, :], ACT.Copy)
                    wait(E("kpt_done"), b + 1)
                    fn(qb[:, 0:4, :].rearrange("p k (h t) -> p (k h) t", h=8),
                       qld[:, :, :, bass.ds(b * TS, TS)].rearrange("p k h t -> p (k h) t"), ACT.Copy)\
                        .then_inc(E("lpt_done"), 1)
                    wait(E("mxd_done"), b + 1)
                    fn(pd[:, :], ps[:, 4, 0:P + TS], ACT.Exp, scale=SCALE, bias=dsum[:, 1:2], accum_out=dsum[:, 2:3])\
                        .then_inc(E("exd_done"), 1)
                    wait(E("pdt_ps"), b + 1)
                    fn(pdt[:, :], ps[:, 5, 0:P], ACT.Copy)
                    fn(pdn[0:TS, :], ps[0:TS, 5, P:2 * P], ACT.Copy).then_inc(E("pdt_done"), 1)
            with ch.loop(4, 0) as i:
                for hh in range(2):
                    e = i * 2 + hh
                    wait(E("ohd_ps"), e + 1)
                    fn(obh[:, bass.ds(e, 1), NP_:NT].squeeze(1), ps[:, 7, 0:P], ACT.Copy).then_inc(E("obhd_done"), 1)
            wait(E("old_done"), NB)
            wait(E("ohd_ps"), FT)
            for k in range(FT):
                fn(oah[:, k, :], oa[:, k, :], ACT.Copy).then_inc(E("oah_done"), 1)
            wait(E("oa_split"), FT)
            with ch.loop(KD, 0) as j:
                for q in range(2):
                    t = j * 3 + (T_MIX + q)
                    act_next(t)
                    wait(blk_used, t * 2 + 2)
                    if q == 0:
                        wait(E("ab_taken"), j)
                    fn(gab[:, q, :], ps[:, (T_MIX + q) % 2, 0:NT], ACT.Sigmoid).then_inc(proj_taken, 1)
                act_next(j * 3 + (T_MIX + 2))
                wait(E("mixed"), j + 1)
                fn(mh[:, bass.ds(j, 1), :].squeeze(1), mm[:, 0, :], ACT.Copy).then_inc(E("mix_hi"), 1)
            with ch.loop(2, 0) as c:
                with ch.loop(8, 0) as i:
                    act_next(c * 8 + i + T_OUT)
            act_norm_stats(ht, jk2[:, :], lambda t: wait(E("acc_taken"), 2), ch)
            act_norm(1, 96)
            for hf in range(2):
                with ch.loop(HJ, 0) as j:
                    for q in range(2):
                        t = j * 2 + (hf * T_HALF + T_FFN + q)
                        act_next(t)
                        if q == 0:
                            wait(blk_used, t * 2 + 2)
                            wait(E("conv_done"), j + hf * HJ)
                            fn(gp[:, 2:2 + NP_], ps[:, 0, 0:NP_], ACT.Copy)
                            fn(seq18(gp[:, 2 + NP_:])[:, :, 2:18], seq16(ps[:, 0, NP_:NT]), ACT.Copy)\
                                .then_inc(E("gate_taken"), 1)
                    wait(E("conv_done"), j + (hf * HJ + 1))
                    wait(E("up_taken"), j + hf * HJ)
                    fn(sg[:, 0:400], cv[:, 0:400], ACT.Silu).then_inc(E("silu_done"), 1)
                    wait(E("up_taken"), j + (hf * HJ + 1))
                    fn(ach[:, bass.ds(j, 1), :].squeeze(1), af[:, :], ACT.Copy).then_inc(E("act_hi"), 1)
                for c in range(2):
                    t0 = hf * T_HALF + c * 11 + T_FFN + 2 * HJ
                    end = hf == 1 and c == 1
                    with ch.loop(10 if end else 11, 0) as i:
                        act_next(i + t0)
                    if end:
                        act_next(t0 + 10, end=True)
            act_norm_stats(ht, jk2[:, :], lambda t: wait(E("acc_taken"), 6), ch)
            wait(E("tails_ps"), 1)
            fn(ctr[:, 0:8, :].rearrange("p (a q) c -> p a (q c)", a=2), ps[0:88, 2:4, :], ACT.Copy)
            fn(ctr[:, 8, :], ps[0:88, 4, 0:P], ACT.Copy).then_inc(E("tails_done"), 1)

        @block.vector
        def _(dve):
            wait = nc.vector.wait_ge
            tt, stt3, cp, ts = (nc.vector.tensor_tensor, nc.vector.scalar_tensor_tensor, nc.vector.tensor_copy,
                                nc.vector.tensor_scalar)
            M, A, S = ALU.mult, ALU.add, ALU.subtract
            ch = Chain(nc.vector, E("dve_chain"))
            wait(E("rstd_done"), 1)
            for t in range(3):
                ts(xt[:, t, :], xt[:, t, :], stat[:, t:t + 1], None, M).then_inc(E("x_scaled"), 1)
            wait(E("params_done"), 1)
            dve_norm(0, 80)
            dve_lo(0, 0)
            wait(E("norm_ps"), KD)
            nc.vector.memset(pb[:, :, 0:1], 0.0)
            nc.vector.memset(rr[:, :, :], 0.0)
            nc.vector.memset(un[:, :, :], 0.0)
            nc.vector.memset(al[:, :, :], 0.0)
            nc.vector.memset(db[:, :, PAD - 1:PAD], 0.0)
            nc.vector.memset(rh[:, :, :], 0.0).then_inc(E("zeroed"), 1)
            wait(E("zeroed"), 1)
            for t in range(4):
                dve_next(t)
                i = t % 2
                ch.link(cp(pb[:, i, 257:PAD:17], shl[:, t, :]))
                wait(proj_taken, t + 1)
                ch.link(tt(db[:, i, 0:PAD - 1], pb[:, i, 0:PAD - 1], pb[:, i, 1:PAD], S))
                mu = prm[:, 112 + t:113 + t]
                stt3(za[:, t, 0:NP_], db[:, i, 0:NP_], mu, pb[:, i, 1:257], M, A)
                stt3(seq16(za[:, t, NP_:NT]), seq17(db[:, i, 257:PAD])[:, :, 0:TS], mu,
                     seq17(pb[:, i, 257:PAD])[:, :, 1:17], M, A)
                cp(taill[:, t, 0:1], pb[:, i, 256:257])
                cp(taill[:, t, 1:9], pb[:, i, 273:PAD:17]).then_inc(E("z_lora_done"), 1)
                wait(E("z_lora_done"), t + 1)
            for q in range(4):
                dve_next(T_FT + q)

            def dve_cut(f):
                def cut(k):
                    q, s = divmod(k, 2)
                    t = f * 4 + (T_FT + 4 + q)
                    dve_lo(t, 1) if s == 0 else dve_lo(t + 1, 0)
                return cut
            wait(E("c2_in"), 16)
            with ch.loop(FT - 1, LINKS["dve_rwkv"]) as f:
                dve_rwkv(f, dve_cut(f), ch)
            dve_rwkv(FT - 1, lambda k: None, ch)

            for j in range(9):
                dve_next(T_MLA + j)
            wait(E("rot_ps"), 1)
            wait(E("c3_in"), 16)
            for j in range(5):
                x = kr2[:, :] if j == 4 else qrp[:, j]
                tt(rtmp[:, j, :], ps[:, 2 + j, 0:NT], sin, M)
                ch.link(tt(x, x, cos, M))
                ch.link(tt(x, x, rtmp[:, j, :], A))
            ch.link(nc.vector.memset(qrz[:, :, :], 0.0))
            for hh in range(2):
                last = cp(qrz[heads(hh), hh:8:2, :], qrp[heads(hh), :, NP_:NT])
            last.then_inc(E("rope_done"), 1)
            wait(E("c_rstd_done"), 1)
            for j in range(4):
                last = stt3(latt[:, j, :], cc[:, j, :], prm[:, 116 + j:117 + j], crs[:, :], M, M)
            last.then_inc(E("latent_done"), 1)
            with ch.loop(4, LINKS["dve_head"]) as i:
                for hh in range(2):
                    e = i * 2 + hh
                    wait(E("ql_ps"), e + 1)
                    cp(qlp[:, :, :], ps[:, 3:7, 0:NP_]).then_inc(E("qlp_done"), 1)
                    wait(E("s_ps"), e + 1)
                    ch.link(stt3(pp[:, :], ps[:, 7, 0:NT], SCALE, amask, M, A))
                    nc.vector.reduce_max(msum[:, 0:1], pp[:, 0:P], AX)
                    ch.link(nc.vector.reduce_max(msum[:, 1:2], pp[:, P:NT], AX))
                    ts(msum[:, 2:4], msum[:, 0:2], -1.0, None, M).then_inc(E("mx_done"), 1)
                    wait(E("ex_done"), e + 1)
                    ch.link(nc.vector.reciprocal(msum[:, 6:8], msum[:, 4:6]))
                    ts(pp[:, 0:P], pp[:, 0:P], msum[:, 6:7], None, M)
                    ts(pp[:, P:NT], pp[:, P:NT], msum[:, 7:8], None, M).then_inc(E("p_done"), 1)
                    wait(E("ol_ps"), e + 1)
                    cp(ol[:, :, :].rearrange("p (a k) t -> p a (k t)", a=2), ps[:, 3:5, :]).then_inc(E("ol_done"), 1)
                    wait(E("obh_done"), e + 1)
                    tt(obl[:, bass.ds(e, 1), 0:NP_].squeeze(1), ps[:, 5, 0:NP_],
                       obh[:, bass.ds(e, 1), 0:NP_].squeeze(1).bitcast(F32), S).then_inc(E("oh_done"), 1)
            with ch.loop(4, LINKS["dve_seq"]) as i:
                for bb in range(2):
                    b = i * 2 + bb
                    wait(E("lpt_ps"), b + 1)
                    cp(kpt[:, :], ps[:, 3, 0:P])
                    cp(qb[:, 4, :].rearrange("p (h t) -> p h t", h=8), qrz[:, :, bass.ds(b * TS, TS)])\
                        .then_inc(E("kpt_done"), 1)
                    wait(E("sd_scores_ps"), b + 1)
                    ch.link(nc.vector.reduce_max(dsum[:, 0:1], ps[:, 4, 0:P + TS], AX))
                    ts(dsum[:, 1:2], dsum[:, 0:1], -SCALE, None, M).then_inc(E("mxd_done"), 1)
                    wait(E("exd_done"), b + 1)
                    ch.link(nc.vector.reciprocal(dsum[:, 3:4], dsum[:, 2:3]))
                    ts(pd[:, :], pd[:, :], dsum[:, 3:4], None, M).then_inc(E("pd_done"), 1)
                    wait(E("old_ps"), b + 1)
                    cp(qld[:, :, :, bass.ds(b * TS, TS)].rearrange("p k h t -> p (k h) t"),
                       ps[:, 6, :].rearrange("p (k t) -> p k t", t=TS)).then_inc(E("old_done"), 1)
            with ch.loop(4, 0) as i:
                for hh in range(2):
                    e = i * 2 + hh
                    wait(E("obhd_done"), e + 1)
                    tt(obl[:, bass.ds(e, 1), NP_:NT].squeeze(1), ps[:, 7, 0:P],
                       obh[:, bass.ds(e, 1), NP_:NT].squeeze(1).bitcast(F32), S).then_inc(E("ohd_done"), 1)
            for k in range(FT):
                wait(E("oah_done"), k + 1)
                tt(oal[:, k, :], oa[:, k, :], oah[:, k, :].bitcast(F32), S).then_inc(E("oa_split"), 1)
            with ch.loop(KD, LINKS["dve_mix"]) as j:
                for q in range(3):
                    dve_next(j * 3 + (T_MIX + q))
                wait(proj_taken, j * 2 + (T_MIX + 2))
                wait(blk_used, j * 6 + (2 * T_MIX + 6))
                wait(E("mix_hi"), j)
                tt(mm[:, 0, :], ps[:, 2, 0:NT], gab[:, 0, :], M)
                tt(mm[:, 1, :], ps[:, 3, 0:NT], gab[:, 1, :], M).then_inc(E("ab_taken"), 1)
                wait(E("ab_taken"), j + 1)
                tt(mm[:, 0, :], mm[:, 0, :], mm[:, 1, :], A).then_inc(E("mixed"), 1)
                wait(E("mix_hi"), j + 1)
                tt(ml[:, bass.ds(j, 1), :].squeeze(1), mm[:, 0, :],
                   mh[:, bass.ds(j, 1), :].squeeze(1).bitcast(F32), S).then_inc(E("mix_done"), 1)

            def add_acc(c, need, done):
                wait(E("acc_taken"), done)
                wait(blk_used, need)
                for t in range(3):
                    for cb in range(2):
                        dst = ht[:, t, bass.ds(c * 1024 + 512 * cb, 512)]
                        last = tt(dst, dst, ps[:, 2 + 2 * t + cb, :], A)
                last.then_inc(E("acc_taken"), 1)
            wait(E("h_in"), 48)
            with ch.loop(2, 0) as c:
                with ch.loop(8, 0) as i:
                    dve_next(c * 8 + i + T_OUT)
                add_acc(c, c * 16 + (2 * T_OUT + 16), c)
            wait(E("acc_taken"), 2)
            wait(E("rstd_done"), 2)
            for t in range(3):
                ts(hn[:, t, :], ht[:, t, :], stat[:, t:t + 1], None, M).then_inc(E("h_scaled"), 1)
            dve_norm(1, 96)
            wait(E("xt_lo"), 2 * KD)
            ch.link(nc.vector.memset(gp[:, 0:2], 0.0))
            for hf in range(2):
                with ch.loop(HJ, LINKS["dve_ffn"]) as j:
                    t = j * 2 + (hf * T_HALF + T_FFN)
                    n = j + hf * HJ
                    prev = cprev[:, :, :, bass.ds(n, 1)].squeeze(3)
                    ch.link(cp(seq18(gp[:, 2 + NP_:])[:, :, 0:2], prev))
                    dve_next(t)
                    wait(E("gate_taken"), n + 1)
                    tap = lambda q: cprm[:, q, bass.ds(n, 1)]
                    wait(E("silu_done"), n)
                    ch.link(ts(cv[:, 0:400], gp[:, 2:402], tap(2), tap(3), M, A))
                    ch.link(stt3(cv[:, 0:400], gp[:, 1:401], tap(1), cv[:, 0:400], M, A))
                    cp(ctail[:, 0, :, bass.ds(n, 1)].squeeze(2), gp[:, NP_:NP_ + 2])
                    cp(ctail[:, 1:9, :, bass.ds(n, 1)].squeeze(3), seq18(gp[:, 2 + NP_:])[:, :, 16:18])
                    stt3(cv[:, 0:400], gp[:, 0:400], tap(0), cv[:, 0:400], M, A).then_inc(E("conv_done"), 1)
                    dve_next(t + 1)
                    wait(E("silu_done"), n + 1)
                    wait(blk_used, t * 2 + 4)
                    wait(E("act_hi"), n)
                    tt(af[:, 0:NP_], sg[:, 0:NP_], ps[:, 1, 0:NP_], M)
                    tt(seq16(af[:, NP_:NT]), seq18(sg[:, 2 + NP_:])[:, :, 0:TS], seq16(ps[:, 1, NP_:NT]), M).then_inc(E("up_taken"), 1)
                    wait(E("act_hi"), n + 1)
                    wait(E("up_taken"), n + 1)
                    tt(acl[:, bass.ds(j, 1), :].squeeze(1), af[:, :],
                       ach[:, bass.ds(j, 1), :].squeeze(1).bitcast(F32), S).then_inc(E("act_done"), 1)
                for c in range(2):
                    t0 = hf * T_HALF + c * 11 + T_FFN + 2 * HJ
                    end = hf == 1 and c == 1
                    with ch.loop(10 if end else 11, 0) as i:
                        dve_next(i + t0)
                    if end:
                        dve_next(t0 + 10, end=True)
                    add_acc(c, (t0 + 11) * 2, 2 * hf + c + 2)
            wait(E("acc_taken"), 6)
            wait(E("rstd_done"), 3)
            wait(E("gf_in"), 16)
            for t in range(3):
                stt3(hn[:, t, :], ht[:, t, :], stat[:, t:t + 1], gf[:, :], M, M).then_inc(E("y_ready"), 1)
            wait(E("tails_ps"), 1)
            cp(rowt[0:72, 0:3, :].rearrange("p g c -> p (g c)"), ps[0:72, 5, 0:NT])
            cp(rowt[0:36, 3, :], ps[0:36, 6, 0:P]).then_inc(E("rkv_tails_done"), 1)


LINKS = {"act_rwkv": 3, "dve_rwkv": 20, "dve_head": 6, "dve_seq": 4, "dve_mix": 0, "dve_ffn": 3}

_INS = ["x_prompt", "x_sample", "cache_mla_latent", "cache_mla_krope", "state_rwkv_wkv", "state_rwkv_shift",
        "state_ffn_conv", "g_mix", "w_in", "mu_shift", "w0", "w2", "a0", "a2", "g2", "k_k", "k_a", "r_k", "lnx_g",
        "lnx_b", "w_o_a", "g_kv", "w_ukv", "w_o_b", "w_out", "g_ffn", "w_ffn_in", "conv_w", "conv_b", "w_ffn_down",
        "g_final"]
_OUTS = [(1, 256, D), (8, 16, D), (1, 1, 256, LAT), (1, 1, 256, 64), (1, 1, 16, 64, 64), (1, 1, 1, RW),
         (1, 1, 2, DFF), (1, 8, 16, LAT), (1, 8, 16, 64), (1, 8, 16, 64, 64), (1, 8, 1, RW), (1, 8, 2, DFF)]


def kernel(**inputs):
    import numpy as _np
    import concourse.bacc as _bacc
    from concourse.bass_utils import run_bass_kernel_spmd as _run

    nc = _bacc.Bacc("TRN2", target_bir_lowering=False, num_devices=1)
    arrays, aps = {}, {}
    for name in _INS:
        x = _np.ascontiguousarray(inputs[name])
        arrays[f"in_{name}"] = x
        aps[name] = nc.dram_tensor(f"in_{name}", x.shape, mybir.dt.from_np(x.dtype), kind="ExternalInput").ap()
    arrays["shape_consts"] = constants()
    consts = nc.dram_tensor("shape_consts", arrays["shape_consts"].shape, F32, kind="ExternalInput").ap()
    outs = [nc.dram_tensor(f"out_{i}", s, F32, kind="ExternalOutput").ap() for i, s in enumerate(_OUTS)]
    build(nc, aps, consts, outs)
    r = _run(nc, [arrays], core_ids=[0])
    return tuple(r.results[0][f"out_{i}"] for i in range(len(_OUTS)))
```

```python
from contextlib import ExitStack, contextmanager

import concourse.bass as bass
from concourse import mybir

F32 = mybir.dt.float32
F32R = mybir.dt.float32r
ALU = mybir.AluOpType
ACT = mybir.ActivationFunctionType
AX = mybir.AxisListType.X

P = 128
D = 2048
NT = 384
NP_ = 256
NB, TS = 8, 16
KD = D // P
W = 1024
FT = W // P
RW = 3520
Q0 = RW
CKV0 = Q0 + 1536
KR0 = CKV0 + 512
G0 = RW + 2112
DFF = 5632
NJ = DFF // P
HJ = NJ // 2
PAST = 128
LAT = 512
SCALE = 192.0 ** -0.5
EPS = 1e-6
GN_EPS = 64e-5
CDEC = 0.6065306597126334
PAD = 257 + NB * 17

C1 = ["ident", "ones"]
C2 = ["bones", "st64", "in64", "st16", "in16", "nl1", "nl1t", "lv2", "lv4", "lv8", "lv16", "lv32"]
C3 = ["rot"]
NC1 = len(C1) * P
NC2 = len(C2) * P + NT + 8
NC3 = P + 3 * NT

T_LORA = 0
T_FT = 4
T_MLA = T_FT + 4 * FT
T_MIX = T_MLA + 9
T_MIX_B = T_MIX + 3 * KD // 2
T_OUT = T_MIX + 3 * KD
T_FFN = T_OUT + KD
T_HALF = 2 * HJ + HJ
T_END = T_FFN + 2 * T_HALF


def constants():
    import numpy as np
    f = np.float32
    s, t = np.arange(P)[:, None], np.arange(P)[None, :]
    m = {"ident": s == t, "ones": s >= 0 * t, "bones": s // 64 == t // 64}
    for c in (64, 16):
        same = s // c == t // c
        m[f"st{c}"], m[f"in{c}"] = same & (s < t), same & (s <= t)
    level = lambda n: (s // (2 * n) == t // (2 * n)) & (s % (2 * n) < n) & (t % (2 * n) >= n)
    m["nl1"] = -level(1).astype(f)
    m["nl1t"] = m["nl1"].T
    for n in (2, 4, 8, 16, 32):
        m[f"lv{n}"] = level(n)
    rot = np.zeros((P, P), f)
    for b in (0, 64):
        for j in range(32):
            rot[b + j + 32, b + j] = -1
            rot[b + j, b + j + 32] = 1
    m["rot"] = rot
    cat = lambda names: [np.broadcast_to(m[n], (P, P)).astype(f) for n in names]
    tok = np.arange(NT)
    first = np.where(tok < NP_, tok % 64 == 0, tok % 16 == 0)
    reset = np.broadcast_to(1 - first.astype(f), (P, NT))
    bm = (s // 16 == np.arange(8)[None]).astype(f)
    half = 32
    inv = (f(10000.0) ** (-np.arange(half, dtype=f) / f(half))).astype(f)
    pos = np.where(tok < NP_, tok, PAST + tok % 16).astype(f)
    ang = (pos[None, :] * inv[np.arange(P) % half][:, None]).astype(f)
    key = np.concatenate([np.arange(128), np.arange(256)])[None]
    q = np.where(np.arange(NT)[None] < 128, s, 128 + s)
    amask = np.where(key // 64 <= q // 64, 0, -1e30)
    out = cat(C1) + cat(C2) + [reset, bm] + cat(C3) + [np.cos(ang), np.sin(ang), amask]
    return np.ascontiguousarray(np.concatenate([np.asarray(a, f) for a in out], 1))


class Chain:

    def __init__(self, eng, sem):
        self.eng, self.sem, self.base, self.k = eng, sem, 0, 0

    def link(self, ins):
        ins.then_inc(self.sem, 1)
        self.k += 1
        self.eng.wait_ge(self.sem, self.base + self.k)

    @contextmanager
    def loop(self, count, steps):
        base, k = self.base, self.k
        with self.eng.Fori(0, count) as i:
            self.base, self.k = i * steps + (base + k), 0
            yield i
            assert self.k == steps, f"the body links {self.k} times"
        self.base, self.k = base, k + count * steps


def build(nc, a, consts, outs):
    (y_prompt, y_sample, lat_p, kr_p, wkv_p, shift_p, conv_p,
     lat_s, kr_s, wkv_s, shift_s, conv_s) = outs
    ctx = ExitStack()
    sems = {}

    def sem(name):
        if name not in sems:
            sems[name] = ctx.enter_context(nc.semaphore(name))
        return sems[name]

    BASE = 16512
    top = [BASE]

    def at(name, shape, off, dt=F32):
        size = 4
        for n in shape[1:]:
            size *= n
        assert off % 32 == 0 and off + size <= 229368, (name, off, size)
        return nc.alloc_sbuf_tensor_at(name, shape, dt, offset=off)

    def region(name, shape, dt=F32):
        off = top[0]
        size = 4
        for n in shape[1:]:
            size *= n
        top[0] = off + (size + 31) // 32 * 32
        return at(name, shape, off, dt)

    with ctx:
        raw = region("w_raw", [P, 2, 8, P])
        hi = region("w_hi", [P, 2, 8, P], F32R)
        lo = region("w_lo", [P, 2, 8, P], F32R)
        xh = region("x_hi", [P, KD, NT], F32R)
        xl = region("x_lo", [P, KD, NT], F32R)
        c1 = region("consts_all", [P, NC1])
        prm = region("params", [P, 120])
        cprm = region("conv_params", [P, 4, NJ])
        cprev = region("conv_prev", [P, NB, 2, NJ])
        shm = region("shift_rkv", [P, NB, 24])
        shl = region("shift_lora", [P, 4, NB])
        stat = region("row_stats", [P, 8])
        tail = region("proj_last_rkv", [P, 9, 24])
        taill = region("proj_last_lora", [P, 4, 9])
        ctail = region("conv_last", [P, 9, 2, NJ])
        area = top[0]
        ident, ones = c1[:, 0:P], c1[:, P:2 * P]

        qn = region("q_nope", [P, FT, NT])
        oa = region("rwkv_out", [P, FT, NT])
        phase = top[0]
        pb = region("proj_pad", [P, 3, PAD])
        c2 = region("consts_rwkv", [P, NC2])
        cm = {n: c2[:, i * P:(i + 1) * P] for i, n in enumerate(C2)}
        reset = c2[:, len(C2) * P:len(C2) * P + NT]
        bmask = c2[:, len(C2) * P + NT:NC2]
        db_off = top[0]
        db = region("proj_diff", [P, 3, PAD])
        vx = at("v_by_sequence", [P, 2, NB, 64], db_off)
        z = region("z", [P, 3, NT])
        wl = region("lora_w2a2", [P, 2, P])
        wg = region("lora_g2", [P, 2, P])
        za = region("z_lora", [P, 4, NT])
        pf = region("params_ft", [P, 10])
        mid = region("decay_mid", [P, 4, 2])
        emid = region("decay_mid_exp", [P, 4, 2])
        sw, aa, gg, cu, dx, e1, e2, e3, kk0, sq, rn, t1, k2, kka, rk = [
            region(n, [P, NT]) for n in ("sig_w", "a_gate", "g_gate", "cum_decay", "cum_excl", "exp_inc", "exp_inv",
                                         "exp_excl", "kk_raw", "square", "norm", "k_scale", "k_mod", "kk_a",
                                         "bonus")]
        al = region("alpha_pad", [P, 2, NT])
        rh = region("rho_pad", [P, 2, NT])
        be = region("beta", [P, NT])
        kp_ = region("kappa", [P, NT])
        n_t, t_x, t_y, t_g, m_t, c_k, c_b = [
            region(n, [P, 6, P]) for n in ("n_t", "t_x", "t_y", "t_g", "m_t", "c_k", "c_b")]
        tok = region("tok_major", [P, 3, 3, P])
        rr = region("r_rhs", [P, 2, P])
        un = region("u_neg", [P, 2, P])
        asd = region("alpha_s0", [P, P])
        s0l = region("s0_load", [64, NB, P])
        s0t = region("s0_t", [P, NB, 64])
        so = region("s_out", [64, NB, P])
        st = region("state", [P, 3, 64])
        sto = region("state_rows", [64, P])
        assert top[0] <= 229368, top[0]
        yb, yc = cu, dx
        x_off = (229368 - 4 * 3 * D) // 32 * 32
        xt = at("x_rows", [P, 3, D], x_off)
        rows = at("param_rows", [P, 14, P], area)
        junk = at("square_junk", [P, D], area + 12288)

        top[0] = phase
        cc = region("c_kv", [P, 4, NT])
        lp = at("past_latent", [P, 2, LAT], phase)
        kpast = at("past_krope", [P, 2, 2, 64], phase + 4096)
        lnew = at("new_latent_rows", [16, 2, LAT], phase + 5120)
        top[0] = phase + 9216
        c3_off = top[0]
        c3 = region("consts_mla", [P, NC3])
        rot, cos, sin, amask = c3[:, 0:P], c3[:, P:P + NT], c3[:, P + NT:P + 2 * NT], c3[:, P + 2 * NT:NC3]
        wkt = at("w_uk_t", [P, LAT], c3_off + 512)
        qrs = at("q_rope_pair", [P, NP_], c3_off + 2560)
        oah_off = top[0]
        oah = region("rwkv_out_hi", [P, FT, NT], F32R)
        oal = region("rwkv_out_lo", [P, FT, NT], F32R)
        ob = region("mla_out", [P, FT, NT])
        after_ob = top[0]
        qrp = region("q_rope", [P, 4, NT])
        latt = region("latent_t", [P, 4, NT])
        kr2 = region("k_rope_t", [P, NT])
        ltok = region("latent_rows", [P, 3, LAT])
        wuk = region("w_ukv_head", [P, 2, 4, 256])
        msum = region("softmax_stats", [P, 8])
        krt = region("k_rope_rows", [P, 3, 64])
        qld_off = top[0]
        qld = region("q_latent_sample", [P, 4, 8, P])
        csq = at("c_square", [P, 4, NT], qld_off)
        rtmp = at("rope_tmp", [P, 5, NT], qld_off + 6144)
        crs = at("c_rstd", [P, NT], qld_off + 13824)
        heads_off = top[0]
        pp = region("probs", [P, NT])
        ptt = region("probs_t", [P, 3, P])
        ol = region("o_latent", [P, 4, NP_])
        qlp = at("q_latent", [P, 4, NP_], top[0] - 4096)
        assert top[0] <= 229368, top[0]
        top[0] = heads_off
        lpt = region("past_latent_t", [P, 4, P])
        kpt = region("past_krope_t", [P, P])
        qb = region("q_sequence", [P, 5, P])
        pd = region("probs_sample", [P, 144])
        pdt = region("probs_sample_t", [P, P])
        pdn = region("probs_new_t", [16, P])
        dsum = region("softmax_stats_sample", [P, 4])
        assert top[0] <= 229368, top[0]
        ga = at("branch_a_gated", [P, KD, NT], area)

        obh = at("mla_out_hi", [P, FT, NT], oah_off, F32R)
        obl = at("mla_out_lo", [P, FT, NT], oah_off + 12288, F32R)
        mh = at("mix_hi", [P, KD, NT], area, F32R)
        top[0] = after_ob
        ml = region("mix_lo", [P, KD, NT], F32R)
        gab = region("gates", [P, 2, NT])
        mm = region("mixed", [P, 2, NT])
        assert top[0] <= 229368
        ht = at("h_rows", [P, 3, D], phase)
        hn = at("h_normed", [P, 3, D], phase + 24576)
        ach = at("act_hi", [P, HJ, NT], phase + 24576, F32R)
        acl = at("act_lo", [P, HJ, NT], phase + 24576 + 33792, F32R)
        gp = at("gate_pad", [P, 2 + NP_ + NB * 18], area)
        cv = at("conv", [P, 402], area + 2048)
        sg = at("silu", [P, 402], area + 4096)
        rowt = at("proj_rows", [72, 4, P], area + 20992)
        af = at("act", [P, NT], area + 6144)
        ctr = at("conv_rows", [88, 9, P], area + 8192)
        gf = at("g_final_all", [P, D], area)
        jk2 = at("square_junk2", [P, D], area + 12800)

        ps = ctx.enter_context(nc.psum_tensor("banks", [P, 8, 512], F32))
        pair = lambda b: ps[:, b:b + 2, :].rearrange("p a n -> p (a n)")[:, 0:6 * P]
        unit = lambda b, u: ps[:, b + u // 4, (u % 4) * P:(u % 4 + 1) * P]
        PARAM_ROWS = [(120, prm[:, :]), (88, cprm[:, 0:2, :]), (88, cprm[:, 2:4, :])]
        PARAM_ROWS += [(88, cprev[:, b]) for b in range(NB)]
        PARAM_ROWS += [(96, shm[:, 0:4, :]), (96, shm[:, 4:8, :]), (32, shl[:, :, :])]
        n_params = [0]
        seq18 = lambda t: t.rearrange("p (b t) -> p b t", t=18)
        BON, M_I, M_S = cm["bones"], {0: cm["in64"], 1: cm["in16"]}, {0: cm["st64"], 1: cm["st16"]}
        
        raw_full = [sem("weights_loaded_0"), sem("weights_loaded_1")]
        hi_done, lo_done, blk_used = sem("hi_done"), sem("lo_done"), sem("blocks_used")
        proj_taken, stores = sem("proj_taken"), sem("stores")
        n_stores = [0]

        def store(eng, dst, src):
            eng.dma_start(dst, src).then_inc(stores, 16)
            n_stores[0] += 16

        def transpose(out, in_):
            n = in_.shape[0]
            return nc.tensor.transpose(out, in_, ident[0:n, 0:n])

        w_in = a["w_in"][0].rearrange("(h k p) c -> h p k c", h=2, p=P)
        w_ffn = a["w_ffn_in"][0].rearrange("(h k p) c -> h p k c", h=2, p=P)
        w_oab = [a["w_o_a"][0].rearrange("(k p) c -> p k c", p=P), a["w_o_b"][0].rearrange("(k p) c -> p k c", p=P)]
        w_out = a["w_out"][0].rearrange("(k p) (h c) -> k p h c", p=P, h=2)
        w_dn = a["w_ffn_down"][0].rearrange("(k p) (h c) -> k p h c", p=P, h=2)
        xp = a["x_prompt"][0].rearrange("(t p) c -> p t c", p=P)
        xs = a["x_sample"].rearrange("b s c -> (b s) c")
        vec = lambda n, lo_=0, n_=None: a[n][0][lo_:(lo_ + n_ if n_ else a[n].shape[1])].rearrange("(t p) -> t p", p=P)

        block = ctx.enter_context(nc.Block())

        OPEN = 1
        OPENED = ["y_out_done", "ol_done", "b_taken", "acc_taken", "ohd_done", "gate_taken", "up_taken",
                  "states_stored", "s_ps", "conv_done", "sd_ps", "a_gated0", "a_gated1", "silu_done", "act_hi"]

        E = sem
        LEVELS = ("lv2", "lv4", "lv8", "lv16", "lv32")
        units = lambda lv: range(6) if lv < 3 else range(4)
        unit_tok = lambda u: slice(256, 384) if u >= 4 else slice(128 * (u % 2), 128 * (u % 2) + 128)
        unit_tile = lambda u: 2 if u >= 4 else u % 2
        unit_head = lambda u: u - 4 if u >= 4 else u // 2
        heads = lambda i: slice(64 * i, 64 * i + 64)
        seq17 = lambda t: t.rearrange("p (b t) -> p b t", t=17)
        seq16 = lambda t: t.rearrange("p (b t) -> p b t", t=TS)
        bc = lambda m, n: m.unsqueeze(1).to_broadcast([P, n, P])

        def pe_rwkv(f, pieces):
            pe, mm_ = nc.tensor, nc.tensor.matmul
            pieces(1)
            pe.wait_ge(E("y_out_done"), OPEN + f)
            pe.wait_ge(E("lora_w_in"), f * 48 + 48)
            mm_(ps[:, 2, 0:NT], wl[0:96, 0, :], za[0:96, 0, :], start=True, stop=True)
            mm_(ps[:, 3, 0:NT], wl[0:96, 1, :], za[0:96, 1, :], start=True, stop=True)
            for k in range(2):
                last = mm_(ps[:, 4, 0:NT], wg[:, k, :], za[:, 2 + k, :], start=k == 0, stop=k == 1)
            last.then_inc(E("lora_ps"), 1)
            pieces(1)
            pe.wait_ge(E("kk_sq_done"), f + 1)
            mm_(ps[:, 5, 0:NT], BON, sq[:, :], start=True, stop=True).then_inc(E("kk_sum_ps"), 1)
            pieces(2)
            pe.wait_ge(E("s0_in"), f * 32 + 32)
            pe.wait_ge(E("rk_done"), f + 1)
            mm_(ps[:, 6, 0:NT], BON, rk[:, :], start=True, stop=True).then_inc(E("rk_sum_ps"), 1)
            for b in range(NB):
                last = transpose(ps[:, 7, 64 * b:64 * b + 64], s0l[:, b, :])
            last.then_inc(E("s0_ps"), 1)
            pieces(3)
            pe.wait_ge(E("gates_done"), f + 1)
            pe.wait_ge(E("abkr_done"), f + 1)
            for i, src in enumerate((kp_, be)):
                for t in range(3):
                    transpose(ps[:, 2 + i, t * P:t * P + P], src[:, t * P:t * P + P])
            for t in range(3):
                last = transpose(ps[:, 4, t * P:t * P + P], z[:, 2, t * P:t * P + P])
            last.then_inc(E("tok_ps"), 1)
            pieces(1)
            pe.wait_ge(E("s0_done"), f + 1)
            for i in range(2):
                for b in range(NB):
                    last = mm_(ps[heads(i), 5, 16 * b:16 * b + 16], s0t[:, b, :],
                               al[:, i, 256 + 16 * b:272 + 16 * b], start=True, stop=True)
            last.then_inc(E("as_ps"), 1)
            pieces(1)
            pe.wait_ge(E("bonus_done"), f + 1)
            for u in range(6):
                last = mm_(unit(6, u), be[:, unit_tok(u)], al[:, unit_head(u), unit_tok(u)], start=True, stop=True)
            last.then_inc(E("nt_ps"), 1)
            pe.wait_ge(E("tok_done"), f + 1)
            pe.wait_ge(E("as_done"), f + 1)
            for u in range(6):
                last = mm_(unit(4, u), kp_[:, unit_tok(u)], al[:, unit_head(u), unit_tok(u)], start=True, stop=True)
            last.then_inc(E("mt_ps"), 1)
            pieces(1)
            pe.wait_ge(E("nt_done"), f + 1)
            for u in range(6):
                last = transpose(unit(2, u), n_t[:, u, :])
            last.then_inc(E("n_ps"), 1)
            pieces(2)
            for lv in range(5):
                pe.wait_ge(E("n_level_done"), f * 5 + (lv + 1))
                if lv == 0:
                    pe.wait_ge(E("t_first_done"), f + 1)
                    pe.wait_ge(E("mt_done"), f + 1)
                else:
                    pe.wait_ge(E("t_done"), f * 5 + lv)
                for u in units(lv):
                    last = mm_(unit(4, u), (c_k, c_b)[lv % 2][:, u, :], t_x[:, u, :], start=True, stop=True)
                last.then_inc(E("g_ps"), 1)
                pieces(1)
                pe.wait_ge(E("g_done"), f * 5 + (lv + 1))
                if lv < 4:
                    for u in units(lv):
                        last = mm_(unit(6, u), t_y[:, u, :], t_g[:, u, :], start=True, stop=True)
                for u in units(lv):
                    last = mm_(unit(2, u), t_g[:, u, :], t_y[:, u, :], start=True, stop=True)
                last.then_inc(E("dt_ps"), 1)
                pieces((2, 2, 2, 1, 1)[lv])
            pe.wait_ge(E("t_done"), f * 5 + 5)
            for b, src in ((4, kp_), (6, be)):
                for u in range(6):
                    last = mm_(unit(b, u), src[:, unit_tok(u)], rh[:, unit_head(u), unit_tok(u)],
                               start=True, stop=True)
                last.then_inc(E("c_ps"), 1)
            pieces(2)
            pe.wait_ge(E("c_done"), f * 2 + 2)

            v = tok[:, 2]
            for c in range(4):
                t, r0, cs = c // 2, 64 * (c % 2), slice(64 * (c % 2), 64 * (c % 2) + 64)
                cols = slice(64 * c, 64 * c + 64)
                if c:
                    pe.wait_ge(E("state_done"), f * 4 + c)
                for i in range(2):
                    last = mm_(ps[r0:r0 + 64, 2, heads(i)], m_t[:, 2 * i + t, cs], v[:, t, heads(i)],
                               start=True, stop=c == 0)
                    if c:
                        last = mm_(ps[r0:r0 + 64, 2, heads(i)], al[:, i, cols], st[:, 1, :], start=False, stop=True)
                last.then_inc(E("r_ps"), 1)
                if c == 0:
                    for i in range(2):
                        mm_(ps[:, 6, heads(i)], m_t[:, 4 + i, :], v[:, 2, heads(i)], start=True, stop=False)
                        last = mm_(ps[:, 6, heads(i)], asd[:, :], ident[:, heads(i)], start=False, stop=True)
                    last.then_inc(E("rd_ps"), 1)
                pieces(1)
                pe.wait_ge(E("r_done"), f * 4 + (c + 1))
                for i in range(2):
                    last = mm_(ps[r0:r0 + 64, 3, heads(i)], t_y[:, 2 * i + t, cs], rr[:, 0, heads(i)],
                               start=True, stop=True)
                last.then_inc(E("u_ps"), 1)
                if c == 0:
                    pieces(1)
                    pe.wait_ge(E("rd_done"), f + 1)
                    for i in range(2):
                        last = mm_(ps[:, 7, heads(i)], t_y[:, 4 + i, :], rr[:, 1, heads(i)], start=True, stop=True)
                    last.then_inc(E("ud_ps"), 1)
                gain = [ps[heads(i), 4, 0:64] for i in range(2)]
                yo = [ps[heads(i), 5, cols] for i in range(2)]
                for i in range(2):
                    mm_(gain[i], tok[r0:r0 + 64, 0, t, heads(i)], v[r0:r0 + 64, t, heads(i)], start=True, stop=False)
                    mm_(yo[i], v[:, t, heads(i)], c_k[:, 2 * i + t, cs], start=True, stop=False)
                    if c:
                        mm_(yo[i], st[:, 1, :], rh[:, i, cols], start=False, stop=False)
                pe.wait_ge(E("u_done"), f * 4 + (c + 1))
                mm_(yo[0], un[:, 0, heads(0)], c_b[:, t, cs], start=False, stop=True)
                for i in range(2):
                    last = mm_(gain[i], tok[r0:r0 + 64, 1, t, heads(i)], un[r0:r0 + 64, 0, heads(i)],
                               start=False, stop=True)
                last.then_inc(E("state_ps"), 1)
                mm_(yo[1], un[:, 0, heads(1)], c_b[:, 2 + t, cs], start=False, stop=True).then_inc(E("y_ps"), 1)
                if c == 0:
                    pe.wait_ge(E("ud_done"), f + 1)
                    for i in range(2):
                        o = ps[heads(i), 5, 256:384]
                        mm_(o, v[:, 2, heads(i)], c_k[:, 4 + i, :], start=True, stop=False, skip_group_check=True)
                        mm_(o, un[:, 1, heads(i)], c_b[:, 4 + i, :], start=False, stop=False, skip_group_check=True)
                        for b in range(NB):
                            last = mm_(ps[heads(i), 5, 256 + 16 * b:272 + 16 * b], s0t[:, b, :],
                                       rh[:, i, 256 + 16 * b:272 + 16 * b], start=False, stop=b == NB - 1,
                                       skip_group_check=True)
                    last.then_inc(E("yd_ps"), 1)
                if c in (1, 2):
                    pe.wait_ge(E("vx_done"), f * 2 + c)
                    for i in range(2):
                        last = mm_(ps[heads(i), 6 + (c - 1), :], tok[:, c - 1, 2, heads(i)],
                                   vx[:, i].rearrange("p b v -> p (b v)"), start=True, stop=True)
                    last.then_inc(E("sd_ps"), 1)
            pe.wait_ge(E("state_done"), f * 4 + 4)
            pe.wait_ge(E("y_raw_done"), f + 1)
            mm_(ps[:, 3, 0:NT], BON, yb[:, :], start=True, stop=True).then_inc(E("mean_ps"), 1)
            transpose(ps[0:64, 2, 0:P], st[:, 0, :]).then_inc(E("sp_t_ps"), 1)
            pe.wait_ge(E("sd_done"), f + 1)
            pe.wait_ge(E("y_sq_done"), f + 1)
            mm_(ps[:, 4, 0:NT], BON, sq[:, :], start=True, stop=True).then_inc(E("var_ps"), 1)
            for b in range(NB):
                last = transpose(ps[0:64, 6 + b // 4, (b % 4) * P:(b % 4 + 1) * P], s0t[:, b, :])
            last.then_inc(E("sd_t_ps"), 1)

        def act_rwkv(f, cut, ch):
            act, fn = nc.scalar, nc.scalar.activation
            cut(0)
            act.wait_ge(E("lora_ps"), f + 1)
            act.wait_ge(E("pf_done"), f + 1)
            fn(sw[:, :], ps[:, 2, 0:NT], ACT.Sigmoid, bias=pf[:, 3:4])
            fn(aa[:, :], ps[:, 3, 0:NT], ACT.Sigmoid, bias=pf[:, 4:5])
            fn(gg[:, :], ps[:, 4, 0:NT], ACT.Copy).then_inc(E("gates_done"), 1)
            act.wait_ge(E("kk_raw_done"), f + 1)
            fn(sq[:, :], kk0[:, :], ACT.Square).then_inc(E("kk_sq_done"), 1)
            act.wait_ge(E("kk_clamped"), f + 1)
            ch.link(fn(rn[:, :], rn[:, :], ACT.Ln))
            ch.link(fn(rn[:, :], rn[:, :], ACT.Exp, scale=-0.5))
            act.wait_ge(E("decay_sums_done"), f + 1)
            fn(e1[:, :], cu[:, :], ACT.Exp, scale=-CDEC)
            fn(e2[:, :], cu[:, :], ACT.Exp, scale=CDEC)
            fn(e3[:, :], dx[:, :], ACT.Exp, scale=-CDEC)
            fn(emid[:, :, :], mid[:, :, :], ACT.Exp, scale=-CDEC).then_inc(E("exps_done"), 1)
            act.wait_ge(E("s0_ps"), f + 1)
            fn(s0t[:, :, :], ps[:, 7, :].rearrange("p (b v) -> p b v", b=NB), ACT.Copy).then_inc(E("s0_done"), 1)
            cut(1)
            act.wait_ge(E("tok_ps"), f + 1)
            fn(tok[:, :, :, :].rearrange("p a t c -> p a (t c)"), ps[:, 2:5, 0:NT], ACT.Copy)\
                .then_inc(E("tok_done"), 1)
            act.wait_ge(E("as_ps"), f + 1)
            fn(asd[:, :], ps[:, 5, 0:P], ACT.Copy).then_inc(E("as_done"), 1)
            cut(2)
            for lv in range(5):
                act.wait_ge(E("g_ps"), f * 5 + (lv + 1))
                n = len(units(lv))
                fn(t_g[:, 0:n, :], pair(4).rearrange("p (u c) -> p u c", u=6)[:, 0:n, :], ACT.Copy)\
                    .then_inc(E("g_done"), 1)
                if lv != 3:
                    cut((3, 4, 5, 0, 6)[lv])
            act.wait_ge(E("rd_ps"), f + 1)
            fn(rr[:, 1, :], ps[:, 6, 0:P], ACT.Copy).then_inc(E("rd_done"), 1)
            cut(7)
            act.wait_ge(E("ud_ps"), f + 1)
            fn(un[:, 1, :], ps[:, 7, 0:P], ACT.Copy, scale=-1.0).then_inc(E("ud_done"), 1)
            act.wait_ge(E("yd_ps"), f + 1)
            act.wait_ge(E("y_ps"), f * 4 + 4)
            fn(yb[:, :], ps[:, 5, 0:NT], ACT.Copy).then_inc(E("y_raw_done"), 1)
            act.wait_ge(E("sp_t_ps"), f + 1)
            act.wait_ge(E("states_stored"), OPEN + f)
            fn(sto[:, :], ps[0:64, 2, 0:P], ACT.Copy).then_inc(E("s_out"), 1)
            act.wait_ge(E("y_centred"), f + 1)
            fn(sq[:, :], yc[:, :], ACT.Square).then_inc(E("y_sq_done"), 1)
            act.wait_ge(E("sd_t_ps"), f + 1)
            fn(so[:, :, :].rearrange("v (h b) c -> v h (b c)", h=2), ps[0:64, 6:8, :], ACT.Copy)\
                .then_inc(E("so_done"), 1)
            act.wait_ge(E("var_ps"), f + 1)
            ch.link(fn(rn[:, :], ps[:, 4, 0:NT], ACT.Ln, scale=1.0 / 64, bias=gneps))
            fn(rn[:, :], rn[:, :], ACT.Exp, scale=-0.5).then_inc(E("y_rstd_done"), 1)

        def dve_rwkv(f, cut, ch):
            dve = nc.vector
            tt, stt3, cp = nc.vector.tensor_tensor, nc.vector.scalar_tensor_tensor, nc.vector.tensor_copy
            M, A, S = ALU.mult, ALU.add, ALU.subtract
            link = ch.link
            cp(pf[:, :], prm[:, 0:80].rearrange("p (g f) -> p g f", f=FT)[:, :, bass.ds(f, 1)].squeeze(2))\
                .then_inc(E("pf_done"), 1)
            link(cp(pb[:, :, 257:PAD:17],
                    shm[:, :, :].rearrange("p b (i f) -> p i f b", f=FT)[:, :, bass.ds(f, 1), :].squeeze(2)))
            dve.wait_ge(E("pf_done"), f + 1)
            dve.wait_ge(proj_taken, f * 4 + (T_FT + 3))
            dve.wait_ge(E("sd_ps"), OPEN + f * 2)
            link(tt(db[:, :, 0:PAD - 1], pb[:, :, 0:PAD - 1], pb[:, :, 1:PAD], S))
            for i in range(3):
                stt3(z[:, i, 0:NP_], db[:, i, 0:NP_], pf[:, i:i + 1], pb[:, i, 1:257], M, A)
                stt3(seq16(z[:, i, NP_:NT]), seq17(db[:, i, 257:PAD])[:, :, 0:TS], pf[:, i:i + 1],
                     seq17(pb[:, i, 257:PAD])[:, :, 1:17], M, A)
            col = lambda q, n: tail[:, q:q + n, :].rearrange("p q (i f) -> p q i f", f=FT)[:, :, :, bass.ds(f, 1)]
            cp(col(0, 1).squeeze(3).squeeze(1), pb[:, :, 256])
            cp(col(1, 8).squeeze(3), pb[:, :, 273:PAD:17].rearrange("p i b -> p b i")).then_inc(E("z_done"), 1)
            dve.wait_ge(E("z_done"), f + 1)
            zr, zk, zv = z[:, 0, :], z[:, 1, :], z[:, 2, :]
            nc.vector.tensor_scalar(kk0[:, :], zk, pf[:, 5:6], None, M).then_inc(E("kk_raw_done"), 1)
            cut(0)
            dve.wait_ge(E("gates_done"), f + 1)
            link(nc.vector.tensor_tensor_scan(cu[:, :], reset, sw[:, :], 0.0, M, A))
            c4 = cu[:, 0:NP_].rearrange("p (c t) -> p c t", c=4)
            link(cp(mid[:, :, :], c4[:, :, 31:64:32]))
            link(tt(c4, c4, mid[:, :, 0:1].to_broadcast([P, 4, 64]), S))
            tt(dx[:, :], cu[:, :], sw[:, :], S).then_inc(E("decay_sums_done"), 1)
            dve.wait_ge(E("kk_sum_ps"), f + 1)
            nc.vector.tensor_scalar(rn[:, :], ps[:, 5, 0:NT], 1e-12, None, ALU.max).then_inc(E("kk_clamped"), 1)
            link(nc.vector.tensor_scalar(t1[:, :], aa[:, :], -1.0, pf[:, 6:7], A, M))
            link(stt3(k2[:, :], t1[:, :], 1.0, zk, A, M))
            stt3(rk[:, :], zr, pf[:, 7:8], k2[:, :], M, M).then_inc(E("rk_done"), 1)
            dve.wait_ge(E("exps_done"), f + 1)
            tt(kp_[:, :], k2[:, :], e2[:, :], M)
            link(tt(rn[:, :], kk0[:, :], rn[:, :], M))
            for i in range(2):
                h = heads(i)
                tt(al[h, i, :], rn[h, :], e3[h, :], M)
                tt(rh[h, i, :], z[h, 0, :], e1[h, :], M)
            link(tt(kka[:, :], rn[:, :], aa[:, :], M))
            tt(be[:, :], kka[:, :], e2[:, :], M).then_inc(E("abkr_done"), 1)
            cut(1)
            dve.wait_ge(E("rk_sum_ps"), f + 1)
            tt(rk[:, :], ps[:, 6, 0:NT], zv, M).then_inc(E("bonus_done"), 1)
            cut(2)
            u6 = lambda b, lo_, n: ps[:, b + lo_ // 4, 0:n * P].rearrange("p (u c) -> p u c", u=n)

            def masked(dst, b, masks):
                tt(dst[:, 0:4, :], u6(b, 0, 4), bc(masks[0], 4), M)
                return tt(dst[:, 4:6, :], u6(b, 4, 2), bc(masks[1], 2), M)
            dve.wait_ge(E("nt_ps"), f + 1)
            masked(n_t, 6, M_S).then_inc(E("nt_done"), 1)
            dve.wait_ge(E("nt_done"), f + 1)
            link(tt(t_y[:, :, :], n_t[:, :, :], bc(cm["nl1"], 6), M))
            link(tt(t_y[:, :, :], t_y[:, :, :], bc(ident, 6), A))
            dve.wait_ge(E("mt_ps"), f + 1)
            masked(m_t, 4, M_S).then_inc(E("mt_done"), 1)
            dve.wait_ge(E("n_ps"), f + 1)
            link(masked(t_x, 2, (cm["nl1t"], cm["nl1t"])))
            tt(t_x[:, :, :], t_x[:, :, :], bc(ident, 6), A).then_inc(E("t_first_done"), 1)
            dve.wait_ge(E("t_first_done"), f + 1)
            for lv in range(5):
                if lv in (0, 1, 3):
                    cut((3, 4, 0, 5)[lv])
                dve.wait_ge(E("dt_ps"), f * 5 + (lv + 1))
                for lo_, n in ((0, 4), (4, 2)) if lv < 3 else ((0, 4),):
                    if lv < 4:
                        tt(t_x[:, lo_:lo_ + n, :], t_x[:, lo_:lo_ + n, :], u6(6, lo_, n), S)
                    last = tt(t_y[:, lo_:lo_ + n, :], t_y[:, lo_:lo_ + n, :], u6(2, lo_, n), S)
                last.then_inc(E("t_done"), 1)
                dve.wait_ge(E("t_done"), f * 5 + (lv + 1))
            cut(6)
            for j, (dst, b) in enumerate(((c_k, 4), (c_b, 6))):
                dve.wait_ge(E("c_ps"), f * 2 + (j + 1))
                masked(dst, b, M_I).then_inc(E("c_done"), 1)
            for c in range(4):
                r = slice(64 * (c % 2), 64 * (c % 2) + 64)
                dve.wait_ge(E("r_ps"), f * 4 + (c + 1))
                cp(rr[r, 0, :], ps[r, 2, 0:P]).then_inc(E("r_done"), 1)
                dve.wait_ge(E("u_ps"), f * 4 + (c + 1))
                nc.vector.tensor_scalar(un[r, 0, :], ps[r, 3, 0:P], -1.0, None, M).then_inc(E("u_done"), 1)
                dve.wait_ge(E("state_ps"), f * 4 + (c + 1))
                e_last = e1[:, 64 * c + 63:64 * c + 64]
                if c == 0:
                    link(nc.vector.tensor_scalar(st[:, 0, :], ps[:, 4, 0:64], e_last, None, M))
                elif c < 3:
                    link(stt3(st[:, 0, :], ps[:, 4, 0:64], e_last, st[:, 2, :], M, A))
                else:
                    stt3(st[:, 0, :], ps[:, 4, 0:64], e_last, st[:, 2, :], M, A).then_inc(E("state_done"), 1)
                if c < 3:
                    dve.wait_ge(E("y_ps"), f * 4 + (c + 1))
                    nc.vector.tensor_scalar(st[:, 2, :], st[:, 0, :], emid_tot(c + 1), None, M)
                    nc.vector.tensor_scalar(st[:, 1, :], st[:, 0, :], emid[:, c + 1, 0:1], None, M)\
                        .then_inc(E("state_done"), 1)
                    dve.wait_ge(E("state_done"), f * 4 + (c + 1))
                if c == 0:
                    cut(7)
                if c < 2:
                    if c == 0:
                        dve.wait_ge(E("tok_done"), f + 1)
                    else:
                        dve.wait_ge(E("ud_done"), f + 1)
                        dve.wait_ge(E("sd_ps"), OPEN + f * 2 + 1)
                    src = tok[:, 2, 2, :] if c == 0 else un[:, 1, :]
                    for i in range(2):
                        last = tt(vx[:, i], src[:, heads(i)].unsqueeze(1).to_broadcast([P, NB, 64]),
                                  bmask.unsqueeze(2).to_broadcast([P, NB, 64]), M)
                    last.then_inc(E("vx_done"), 1)
            dve.wait_ge(E("yd_ps"), f + 1)
            dve.wait_ge(E("sd_ps"), OPEN + f * 2 + 2)
            p3 = lambda b: ps[:, b, :].rearrange("p (b v) -> p b v", b=NB)
            link(tt(s0t[:, :, :], s0t[:, :, :], p3(6), A))
            link(tt(s0t[:, :, :], s0t[:, :, :], p3(7), A))
            tt(s0t[:, :, :], s0t[:, :, :],
               e1[:, 256 + TS - 1:NT:TS].unsqueeze(2).to_broadcast([P, NB, 64]), M).then_inc(E("sd_done"), 1)
            dve.wait_ge(E("mean_ps"), f + 1)
            stt3(yc[:, :], ps[:, 3, 0:NT], -1.0 / 64, yb[:, :], M, A).then_inc(E("y_centred"), 1)
            dve.wait_ge(E("y_rstd_done"), f + 1)
            dve.wait_ge(E("y_centred"), f + 1)
            link(tt(yc[:, :], yc[:, :], rn[:, :], M))
            link(nc.vector.tensor_scalar(yc[:, :], yc[:, :], pf[:, 8:9], pf[:, 9:10], M, A))
            link(tt(yc[:, :], yc[:, :], rk[:, :], A))
            tt(oa[:, bass.ds(f, 1), :].squeeze(1), yc[:, :], gg[:, :], M).then_inc(E("y_out_done"), 1)
            dve.wait_ge(E("y_out_done"), OPEN + f + 1)

        emid_tot = lambda c: emid[:, c, 1:2]
        def full(t):
            return 16 * t + 16 + 16 * min(max(t - (T_MLA + 3), 0), 5)

        def act_hi(t, s, cnt=None):
            nc.scalar.wait_ge(raw_full[s], full(t) if cnt is None else cnt)
            if not (isinstance(t, int) and t == 0):
                nc.scalar.wait_ge(blk_used, t * 2 + (s - 1))
            nc.scalar.activation(hi[:, s], raw[:, s], ACT.Copy).then_inc(hi_done, 1)

        def dve_lo(t, s):
            nc.vector.wait_ge(hi_done, t * 2 + (s + 1))
            nc.vector.tensor_tensor(lo[:, s], raw[:, s], hi[:, s].bitcast(F32), ALU.subtract).then_inc(lo_done, 1)

        def pe_block(t, s, out, ks=range(8)):
            if ks[0] == 0:
                nc.tensor.wait_ge(lo_done, t * 2 + (s + 1))
            for k in ks:
                kt = 8 * s + k
                nc.tensor.matmul(out, hi[:, s, k, :], xh[:, kt, :], start=kt == 0, stop=False)
                nc.tensor.matmul(out, hi[:, s, k, :], xl[:, kt, :], start=False, stop=False)
                last = nc.tensor.matmul(out, lo[:, s, k, :], xh[:, kt, :], start=False, stop=kt == 15)
            if ks[-1] == 7:
                last.then_inc(blk_used, 1)

        def pe_half(t, s, xh_, xl_, out, ks=range(8)):
            if ks[0] == 0:
                nc.tensor.wait_ge(lo_done, t * 2 + (s + 1))
            for k in ks:
                nc.tensor.matmul(out, hi[:, s, k, :], xh_[:, k, :], start=k == 0, stop=False)
                nc.tensor.matmul(out, hi[:, s, k, :], xl_[:, k, :], start=False, stop=False)
                last = nc.tensor.matmul(out, lo[:, s, k, :], xh_[:, k, :], start=False, stop=k == 7)
            if ks[-1] == 7:
                last.then_inc(blk_used, 1)

        def pe_proj(t, p):
            if p >= 2:
                nc.tensor.wait_ge(proj_taken, p - 1)
            for s in range(2):
                pe_block(t, s, ps[:, p % 2, 0:NT])

        def act_next(t, end=False):
            static = isinstance(t, int)
            act_hi(t, 1, full(t) if static else t * 16 + 96)
            if not end:
                act_hi(t + 1, 0, full(t + 1) if static else t * 16 + 112)

        def dve_next(t, end=False):
            dve_lo(t, 1)
            if not end:
                dve_lo(t + 1, 0)

        def pe_norm(src, first, ready, taken):
            for kt in range(KD):
                bank = 2 + kt % 6
                if kt == 0:
                    nc.tensor.wait_ge(ready, 3)
                if kt >= 6:
                    nc.tensor.wait_ge(taken, first * KD + kt - 5)
                for t in range(3):
                    last = transpose(ps[:, bank, t * P:t * P + P], src[:, t, kt * P:kt * P + P])
                last.then_inc(E("norm_ps"), 1)

        def act_norm_stats(src, sq_out, arrived, ch):
            for t in range(3):
                arrived(t)
                nc.scalar.activation(sq_out, src[:, t, :], ACT.Square, accum_out=stat[:, t:t + 1])\
                    .then_inc(E("sum_sq"), 1)
                nc.scalar.wait_ge(E("sum_sq"), sumsq[0] + t + 1)
            sumsq[0] += 3
            ch.link(nc.scalar.activation(stat[:, 3:6], stat[:, 0:3], ACT.Ln, scale=1.0 / D, bias=epsb))
            nc.scalar.activation(stat[:, 0:3], stat[:, 3:6], ACT.Exp, scale=-0.5).then_inc(E("rstd_done"), 1)
        sumsq = [0]
        epsb, gneps = EPS, GN_EPS

        def act_norm(first, gcol):
            for kt in range(KD):
                nc.scalar.wait_ge(E("norm_ps"), first * KD + kt + 1)
                nc.scalar.activation(xh[:, kt, :], ps[:, 2 + kt % 6, 0:NT], ACT.Identity,
                                     scale=prm[:, gcol + kt:gcol + kt + 1]).then_inc(E("xh_done"), 1)

        def dve_norm(first, gcol):
            for kt in range(KD):
                nc.vector.wait_ge(E("xh_done"), first * KD + kt + 1)
                nc.vector.scalar_tensor_tensor(xl[:, kt, :], ps[:, 2 + kt % 6, 0:NT], prm[:, gcol + kt:gcol + kt + 1],
                                               xh[:, kt, :].bitcast(F32), ALU.mult, ALU.subtract)\
                    .then_inc(E("xt_lo"), 1)

        @block.sync
        def _(sp):
            def block_in(t, s, dst, src):
                sp.dma_start(dst, src).then_inc(raw_full[s], 16)

            def free(t, s):
                if not (isinstance(t, int) and t == 0):
                    sp.wait_ge(lo_done, t * 2 + (s - 1))

            def tile_in(t, src):
                for s in range(2):
                    free(t, s)
                    block_in(t, s, raw[:, s], src(s))

            sp.dma_start(c1[:, :], consts[:, 0:NC1]).then_inc(sem("c1_in"), 16)
            for t in range(3):
                sp.dma_start(xt[:, t, :], xp[:, t, :] if t < 2 else xs).then_inc(sem(f"x_in{t}"), 16)
            for j, c in enumerate((3072, 3168, 3264, 3392)):
                tile_in(T_LORA + j, lambda s: w_in[s][:, :, c:c + P])
            with sp.Fori(0, FT) as f:
                for q, (c, w) in enumerate(((0, P), (W, P), (2 * W, P), (Q0, 192))):
                    tile_in(T_FT + q + f * 4, lambda s: w_in[s][:, :, bass.ds(f * w + c, P)])
            for j in range(9):
                t = T_MLA + j
                for s in range(2):
                    free(t, s)
                    if j < 4:
                        c = CKV0 + j * P
                        block_in(t, s, raw[:, s], w_in[s][:, :, c:c + P])
                    else:
                        g0 = Q0 + 384 * (j - 4)
                        cols = (g0 + 128, g0 + 320) if j < 8 else (KR0, KR0)
                        for g, c in enumerate(cols):
                            block_in(t, s, raw[:, s, :, 64 * g:64 * g + 64], w_in[s][:, :, c:c + 64])
            for t0, g, w, j0, pairs in ((T_MIX, 0, 0, KD // 2, 4), (T_MIX + 12, 0, 0, 0, 4), (T_MIX_B, D, 1, 0, 8)):
                with sp.Fori(1, pairs + 1) as i1:
                    for q in range(2):
                        tile_in(i1 * 3 + (t0 + q - 3),
                                lambda s: w_in[s][:, :, bass.ds(i1 * (2 * P) + (G0 + g + (j0 + q - 2) * P), P)])
                    tile_in(i1 * 3 + (t0 - 1),
                            lambda s: w_oab[w][:, :, bass.ds(i1 * (2 * P) + (j0 + s - 2) * P, P)])

            def wide_tiles(t0, ch, count, w, row0):
                with sp.Fori(0, count) as i:
                    t = i + t0
                    for s in range(2):
                        free(t, s)
                        src = w[bass.ds(i * 2 + (row0 + s), 1), :, bass.ds(ch, 1), :].squeeze(2).squeeze(0)
                        sp.dma_start(raw[:, s].rearrange("p k c -> p (k c)"), src).then_inc(raw_full[s], 16)

            with sp.Fori(0, 2) as ch:
                wide_tiles(ch * 8 + T_OUT, ch, 8, w_out, 0)
            with sp.Fori(0, 2) as hf:
                with sp.Fori(0, HJ) as j:
                    for q in range(2):
                        tile_in(hf * T_HALF + j * 2 + (T_FFN + q),
                                lambda s: w_ffn[s][:, :, bass.ds(hf * (HJ * P) + j * P + q * DFF, P)])
                with sp.Fori(0, 2) as ch:
                    wide_tiles(hf * T_HALF + ch * 11 + (T_FFN + 2 * HJ), ch, 11, w_dn, hf * HJ)

        @block.gpsimd
        def _(pool):
            for name in OPENED:
                pool.sem_inc(sem(name), OPEN)
            seen = sem("params_in")
            n = [0]

            def load(dst, src):
                pool.dma_start(dst, src).then_inc(seen, 16)
                n[0] += 16
            load(rows[0:24, 0, :], vec("mu_shift", 0, 3072))
            for i, nm in enumerate(("w0", "a0", "k_k", "k_a")):
                load(rows[24 + 8 * i:32 + 8 * i, 0, :], vec(nm))
            load(rows[56:64, 0, :], a["r_k"][0].rearrange("(t h) n -> t (h n)", h=2))
            load(rows[64:72, 0, :], vec("lnx_g"))
            load(rows[72:80, 0, :], vec("lnx_b"))
            load(rows[80:96, 0, :], vec("g_mix"))
            load(rows[96:112, 0, :], vec("g_ffn"))
            for i, c in enumerate((3072, 3168, 3264, 3392)):
                load(rows[112 + i:113 + i, 0, :], vec("mu_shift", c, P))
                load(rows[8 * i:8 * i + 8, 13, :], a["state_rwkv_shift"][0, :, 0, c:c + P])
            load(rows[116:120, 0, :], vec("g_kv"))
            load(rows[0:88, 1, :], a["conv_w"][0, 0:2, :].rearrange("j (t p) -> (j t) p", p=P))
            load(rows[0:44, 2, :], a["conv_w"][0, 2, :].rearrange("(t p) -> t p", p=P))
            load(rows[44:88, 2, :], vec("conv_b"))
            for b in range(NB):
                load(rows[0:88, 3 + b, :], a["state_ffn_conv"][0, b].rearrange("r (t p) -> (r t) p", p=P))
                load(rows[24 * (b % 4):24 * (b % 4) + 24, 11 + b // 4, :],
                     a["state_rwkv_shift"][0, b, 0, 0:3072].rearrange("(t p) -> t p", p=P))
            n_params[0] = n[0]
            pool.dma_start(c2[:, :], consts[:, NC1:NC1 + NC2]).then_inc(sem("c2_in"), 16)

            def lora_in(f):
                for i, nm in enumerate(("w2", "a2")):
                    pool.dma_start(wl[0:96, i, :], a[nm][0][:, bass.ds(f * P, P)]).then_inc(sem("lora_w_in"), 16)
                pool.dma_start(wg[:, :, :], a["g2"][0].rearrange("(k p) c -> p k c", p=P)[:, :, bass.ds(f * P, P)])\
                    .then_inc(sem("lora_w_in"), 16)

            def s0_in(f):
                for i in range(2):
                    src = a["state_rwkv_wkv"][0].rearrange("b (f i) v k -> i f v b k", i=2)[i][bass.ds(f, 1)]
                    pool.dma_start(s0l[:, :, 64 * i:64 * i + 64], src.squeeze(0)).then_inc(sem("s0_in"), 16)

            pool.wait_ge(sem("xt_lo"), KD)
            lora_in(0)
            s0_in(0)

            def rwkv(f, last):
                pool.wait_ge(sem("nt_done"), f + 1)
                for lv, name in enumerate(LEVELS):
                    if lv >= 2:
                        pool.wait_ge(sem("g_ps"), f * 5 + (lv - 1))
                    n_u = len(units(lv))
                    nc.gpsimd.tensor_tensor((c_k, c_b)[lv % 2][:, 0:n_u, :], n_t[:, 0:n_u, :], bc(cm[name], n_u),
                                            ALU.mult).then_inc(sem("n_level_done"), 1)
                if not last:
                    pool.wait_ge(sem("gates_done"), f + 1)
                    lora_in(f + 1)
                    pool.wait_ge(sem("s0_done"), f + 1)
                    s0_in(f + 1)
                pool.wait_ge(sem("s_out"), f + 1)
                pool.wait_ge(sem("so_done"), f + 1)
                dst = wkv_s[0].rearrange("b (f i) v k -> i f v b k", i=2)
                dp = wkv_p[0, 0].rearrange("(f i) v k -> f v i k", i=2)
                one = lambda ap: ap[f] if last else ap[bass.ds(f, 1)].squeeze(0)
                for i in range(2):
                    pool.dma_start(one(dst[i]), so[:, :, 64 * i:64 * i + 64]).then_inc(sem("state_stores"), 16)
                pool.dma_start(one(dp), sto[:, :].rearrange("v (i k) -> v i k", i=2))\
                    .then_inc(sem("state_stores"), 16)
                pool.wait_ge(sem("state_stores"), f * 48 + 48)
                pool.sem_inc(sem("states_stored"), 1)

            pool.wait_ge(sem("c2_in"), 16)
            with pool.Fori(0, FT - 1) as f:
                rwkv(f, False)
            rwkv(FT - 1, True)

            pool.wait_ge(sem("y_out_done"), OPEN + FT)
            pool.dma_start(c3[:, :], consts[:, NC1 + NC2:NC1 + NC2 + NC3]).then_inc(sem("c3_in"), 16)
            w_ukv = a["w_ukv"][0].rearrange("(k p) c -> p k c", p=P)

            def head_in(i, hh):
                pool.dma_start(wuk[:, hh], w_ukv[:, :, bass.ds(i * 512 + 256 * hh, 256)])\
                    .then_inc(sem(f"wuk_in{hh}"), 16)

            def past_in(i, bb):
                b = i * 2 + bb
                one = lambda ap: ap[bass.ds(b, 1)].squeeze(0)
                pool.dma_start(lp[:, bb, :], one(a["cache_mla_latent"][0])).then_inc(sem(f"past_in{bb}"), 16)
                pool.dma_start(kpast[:, bb], one(a["cache_mla_krope"][0]).unsqueeze(1).to_broadcast([P, 2, 64]))\
                    .then_inc(sem(f"past_in{bb}"), 16)
                pool.dma_start(lnew[0:TS, bb, :], one(lat_s[0])).then_inc(sem(f"past_in{bb}"), 16)

            for hh in range(2):
                head_in(0, hh)
            pool.wait_ge(sem("latent_rows_done"), 1)
            store(pool, lat_p[0, 0].rearrange("(t p) c -> p t c", p=P), ltok[:, 0:2, :])
            pool.dma_start(lat_s[0].rearrange("b s c -> (b s) c"), ltok[:, 2, :]).then_inc(sem("new_latent_stored"), 16)
            store(pool, kr_p[0, 0].rearrange("(t p) c -> p t c", p=P), krt[:, 0:2, :])
            store(pool, kr_s[0].rearrange("b s c -> (b s) c"), krt[:, 2, :])
            pool.wait_ge(sem("new_latent_stored"), 16)
            pool.wait_ge(sem("latent_done"), 1)
            for bb in range(2):
                past_in(0, bb)
            with pool.Fori(0, 3) as i:
                for hh in range(2):
                    pool.wait_ge(sem("oh_ps"), i * 2 + (hh + 1))
                    head_in(i + 1, hh)
            for hh in range(2):
                pool.wait_ge(sem("oh_ps"), 7 + hh)
                head_in(0, hh)
            with pool.Fori(0, 3) as i:
                for bb in range(2):
                    pool.wait_ge(sem("old_ps"), i * 2 + (bb + 1))
                    past_in(i + 1, bb)
            with pool.Fori(0, 3) as i:
                for hh in range(2):
                    pool.wait_ge(sem("ohd_ps"), i * 2 + (hh + 1))
                    head_in(i + 1, hh)
            pool.wait_ge(blk_used, 2 * T_OUT)
            for t in range(3):
                pool.dma_start(ht[:, t, :], xp[:, t, :] if t < 2 else xs).then_inc(sem("h_in"), 16)
            pool.wait_ge(sem("act_done"), 2 * HJ)
            pool.dma_start(gf[:, :], a["g_final"].partition_broadcast(P)).then_inc(sem("gf_in"), 16)
            for t in range(3):
                pool.wait_ge(sem("y_ready"), t + 1)
                store(pool, y_prompt[0].rearrange("(t p) c -> p t c", p=P)[:, t, :] if t < 2
                      else y_sample.rearrange("b s c -> (b s) c"), hn[:, t, :])
            pool.wait_ge(sem("tails_done"), 1)
            for q in range(9):
                dst = conv_p[0, 0] if q == 0 else conv_s[0, q - 1]
                store(pool, dst.rearrange("r (t p) -> (r t) p", p=P), ctr[:, q, :])
            pool.wait_ge(sem("rkv_tails_done"), 1)
            shp, shs = shift_p[0, 0], shift_s[0, :, 0]
            for q in range(9):
                dst = (shp[0] if q == 0 else shs[q - 1])[0:3072].rearrange("(t p) -> t p", p=P)
                store(pool, dst, rowt[24 * (q % 3):24 * (q % 3) + 24, q // 3, :])
            for l, (c, w) in enumerate(((3072, 96), (3168, 96), (3264, P), (3392, P))):
                store(pool, shp[:, c:c + w], rowt[9 * l:9 * l + 1, 3, 0:w])
                store(pool, shs[:, c:c + w], rowt[9 * l + 1:9 * l + 9, 3, 0:w])
            pool.wait_ge(stores, n_stores[0])

        @block.tensor
        def _(pe):
            mm_ = nc.tensor.matmul
            pe.wait_ge(E("c1_in"), 16)
            pe.wait_ge(E("params_in"), n_params[0])
            for i, (r, bank) in enumerate(PARAM_ROWS):
                last = transpose(ps[:, 2 + i // 4, (i % 4) * P:(i % 4) * P + r], rows[0:r, i, :])
            last.then_inc(E("params_ps"), 1)
            pe.wait_ge(E("params_done"), 1)
            pe_norm(xt, 0, E("x_scaled"), E("xt_lo"))
            pe.wait_ge(E("xt_lo"), KD)
            for t in range(4):
                pe_proj(T_LORA + t, t)
            pe.wait_ge(E("c2_in"), 16)
            for q in range(4):
                pe_proj(T_FT + q, 4 + q)
            pe.wait_ge(E("z_lora_done"), 4)
            pe.wait_ge(E("zeroed"), 1)

            with pe.Fori(0, FT - 1) as f:
                done = 0

                def pieces(n):
                    nonlocal done
                    for piece in range(done, done + n):
                        q, s, part = piece // 8, piece // 4 % 2, piece % 4
                        if piece % 8 == 0:
                            pe.wait_ge(proj_taken, f * 4 + (8 + q - 1))
                        pe_block(f * 4 + (T_FT + 4 + q), s, ps[:, q % 2, 0:NT], range(2 * part, 2 * part + 2))
                    done += n
                pe_rwkv(f, pieces)
                assert done == 32
            done = 0

            def last_pieces(n):
                nonlocal done
                for piece in range(done, done + n):
                    q, s, part = piece // 8, piece // 4 % 2, piece % 4
                    if piece % 8 == 0:
                        pe.wait_ge(proj_taken, T_MLA + q - 1)
                    pe_block(T_MLA + q, s, ps[:, (T_MLA + q) % 2, 0:NT], range(2 * part, 2 * part + 2))
                done += n
            pe_rwkv(FT - 1, last_pieces)

            for j in range(4, 9):
                pe_proj(T_MLA + j, T_MLA + j)
            pe.wait_ge(E("c3_in"), 16)
            pe.wait_ge(E("y_out_done"), OPEN + FT)
            pe.wait_ge(E("c_sq_done"), 1)
            for j in range(4):
                last = mm_(ps[:, 7, 0:NT], ones, csq[:, j, :], start=j == 0, stop=j == 3)
            last.then_inc(E("c_sum_ps"), 1)
            pe.wait_ge(proj_taken, T_MIX)
            for j in range(5):
                last = mm_(ps[:, 2 + j, 0:NT], rot, (kr2 if j == 4 else qrp[:, j])[:, :], start=True, stop=True)
            last.then_inc(E("rot_ps"), 1)
            pe.wait_ge(E("rope_done"), 1)
            pe.wait_ge(E("latent_done"), 1)
            for t in range(3):
                for j in range(4):
                    transpose(ps[:, 2 + t, j * P:j * P + P], latt[:, j, t * P:t * P + P])
                last = transpose(ps[:, 5, t * P:t * P + P], kr2[:, t * P:t * P + P])
            last.then_inc(E("latent_rows_ps"), 1)

            def side(pair_no):
                done = 0

                def pieces(n):
                    nonlocal done
                    for piece in range(done, done + n):
                        b, part = piece // 4, piece % 4
                        t, q, s = pair_no * 3 + (T_MIX + b // 2), b // 2, b % 2
                        ks = range(2 * part, 2 * part + 2)
                        if q < 2:
                            if piece % 8 == 0:
                                pe.wait_ge(E(f"a_gated{q}"), OPEN + pair_no)
                            pe_block(t, s, ps[:, q, 0:NT], ks)
                        else:
                            if part == 0:
                                pe.wait_ge(proj_taken, pair_no * 2 + (T_MIX + s + 1))
                            pe_half(t, s, oah, oal, ps[:, s, 0:NT], ks)
                    done += n
                return pieces

            def prompt_head(i, hh, pieces):
                e = i * 2 + hh
                w = wuk[:, hh]
                pe.wait_ge(E(f"wuk_in{hh}"), i * 16 + 16)
                for kc in range(4):
                    last = transpose(ps[:, 2, kc * P:kc * P + P], w[:, kc, 0:P])
                last.then_inc(E("wk_ps"), 1)
                pieces(1)
                pe.wait_ge(E("wk_done"), e + 1)
                pe.wait_ge(E("ol_done"), OPEN + e)
                for kc in range(4):
                    last = mm_(ps[:, 3 + kc, 0:NT], wkt[:, kc * P:kc * P + P],
                               qn[:, bass.ds(e, 1), :].squeeze(1), start=True, stop=True)
                last.then_inc(E("ql_ps"), 1)
                pieces(2)
                pe.wait_ge(E("ql_done"), e + 1)
                h = heads(hh)
                for t, (c0, n) in enumerate(((0, P), (P, 2 * P))):
                    for kc in range(4):
                        mm_(ps[:, 7, c0:c0 + n], qlp[:, kc, t * P:t * P + P], latt[:, kc, 0:n],
                            start=kc == 0, stop=False)
                    last = mm_(ps[:, 7, c0:c0 + n], qrs[h, t * P:t * P + P], kr2[h, 0:n], start=False, stop=True)
                last.then_inc(E("s_ps"), 1)
                pieces(4)
                pe.wait_ge(E("p_done"), e + 1)
                for j in range(3):
                    last = transpose(ps[:, 2, j * P:j * P + P], pp[:, j * P:j * P + P])
                last.then_inc(E("pt_ps"), 1)
                pieces(1)
                pe.wait_ge(E("pt_done"), e + 1)
                o = ps[:, 3:5, :].rearrange("p a (k t) -> p (a k) t", k=2)
                for kc in range(4):
                    mm_(o[:, kc, 0:P], ltok[:, 0, kc * P:kc * P + P], ptt[:, 0, :], start=True, stop=True)
                    mm_(o[:, kc, P:2 * P], ltok[:, 0, kc * P:kc * P + P], ptt[:, 1, :], start=True, stop=False)
                    last = mm_(o[:, kc, P:2 * P], ltok[:, 1, kc * P:kc * P + P], ptt[:, 2, :], start=False, stop=True)
                last.then_inc(E("ol_ps"), 1)
                pieces(2)
                pe.wait_ge(E("ol_done"), OPEN + e + 1)
                for kc in range(4):
                    last = mm_(ps[:, 5, 0:NP_], w[:, kc, P:2 * P], ol[:, kc, :], start=kc == 0, stop=kc == 3)
                last.then_inc(E("oh_ps"), 1)
                pieces(2)
                pe.wait_ge(E("oh_done"), e + 1)

            pe.wait_ge(E("latent_rows_done"), 1)
            pe.wait_ge(E("oa_split"), FT)
            with pe.Fori(0, 4) as i:
                pieces = side(i)
                for hh in range(2):
                    prompt_head(i, hh, pieces)

            with pe.Fori(0, 4) as i:
                pieces = side(i + 4)
                for bb in range(2):
                    b = i * 2 + bb
                    pe.wait_ge(E(f"past_in{bb}"), i * 48 + 48)
                    for kc in range(4):
                        transpose(ps[:, 2, kc * P:kc * P + P], lp[:, bb, kc * P:kc * P + P])
                    transpose(ps[:, 3, 0:P], kpast[:, bb].rearrange("p r c -> p (r c)")).then_inc(E("lpt_ps"), 1)
                    pieces(3)
                    pe.wait_ge(E("lpt_done"), b + 1)
                    for kc in range(5):
                        k_ = lpt[:, kc, :] if kc < 4 else kpt[:, :]
                        mm_(ps[:, 4, 0:P], qb[:, kc, :], k_, start=kc == 0, stop=kc == 4)
                    for kc in range(5):
                        k_ = (latt[:, kc, :] if kc < 4 else kr2[:, :])[:, bass.ds(b * TS + NP_, TS)]
                        last = mm_(ps[:, 4, P:P + TS], qb[:, kc, :], k_, start=kc == 0, stop=kc == 4)
                    last.then_inc(E("sd_scores_ps"), 1)
                    pieces(4)
                    pe.wait_ge(E("pd_done"), b + 1)
                    transpose(ps[:, 5, 0:P], pd[:, 0:P])
                    transpose(ps[0:TS, 5, P:2 * P], pd[:, P:P + TS]).then_inc(E("pdt_ps"), 1)
                    pieces(2)
                    pe.wait_ge(E("pdt_done"), b + 1)
                    for kc in range(4):
                        mm_(ps[:, 6, kc * P:kc * P + P], lp[:, bb, kc * P:kc * P + P], pdt[:, :], start=True, stop=False)
                        last = mm_(ps[:, 6, kc * P:kc * P + P], lnew[0:TS, bb, kc * P:kc * P + P], pdn[0:TS, :],
                                   start=False, stop=True)
                    last.then_inc(E("old_ps"), 1)
                    pieces(3)
                    pe.wait_ge(E("old_done"), b + 1)
            with pe.Fori(0, 4) as i:
                for hh in range(2):
                    e = i * 2 + hh
                    pe.wait_ge(E(f"wuk_in{hh}"), i * 16 + 80)
                    pe.wait_ge(E("ohd_done"), OPEN + e)
                    for kc in range(4):
                        last = mm_(ps[:, 7, 0:P], wuk[:, hh, kc, P:2 * P],
                                   qld[:, kc, bass.ds(e, 1), :].squeeze(1), start=kc == 0, stop=kc == 3)
                    last.then_inc(E("ohd_ps"), 1)

            pe.wait_ge(E("a_gated0"), OPEN + KD // 2)
            pe.wait_ge(E("a_gated1"), OPEN + KD // 2)
            with pe.Fori(0, KD // 2) as i:
                for q in range(2):
                    pe.wait_ge(proj_taken, i * 2 + (T_MIX + KD + q - 1))
                    for s in range(2):
                        pe_block(i * 3 + (T_MIX_B + q), s, ps[:, q, 0:NT])
                pe.wait_ge(E("ob_split"), FT)
                for s in range(2):
                    pe.wait_ge(E("b_taken"), OPEN + i * 2)
                    pe_half(i * 3 + (T_MIX_B + 2), s, obh, obl, ps[:, 2 + s, 0:NT])

            def wide(t0, ch_no, kts, lh, ll):
                pe.wait_ge(E("acc_taken"), OPEN + ch_no)
                for kt in range(kts):
                    s = kt % 2
                    pe.wait_ge(lo_done, t0 * 2 + (kt + 1))
                    wh, wlo = (x[:, s].rearrange("p k c -> p (k c)") for x in (hi, lo))
                    for t in range(3):
                        l_h, l_l = lh[:, kt, t * P:t * P + P], ll[:, kt, t * P:t * P + P]
                        for n, (l_, w_) in enumerate(((l_h, wh), (l_h, wlo), (l_l, wh))):
                            for cb in range(2):
                                last = mm_(ps[:, 2 + 2 * t + cb, :], l_, w_[:, 512 * cb:512 * cb + 512],
                                           start=kt == 0 and n == 0, stop=kt == kts - 1 and n == 2)
                    last.then_inc(blk_used, 1)

            pe.wait_ge(E("mix_done"), KD)
            with pe.Fori(0, 2) as ch:
                wide(ch * 8 + T_OUT, ch, 16, mh, ml)
            pe.wait_ge(E("acc_taken"), OPEN + 2)
            pe_norm(hn, 1, E("h_scaled"), E("xt_lo"))
            pe.wait_ge(E("xt_lo"), 2 * KD)
            for hf in range(2):
                with pe.Fori(0, HJ) as j:
                    for q in range(2):
                        t = j * 2 + (hf * T_HALF + T_FFN + q)
                        pe.wait_ge(E(("gate_taken", "up_taken")[q]), OPEN + j + hf * HJ)
                        for s in range(2):
                            pe_block(t, s, ps[:, q, 0:NT])
                pe.wait_ge(E("act_done"), hf * HJ + HJ)
                with pe.Fori(0, 2) as ch:
                    wide(ch * 11 + (hf * T_HALF + T_FFN + 2 * HJ), ch + (hf * 2 + 2), HJ, ach, acl)
            pe.wait_ge(E("acc_taken"), OPEN + 6)
            for q in range(9):
                last = transpose(ps[0:88, 2 + q // 4, (q % 4) * P:(q % 4 + 1) * P],
                                 ctail[:, q].rearrange("p r j -> p (r j)"))
            for g in range(3):
                last = transpose(ps[0:72, 5, g * P:g * P + P], tail[:, 3 * g:3 * g + 3, :].rearrange("p q t -> p (q t)"))
            last = transpose(ps[0:36, 6, 0:P], taill[:, :, :].rearrange("p l q -> p (l q)"))
            last.then_inc(E("tails_ps"), 1)

        @block.scalar
        def _(act):
            fn = nc.scalar.activation
            ch = Chain(nc.scalar, E("act_chain"))
            act_norm_stats(xt, junk[:, :], lambda t: act.wait_ge(E(f"x_in{t}"), 16), ch)
            act.wait_ge(E("params_ps"), 1)
            for i, (r, dst) in enumerate(PARAM_ROWS):
                last = fn(dst, ps[:, 2 + i // 4, (i % 4) * P:(i % 4) * P + r].rearrange(
                    "p (a c) -> p a c", a=dst.shape[1]) if len(dst.shape) == 3 else
                    ps[:, 2 + i // 4, (i % 4) * P:(i % 4) * P + r], ACT.Copy)
            last.then_inc(E("params_done"), 1)
            act.wait_ge(E("params_done"), 1)
            act_norm(0, 80)
            act_hi(0, 0)

            def taken(t, p, dst, sem_=proj_taken):
                act.wait_ge(blk_used, t * 2 + 2)
                fn(dst, ps[:, p % 2, 0:NT], ACT.Copy).then_inc(sem_, 1)

            def taken_pad(t, p, i):
                act.wait_ge(blk_used, t * 2 + 2)
                fn(pb[:, i, 1:257], ps[:, p % 2, 0:NP_], ACT.Copy)
                fn(seq17(pb[:, i, 257:PAD])[:, :, 1:17], seq16(ps[:, p % 2, NP_:NT]), ACT.Copy)\
                    .then_inc(proj_taken, 1)

            for t in range(4):
                act_next(t)
                if t >= 2:
                    act.wait_ge(E("z_lora_done"), t - 1)
                taken_pad(t, t, t % 2)
                if t == 2:
                    act.wait_ge(E("z_lora_done"), 1)
                    fn(za[0:96, 0, :], za[0:96, 0, :], ACT.Tanh)
            act.wait_ge(E("z_lora_done"), 4)
            ch.link(fn(za[:, 2:4, :], za[:, 2:4, :], ACT.Sigmoid))
            for q in range(4):
                act_next(T_FT + q)
                if q < 3:
                    taken_pad(T_FT + q, q, q)

            def act_cut(f):
                def cut(k):
                    q, s = divmod(k, 2)
                    t = f * 4 + (T_FT + 4 + q)
                    if s == 0:
                        if q == 0:
                            taken(t - 1, 1, qn[:, bass.ds(f, 1), :].squeeze(1))
                        else:
                            if q == 1:
                                act.wait_ge(E("z_done"), f + 1)
                            taken_pad(t - 1, q - 1, q - 1)
                    if s == 0:
                        act_hi(t, 1, t * 16 + 16)
                    else:
                        act_hi(t + 1, 0, t * 16 + 32)
                return cut
            act.wait_ge(E("zeroed"), 1)
            with ch.loop(FT - 1, LINKS["act_rwkv"]) as f:
                act_rwkv(f, act_cut(f), ch)

            def last_cut(k):
                q, s = divmod(k, 2)
                t = T_MLA + q
                if k == 0:
                    taken(t - 1, 1, qn[:, FT - 1, :])
                elif s == 0:
                    if q == 1:
                        act.wait_ge(E("z_done"), FT)
                    taken(t - 1, t - 1, cc[:, q - 1])
                act_hi(t + s, 1 - s)
            act_rwkv(FT - 1, last_cut, ch)

            act.wait_ge(E("y_out_done"), OPEN + FT)
            act.wait_ge(E("states_stored"), OPEN + FT)
            taken(T_MLA + 3, T_MLA + 3, cc[:, 3])
            act.wait_ge(proj_taken, T_MLA + 4)
            fn(csq[:, :, :], cc[:, :, :], ACT.Square).then_inc(E("c_sq_done"), 1)
            for j in range(4, 9):
                t = T_MLA + j
                act_next(t)
                for k in range((j - 4) * 2, (j - 3) * 2 if j < 8 else 8):
                    fn(oah[:, k, :], oa[:, k, :], ACT.Copy).then_inc(E("oah_done"), 1)
                taken(t, t, qrp[:, j - 4] if j < 8 else kr2[:, :])
            act.wait_ge(E("oa_split"), FT)
            act.wait_ge(E("c_sum_ps"), 1)
            ch.link(fn(crs[:, :], ps[:, 7, 0:NT], ACT.Ln, scale=1.0 / LAT, bias=epsb))
            fn(crs[:, :], crs[:, :], ACT.Exp, scale=-0.5).then_inc(E("c_rstd_done"), 1)
            act.wait_ge(E("latent_rows_ps"), 1)
            fn(ltok[:, :, :], ps[:, 2:5, :], ACT.Copy)
            fn(krt[:, :, :], ps[:, 5, 0:NT].rearrange("p (t c) -> p t c", t=3)[:, :, 0:64], ACT.Copy)\
                .then_inc(E("latent_rows_done"), 1)

            def side_cut(pair_no, k):
                b, s = divmod(k, 2)
                t = pair_no * 3 + (T_MIX + b)
                if s == 0:
                    act_hi(t, 1, t * 16 + 96)
                else:
                    act_hi(t + 1, 0, t * 16 + 112)

            def side_gate(pair_no, q, j):
                t = pair_no * 3 + (T_MIX + q)
                act.wait_ge(blk_used, t * 2 + 2)
                fn(ga[:, bass.ds(j, 1), :].squeeze(1), ps[:, q, 0:NT], ACT.Sigmoid).then_inc(proj_taken, 1)

            with ch.loop(4, 0) as i:
                for hh in range(2):
                    e = i * 2 + hh
                    act.wait_ge(E("wk_ps"), e + 1)
                    fn(wkt[:, :], ps[:, 2, :], ACT.Copy).then_inc(E("wk_done"), 1)
                    side_cut(i, 3 * hh)
                    if hh == 0:
                        act.wait_ge(E("s_ps"), OPEN + e)
                        fn(qrs[:, :], qrp[:, bass.ds(i, 1), 0:NP_].squeeze(1), ACT.Copy)
                    act.wait_ge(E("ql_ps"), e + 1)
                    act.wait_ge(E("qlp_done"), e + 1)
                    fn(qld[:, :, bass.ds(e, 1), :].squeeze(2), ps[:, 3:7, NP_:NT], ACT.Copy).then_inc(E("ql_done"), 1)
                    act.wait_ge(E("mx_done"), e + 1)
                    for t, (c0, n) in enumerate(((0, P), (P, 2 * P))):
                        last = fn(pp[:, c0:c0 + n], pp[:, c0:c0 + n], ACT.Exp, bias=msum[:, 2 + t:3 + t],
                                  accum_out=msum[:, 4 + t:5 + t])
                    last.then_inc(E("ex_done"), 1)
                    side_cut(i, 3 * hh + 1)
                    if hh == 1:
                        side_gate(i, 1, i * 2 + (KD // 2 + 1))
                    act.wait_ge(E("pt_ps"), e + 1)
                    fn(ptt[:, :, :], ps[:, 2, 0:NT].rearrange("p (j c) -> p j c", j=3), ACT.Copy)\
                        .then_inc(E("pt_done"), 1)
                    side_cut(i, 3 * hh + 2)
                    if hh == 0:
                        side_gate(i, 0, i * 2 + KD // 2)
                    act.wait_ge(E("oh_ps"), e + 1)
                    fn(ob[:, bass.ds(e, 1), 0:NP_].squeeze(1), ps[:, 5, 0:NP_], ACT.Copy).then_inc(E("oh_done"), 1)
            with ch.loop(4, 0) as i:
                for bb in range(2):
                    b = i * 2 + bb
                    act.wait_ge(E("lpt_ps"), b + 1)
                    fn(lpt[:, :, :].rearrange("p k c -> p (k c)"), ps[:, 2, :], ACT.Copy)
                    act.wait_ge(E("kpt_done"), b + 1)
                    fn(qb[:, 0:4, :].rearrange("p k (h t) -> p (k h) t", h=8),
                       qld[:, :, :, bass.ds(b * TS, TS)].rearrange("p k h t -> p (k h) t"), ACT.Copy)\
                        .then_inc(E("lpt_done"), 1)
                    side_cut(i + 4, 3 * bb)
                    act.wait_ge(E("mxd_done"), b + 1)
                    fn(pd[:, :], ps[:, 4, 0:P + TS], ACT.Exp, scale=SCALE, bias=dsum[:, 1:2], accum_out=dsum[:, 2:3])\
                        .then_inc(E("exd_done"), 1)
                    side_cut(i + 4, 3 * bb + 1)
                    if bb == 1:
                        side_gate(i + 4, 1, i * 2 + 1)
                    act.wait_ge(E("pdt_ps"), b + 1)
                    fn(pdt[:, :], ps[:, 5, 0:P], ACT.Copy)
                    fn(pdn[0:TS, :], ps[0:TS, 5, P:2 * P], ACT.Copy).then_inc(E("pdt_done"), 1)
                    side_cut(i + 4, 3 * bb + 2)
                    if bb == 0:
                        side_gate(i + 4, 0, i * 2)
            with ch.loop(4, 0) as i:
                for hh in range(2):
                    e = i * 2 + hh
                    act.wait_ge(E("ohd_ps"), e + 1)
                    fn(ob[:, bass.ds(e, 1), NP_:NT].squeeze(1), ps[:, 7, 0:P], ACT.Copy).then_inc(E("ohd_done"), 1)
            act_hi(T_MIX_B, 1)
            act.wait_ge(E("old_done"), NB)
            act.wait_ge(E("ohd_done"), OPEN + FT)
            for k in range(FT):
                fn(obh[:, k, :], ob[:, k, :], ACT.Copy).then_inc(E("obh_done"), 1)

            def mix_pair(i, last):
                t = i * 3 + T_MIX_B
                count = lambda blk: t * 16 + (96 + 16 * (blk // 2))
                for q in range(2):
                    for blk in (2 * q + 2, 2 * q + 3):
                        act_hi(t + blk // 2, blk % 2, count(blk))
                    act.wait_ge(blk_used, t * 2 + (2 * q + 2))
                    act.wait_ge(E("b_taken"), OPEN + i * 2)
                    fn(gab[:, q, :], ps[:, q, 0:NT], ACT.Sigmoid).then_inc(proj_taken, 1)
                for q in range(2):
                    if not (last and q == 1):
                        act_hi(t + 3, q, count(6))
                    act.wait_ge(E("mixed"), i * 2 + (q + 1))
                    dst = mh[:, i * 2 + q, :] if last else mh[:, bass.ds(i * 2 + q, 1), :].squeeze(1)
                    fn(dst, mm[:, q, :], ACT.Copy).then_inc(E("mix_hi"), 1)

            with ch.loop(KD // 2 - 1, 0) as i:
                mix_pair(i, False)
            mix_pair(KD // 2 - 1, True)
            with ch.loop(2, 0) as c:
                with ch.loop(8, 0) as i:
                    act_next(c * 8 + i + T_OUT)
            act_norm_stats(ht, jk2[:, :], lambda t: act.wait_ge(E("acc_taken"), OPEN + 2), ch)
            act_norm(1, 96)
            for hf in range(2):
                with ch.loop(HJ, 0) as j:
                    for q in range(2):
                        t = j * 2 + (hf * T_HALF + T_FFN + q)
                        act_next(t)
                        if q == 0:
                            act.wait_ge(blk_used, t * 2 + 2)
                            act.wait_ge(E("conv_done"), OPEN + j + hf * HJ)
                            fn(gp[:, 2:2 + NP_], ps[:, 0, 0:NP_], ACT.Copy)
                            fn(seq18(gp[:, 2 + NP_:])[:, :, 2:18], seq16(ps[:, 0, NP_:NT]), ACT.Copy)\
                                .then_inc(E("gate_taken"), 1)
                    act.wait_ge(E("conv_done"), OPEN + j + (hf * HJ + 1))
                    act.wait_ge(E("up_taken"), OPEN + j + hf * HJ)
                    fn(sg[:, 0:400], cv[:, 0:400], ACT.Silu).then_inc(E("silu_done"), 1)
                    act.wait_ge(E("up_taken"), OPEN + j + (hf * HJ + 1))
                    fn(ach[:, bass.ds(j, 1), :].squeeze(1), af[:, :], ACT.Copy).then_inc(E("act_hi"), 1)
                for c in range(2):
                    t0 = hf * T_HALF + c * 11 + T_FFN + 2 * HJ
                    end = hf == 1 and c == 1
                    with ch.loop(10 if end else 11, 0) as i:
                        act_next(i + t0)
                    if end:
                        act_next(t0 + 10, end=True)
            act_norm_stats(ht, jk2[:, :], lambda t: act.wait_ge(E("acc_taken"), OPEN + 6), ch)
            act.wait_ge(E("tails_ps"), 1)
            fn(ctr[:, 0:8, :].rearrange("p (a q) c -> p a (q c)", a=2), ps[0:88, 2:4, :], ACT.Copy)
            fn(ctr[:, 8, :], ps[0:88, 4, 0:P], ACT.Copy).then_inc(E("tails_done"), 1)

        @block.vector
        def _(dve):
            tt, stt3, cp, ts = (nc.vector.tensor_tensor, nc.vector.scalar_tensor_tensor, nc.vector.tensor_copy,
                                nc.vector.tensor_scalar)
            M, A, S = ALU.mult, ALU.add, ALU.subtract
            ch = Chain(nc.vector, E("dve_chain"))
            dve.wait_ge(E("rstd_done"), 1)
            for t in range(3):
                ts(xt[:, t, :], xt[:, t, :], stat[:, t:t + 1], None, M).then_inc(E("x_scaled"), 1)
            dve.wait_ge(E("params_done"), 1)
            dve_norm(0, 80)
            dve_lo(0, 0)
            dve.wait_ge(E("norm_ps"), KD)
            nc.vector.memset(pb[:, :, 0:1], 0.0)
            nc.vector.memset(rr[:, :, :], 0.0)
            nc.vector.memset(un[:, :, :], 0.0)
            nc.vector.memset(al[:, :, :], 0.0)
            nc.vector.memset(db[:, :, PAD - 1:PAD], 0.0)
            nc.vector.memset(rh[:, :, :], 0.0).then_inc(E("zeroed"), 1)
            dve.wait_ge(E("zeroed"), 1)
            for t in range(4):
                dve_next(t)
                i = t % 2
                ch.link(cp(pb[:, i, 257:PAD:17], shl[:, t, :]))
                dve.wait_ge(proj_taken, t + 1)
                ch.link(tt(db[:, i, 0:PAD - 1], pb[:, i, 0:PAD - 1], pb[:, i, 1:PAD], S))
                mu = prm[:, 112 + t:113 + t]
                stt3(za[:, t, 0:NP_], db[:, i, 0:NP_], mu, pb[:, i, 1:257], M, A)
                stt3(seq16(za[:, t, NP_:NT]), seq17(db[:, i, 257:PAD])[:, :, 0:TS], mu,
                     seq17(pb[:, i, 257:PAD])[:, :, 1:17], M, A)
                cp(taill[:, t, 0:1], pb[:, i, 256:257])
                cp(taill[:, t, 1:9], pb[:, i, 273:PAD:17]).then_inc(E("z_lora_done"), 1)
                dve.wait_ge(E("z_lora_done"), t + 1)
            for q in range(4):
                dve_next(T_FT + q)

            def dve_cut(f):
                def cut(k):
                    q, s = divmod(k, 2)
                    t = f * 4 + (T_FT + 4 + q)
                    dve_lo(t, 1) if s == 0 else dve_lo(t + 1, 0)
                return cut
            dve.wait_ge(E("c2_in"), 16)
            with ch.loop(FT - 1, LINKS["dve_rwkv"]) as f:
                dve_rwkv(f, dve_cut(f), ch)
            dve_rwkv(FT - 1, dve_cut(FT - 1), ch)

            for j in range(4, 9):
                dve_next(T_MLA + j)
                for k in range((j - 4) * 2, (j - 3) * 2 if j < 8 else 8):
                    dve.wait_ge(E("oah_done"), k + 1)
                    tt(oal[:, k, :], oa[:, k, :], oah[:, k, :].bitcast(F32), S).then_inc(E("oa_split"), 1)
            dve.wait_ge(E("rot_ps"), 1)
            dve.wait_ge(E("c3_in"), 16)
            for j in range(5):
                x = kr2[:, :] if j == 4 else qrp[:, j]
                tt(rtmp[:, j, :], ps[:, 2 + j, 0:NT], sin, M)
                ch.link(tt(x, x, cos, M))
                last = tt(x, x, rtmp[:, j, :], A)
            last.then_inc(E("rope_done"), 1)
            dve.wait_ge(E("c_rstd_done"), 1)
            for j in range(4):
                last = stt3(latt[:, j, :], cc[:, j, :], prm[:, 116 + j:117 + j], crs[:, :], M, M)
            last.then_inc(E("latent_done"), 1)

            def side_lo(pair_no, k):
                b, s = divmod(k, 2)
                t = pair_no * 3 + (T_MIX + b)
                dve_lo(t, 1) if s == 0 else dve_lo(t + 1, 0)

            def side_product(pair_no, q, j):
                dve.wait_ge(blk_used, pair_no * 6 + (2 * T_MIX + 4 + q + 1))
                g = ga[:, bass.ds(j, 1), :].squeeze(1)
                tt(g, ps[:, q, 0:NT], g, M).then_inc(E(f"a_gated{q}"), 1)

            with ch.loop(4, LINKS["dve_head"]) as i:
                for hh in range(2):
                    e = i * 2 + hh
                    dve.wait_ge(E("ql_ps"), e + 1)
                    cp(qlp[:, :, :], ps[:, 3:7, 0:NP_]).then_inc(E("qlp_done"), 1)
                    side_lo(i, 3 * hh)
                    dve.wait_ge(E("s_ps"), OPEN + e + 1)
                    ch.link(stt3(pp[:, :], ps[:, 7, 0:NT], SCALE, amask, M, A))
                    nc.vector.reduce_max(msum[:, 0:1], pp[:, 0:P], AX)
                    ch.link(nc.vector.reduce_max(msum[:, 1:2], pp[:, P:NT], AX))
                    ts(msum[:, 2:4], msum[:, 0:2], -1.0, None, M).then_inc(E("mx_done"), 1)
                    dve.wait_ge(E("ex_done"), e + 1)
                    ch.link(nc.vector.reciprocal(msum[:, 6:8], msum[:, 4:6]))
                    ts(pp[:, 0:P], pp[:, 0:P], msum[:, 6:7], None, M)
                    ts(pp[:, P:NT], pp[:, P:NT], msum[:, 7:8], None, M).then_inc(E("p_done"), 1)
                    side_lo(i, 3 * hh + 1)
                    dve.wait_ge(E("ol_ps"), e + 1)
                    cp(ol[:, :, :].rearrange("p (a k) t -> p a (k t)", a=2), ps[:, 3:5, :]).then_inc(E("ol_done"), 1)
                    if hh == 1:
                        side_product(i, 0, i * 2 + KD // 2)
                    side_lo(i, 3 * hh + 2)
                side_product(i, 1, i * 2 + (KD // 2 + 1))
            dve.wait_ge(E("oh_ps"), FT)
            ch.link(nc.vector.memset(qb[:, 4, :], 0.0))
            with ch.loop(4, LINKS["dve_seq"]) as i:
                for bb in range(2):
                    b = i * 2 + bb
                    dve.wait_ge(E("lpt_ps"), b + 1)
                    cp(kpt[:, :], ps[:, 3, 0:P])
                    for hh in range(2):
                        last = cp(qb[heads(hh), 4, :].rearrange("p (h t) -> p h t", h=8)[:, hh:8:2, :],
                                  qrp[heads(hh), :, bass.ds(b * TS + NP_, TS)])
                    last.then_inc(E("kpt_done"), 1)
                    side_lo(i + 4, 3 * bb)
                    dve.wait_ge(E("sd_scores_ps"), b + 1)
                    ch.link(nc.vector.reduce_max(dsum[:, 0:1], ps[:, 4, 0:P + TS], AX))
                    ts(dsum[:, 1:2], dsum[:, 0:1], -SCALE, None, M).then_inc(E("mxd_done"), 1)
                    dve.wait_ge(E("exd_done"), b + 1)
                    ch.link(nc.vector.reciprocal(dsum[:, 3:4], dsum[:, 2:3]))
                    ts(pd[:, :], pd[:, :], dsum[:, 3:4], None, M).then_inc(E("pd_done"), 1)
                    side_lo(i + 4, 3 * bb + 1)
                    dve.wait_ge(E("old_ps"), b + 1)
                    cp(qld[:, :, :, bass.ds(b * TS, TS)].rearrange("p k h t -> p (k h) t"),
                       ps[:, 6, :].rearrange("p (k t) -> p k t", t=TS)).then_inc(E("old_done"), 1)
                    if bb == 1:
                        side_product(i + 4, 0, i * 2)
                    side_lo(i + 4, 3 * bb + 2)
                side_product(i + 4, 1, i * 2 + 1)
            dve_lo(T_MIX_B, 1)
            for k in range(FT):
                dve.wait_ge(E("obh_done"), k + 1)
                tt(obl[:, k, :], ob[:, k, :], obh[:, k, :].bitcast(F32), S).then_inc(E("ob_split"), 1)

            def mix_pair(i, last):
                t = i * 3 + T_MIX_B
                tile_of = lambda x, j: x[:, j, :] if last else x[:, bass.ds(j, 1), :].squeeze(1)
                for blk in range(2, 6):
                    dve_lo(t + blk // 2, blk % 2)
                for q in range(2):
                    if not (last and q == 1):
                        dve_lo(t + 3, q)
                    j = i * 2 + q
                    dve.wait_ge(proj_taken, j + (T_MIX + KD + 1))
                    dve.wait_ge(blk_used, t * 2 + (5 + q))
                    tt(mm[:, q, :], ps[:, 2 + q, 0:NT], gab[:, q, :], M).then_inc(E("b_taken"), 1)
                    dve.wait_ge(E("b_taken"), OPEN + j + 1)
                    tt(mm[:, q, :], mm[:, q, :], tile_of(ga, j), A).then_inc(E("mixed"), 1)
                    dve.wait_ge(E("mix_hi"), j + 1)
                    tt(tile_of(ml, j), mm[:, q, :], tile_of(mh, j).bitcast(F32), S).then_inc(E("mix_done"), 1)

            with ch.loop(KD // 2 - 1, 0) as i:
                mix_pair(i, False)
            mix_pair(KD // 2 - 1, True)

            def add_acc(c, need, done):
                dve.wait_ge(E("acc_taken"), OPEN + done)
                dve.wait_ge(blk_used, need)
                for t in range(3):
                    for cb in range(2):
                        dst = ht[:, t, bass.ds(c * 1024 + 512 * cb, 512)]
                        last = tt(dst, dst, ps[:, 2 + 2 * t + cb, :], A)
                last.then_inc(E("acc_taken"), 1)
            dve.wait_ge(E("h_in"), 48)
            with ch.loop(2, 0) as c:
                with ch.loop(8, 0) as i:
                    dve_next(c * 8 + i + T_OUT)
                add_acc(c, c * 16 + (2 * T_OUT + 16), c)
            dve.wait_ge(E("acc_taken"), OPEN + 2)
            dve.wait_ge(E("rstd_done"), 2)
            for t in range(3):
                ts(hn[:, t, :], ht[:, t, :], stat[:, t:t + 1], None, M).then_inc(E("h_scaled"), 1)
            dve_norm(1, 96)
            dve.wait_ge(E("xt_lo"), 2 * KD)
            ch.link(nc.vector.memset(gp[:, 0:2], 0.0))
            for hf in range(2):
                with ch.loop(HJ, LINKS["dve_ffn"]) as j:
                    t = j * 2 + (hf * T_HALF + T_FFN)
                    n = j + hf * HJ
                    prev = cprev[:, :, :, bass.ds(n, 1)].squeeze(3)
                    ch.link(cp(seq18(gp[:, 2 + NP_:])[:, :, 0:2], prev))
                    dve_next(t)
                    dve.wait_ge(E("gate_taken"), OPEN + n + 1)
                    tap = lambda q: cprm[:, q, bass.ds(n, 1)]
                    dve.wait_ge(E("silu_done"), OPEN + n)
                    ch.link(ts(cv[:, 0:400], gp[:, 2:402], tap(2), tap(3), M, A))
                    ch.link(stt3(cv[:, 0:400], gp[:, 1:401], tap(1), cv[:, 0:400], M, A))
                    cp(ctail[:, 0, :, bass.ds(n, 1)].squeeze(2), gp[:, NP_:NP_ + 2])
                    cp(ctail[:, 1:9, :, bass.ds(n, 1)].squeeze(3), seq18(gp[:, 2 + NP_:])[:, :, 16:18])
                    stt3(cv[:, 0:400], gp[:, 0:400], tap(0), cv[:, 0:400], M, A).then_inc(E("conv_done"), 1)
                    dve_next(t + 1)
                    dve.wait_ge(E("silu_done"), OPEN + n + 1)
                    dve.wait_ge(blk_used, t * 2 + 4)
                    dve.wait_ge(E("act_hi"), OPEN + n)
                    tt(af[:, 0:NP_], sg[:, 0:NP_], ps[:, 1, 0:NP_], M)
                    tt(seq16(af[:, NP_:NT]), seq18(sg[:, 2 + NP_:])[:, :, 0:TS], seq16(ps[:, 1, NP_:NT]), M).then_inc(E("up_taken"), 1)
                    dve.wait_ge(E("act_hi"), OPEN + n + 1)
                    dve.wait_ge(E("up_taken"), OPEN + n + 1)
                    tt(acl[:, bass.ds(j, 1), :].squeeze(1), af[:, :],
                       ach[:, bass.ds(j, 1), :].squeeze(1).bitcast(F32), S).then_inc(E("act_done"), 1)
                for c in range(2):
                    t0 = hf * T_HALF + c * 11 + T_FFN + 2 * HJ
                    end = hf == 1 and c == 1
                    with ch.loop(10 if end else 11, 0) as i:
                        dve_next(i + t0)
                    if end:
                        dve_next(t0 + 10, end=True)
                    add_acc(c, (t0 + 11) * 2, 2 * hf + c + 2)
            dve.wait_ge(E("acc_taken"), OPEN + 6)
            dve.wait_ge(E("rstd_done"), 3)
            dve.wait_ge(E("gf_in"), 16)
            for t in range(3):
                stt3(hn[:, t, :], ht[:, t, :], stat[:, t:t + 1], gf[:, :], M, M).then_inc(E("y_ready"), 1)
            dve.wait_ge(E("tails_ps"), 1)
            cp(rowt[0:72, 0:3, :].rearrange("p g c -> p (g c)"), ps[0:72, 5, 0:NT])
            cp(rowt[0:36, 3, :], ps[0:36, 6, 0:P]).then_inc(E("rkv_tails_done"), 1)


LINKS = {"act_rwkv": 3, "dve_rwkv": 20, "dve_head": 6, "dve_seq": 4, "dve_ffn": 3}

_INS = ["x_prompt", "x_sample", "cache_mla_latent", "cache_mla_krope", "state_rwkv_wkv", "state_rwkv_shift",
        "state_ffn_conv", "g_mix", "w_in", "mu_shift", "w0", "w2", "a0", "a2", "g2", "k_k", "k_a", "r_k", "lnx_g",
        "lnx_b", "w_o_a", "g_kv", "w_ukv", "w_o_b", "w_out", "g_ffn", "w_ffn_in", "conv_w", "conv_b", "w_ffn_down",
        "g_final"]
_OUTS = [(1, 256, D), (8, 16, D), (1, 1, 256, LAT), (1, 1, 256, 64), (1, 1, 16, 64, 64), (1, 1, 1, RW),
         (1, 1, 2, DFF), (1, 8, 16, LAT), (1, 8, 16, 64), (1, 8, 16, 64, 64), (1, 8, 1, RW), (1, 8, 2, DFF)]


def kernel(**inputs):
    import numpy as _np
    import concourse.bacc as _bacc
    from concourse.bass_utils import run_bass_kernel_spmd as _run

    nc = _bacc.Bacc("TRN2", target_bir_lowering=False, num_devices=1)
    arrays, aps = {}, {}
    for name in _INS:
        x = _np.ascontiguousarray(inputs[name])
        arrays[f"in_{name}"] = x
        aps[name] = nc.dram_tensor(f"in_{name}", x.shape, mybir.dt.from_np(x.dtype), kind="ExternalInput").ap()
    arrays["shape_consts"] = constants()
    consts = nc.dram_tensor("shape_consts", arrays["shape_consts"].shape, F32, kind="ExternalInput").ap()
    outs = [nc.dram_tensor(f"out_{i}", s, F32, kind="ExternalOutput").ap() for i, s in enumerate(_OUTS)]
    build(nc, aps, consts, outs)
    r = _run(nc, [arrays], core_ids=[0])
    return tuple(r.results[0][f"out_{i}"] for i in range(len(_OUTS)))
```

```python
from contextlib import ExitStack, contextmanager

import concourse.bass as bass
from concourse import mybir

F32 = mybir.dt.float32
F32R = mybir.dt.float32r
ALU = mybir.AluOpType
ACT = mybir.ActivationFunctionType
AX = mybir.AxisListType.X

P = 128
D = 2048
NT = 384
NP_ = 256
NB, TS = 8, 16
KD = D // P
W = 1024
FT = W // P
RW = 3520
Q0 = RW
CKV0 = Q0 + 1536
KR0 = CKV0 + 512
G0 = RW + 2112
DFF = 5632
NJ = DFF // P
HJ = NJ // 2
PAST = 128
LAT = 512
SCALE = 192.0 ** -0.5
EPS = 1e-6
GN_EPS = 64e-5
CDEC = 0.6065306597126334
PAD = 257 + NB * 17

C1 = ["ident", "ones"]
C2 = ["bones", "st64", "in64", "st16", "in16", "nl1", "nl1t", "lv2", "lv4", "lv8", "lv16", "lv32"]
C3 = ["rot"]
NC1 = len(C1) * P
NC2 = len(C2) * P + NT + 8
NC3 = P + 3 * NT

T_LORA = 0
T_FT = 4
T_MLA = T_FT + 4 * FT
T_MIX = T_MLA + 9
T_MIX_B = T_MIX + 3 * KD // 2
T_OUT = T_MIX + 3 * KD
T_FFN = T_OUT + KD
T_HALF = 2 * HJ + HJ


def constants():
    import numpy as np
    f = np.float32
    s, t = np.arange(P)[:, None], np.arange(P)[None, :]
    m = {"ident": s == t, "ones": s >= 0 * t, "bones": s // 64 == t // 64}
    for c in (64, 16):
        same = s // c == t // c
        m[f"st{c}"], m[f"in{c}"] = same & (s < t), same & (s <= t)
    level = lambda n: (s // (2 * n) == t // (2 * n)) & (s % (2 * n) < n) & (t % (2 * n) >= n)
    m["nl1"] = -level(1).astype(f)
    m["nl1t"] = m["nl1"].T
    for n in (2, 4, 8, 16, 32):
        m[f"lv{n}"] = level(n)
    rot = np.zeros((P, P), f)
    for b in (0, 64):
        for j in range(32):
            rot[b + j + 32, b + j] = -1
            rot[b + j, b + j + 32] = 1
    m["rot"] = rot
    cat = lambda names: [np.broadcast_to(m[n], (P, P)).astype(f) for n in names]
    tok = np.arange(NT)
    first = np.where(tok < NP_, tok % 64 == 0, tok % 16 == 0)
    reset = np.broadcast_to(1 - first.astype(f), (P, NT))
    bm = (s // 16 == np.arange(8)[None]).astype(f)
    half = 32
    inv = (f(10000.0) ** (-np.arange(half, dtype=f) / f(half))).astype(f)
    pos = np.where(tok < NP_, tok, PAST + tok % 16).astype(f)
    ang = (pos[None, :] * inv[np.arange(P) % half][:, None]).astype(f)
    key = np.concatenate([np.arange(128), np.arange(256)])[None]
    q = np.where(np.arange(NT)[None] < 128, s, 128 + s)
    amask = np.where(key // 64 <= q // 64, 0, -1e30)
    out = cat(C1) + cat(C2) + [reset, bm] + cat(C3) + [np.cos(ang), np.sin(ang), amask]
    return np.ascontiguousarray(np.concatenate([np.asarray(a, f) for a in out], 1))


class Chain:

    def __init__(self, eng, sem):
        self.eng, self.sem, self.base, self.k = eng, sem, 0, 0

    def link(self, ins):
        ins.then_inc(self.sem, 1)
        self.k += 1
        self.eng.wait_ge(self.sem, self.base + self.k)

    @contextmanager
    def loop(self, count, steps):
        base, k = self.base, self.k
        with self.eng.Fori(0, count) as i:
            self.base, self.k = i * steps + (base + k), 0
            yield i
            assert self.k == steps, f"the body links {self.k} times"
        self.base, self.k = base, k + count * steps


def build(nc, a, consts, outs):
    (y_prompt, y_sample, lat_p, kr_p, wkv_p, shift_p, conv_p,
     lat_s, kr_s, wkv_s, shift_s, conv_s) = outs
    ctx = ExitStack()
    sems = {}

    def sem(name):
        if name not in sems:
            sems[name] = ctx.enter_context(nc.semaphore(name))
        return sems[name]

    BASE = 16512
    top = [BASE]

    def at(name, shape, off, dt=F32):
        size = 4
        for n in shape[1:]:
            size *= n
        assert off % 32 == 0 and off + size <= 229368, (name, off, size)
        return nc.alloc_sbuf_tensor_at(name, shape, dt, offset=off)

    def region(name, shape, dt=F32):
        off = top[0]
        size = 4
        for n in shape[1:]:
            size *= n
        top[0] = off + (size + 31) // 32 * 32
        return at(name, shape, off, dt)

    with ctx:
        raw = region("w_raw", [P, 2, 8, P])
        hi = region("w_hi", [P, 2, 8, P], F32R)
        lo = region("w_lo", [P, 2, 8, P], F32R)
        xh = region("x_hi", [P, KD, NT], F32R)
        xl = region("x_lo", [P, KD, NT], F32R)
        c1 = region("consts_all", [P, NC1])
        prm = region("params", [P, 120])
        cprm = region("conv_params", [P, 4, NJ])
        cprev = region("conv_prev", [P, NB, 2, NJ])
        shm = region("shift_rkv", [P, NB, 24])
        shl = region("shift_lora", [P, 4, NB])
        stat = region("row_stats", [P, 8])
        hsum = region("half_row_sums", [P, 6])
        tail = region("proj_last_rkv", [P, 9, 24])
        taill = region("proj_last_lora", [P, 4, 9])
        ctail = region("conv_last", [P, 9, 2, NJ])
        area = top[0]
        ident, ones = c1[:, 0:P], c1[:, P:2 * P]

        qn = region("q_nope", [P, FT, NT])
        oa = region("rwkv_out", [P, FT, NT])
        phase = top[0]
        pb = region("proj_pad", [P, 3, PAD])
        c2 = region("consts_rwkv", [P, NC2])
        cm = {n: c2[:, i * P:(i + 1) * P] for i, n in enumerate(C2)}
        reset = c2[:, len(C2) * P:len(C2) * P + NT]
        bmask = c2[:, len(C2) * P + NT:NC2]
        db_off = top[0]
        db = region("proj_diff", [P, 3, PAD])
        vx = at("v_by_sequence", [P, 2, NB, 64], db_off)
        z = region("z", [P, 3, NT])
        wl = region("lora_w2a2", [P, 2, P])
        wg = region("lora_g2", [P, 2, P])
        za = region("z_lora", [P, 4, NT])
        pf = region("params_ft", [P, 10])
        pfl = region("params_ft_norm", [P, 2])
        mid = region("decay_mid", [P, 4, 2])
        emid = region("decay_mid_exp", [P, 4, 2])
        sw, aa, gg, cu, dx, e1, e2, e3, kk0, sq, rn, t1, k2, kka, rk = [
            region(n, [P, NT]) for n in ("sig_w", "a_gate", "g_gate", "cum_decay", "cum_excl", "exp_inc", "exp_inv",
                                         "exp_excl", "kk_raw", "square", "norm", "k_scale", "k_mod", "kk_a",
                                         "bonus")]
        al = region("alpha_pad", [P, 2, NT])
        rh = region("rho_pad", [P, 2, NT])
        be = region("beta", [P, NT])
        kp_ = region("kappa", [P, NT])
        n_t, t_x, t_y, t_g, m_t, c_k, c_b = [
            region(n, [P, 6, P]) for n in ("n_t", "t_x", "t_y", "t_g", "m_t", "c_k", "c_b")]
        tok = region("tok_major", [P, 3, 3, P])
        rr = region("r_rhs", [P, 2, P])
        un = region("u_neg", [P, 2, P])
        asd = region("alpha_s0", [P, P])
        s0l = region("s0_load", [64, NB, P])
        s0t = region("s0_t", [P, NB, 64])
        so = region("s_out", [64, NB, P])
        st = region("state", [P, 3, 64])
        sto = region("state_rows", [64, P])
        assert top[0] <= 229368, top[0]
        yb, yc = cu, dx
        x_off = (229368 - 4 * 3 * D) // 32 * 32
        xt = at("x_rows", [P, 3, D], x_off)
        rows = at("param_rows", [P, 14, P], area)
        junk = at("square_junk", [P, D], area + 12288)

        top[0] = phase
        cc = region("c_kv", [P, 4, NT])
        lp = at("past_latent", [P, 2, LAT], phase)
        kpast = at("past_krope", [P, 2, 2, 64], phase + 4096)
        lnew = at("new_latent_rows", [16, 2, LAT], phase + 5120)
        top[0] = phase + 9216
        c3_off = top[0]
        c3 = region("consts_mla", [P, NC3])
        rot, cos, sin, amask = c3[:, 0:P], c3[:, P:P + NT], c3[:, P + NT:P + 2 * NT], c3[:, P + 2 * NT:NC3]
        wkt = at("w_uk_t", [P, LAT], c3_off + 512)
        qrs = at("q_rope_pair", [P, NP_], c3_off + 2560)
        oah_off = top[0]
        oah = region("rwkv_out_hi", [P, FT, NT], F32R)
        oal = region("rwkv_out_lo", [P, FT, NT], F32R)
        ob = region("mla_out", [P, FT, NT])
        after_ob = top[0]
        qrp = region("q_rope", [P, 4, NT])
        latt = region("latent_t", [P, 4, NT])
        kr2 = region("k_rope_t", [P, NT])
        ltok = region("latent_rows", [P, 3, LAT])
        wuk = region("w_ukv_head", [P, 2, 4, 256])
        msum = region("softmax_stats", [P, 8])
        krt = region("k_rope_rows", [P, 3, 64])
        qld_off = top[0]
        qld = region("q_latent_sample", [P, 4, 8, P])
        csq = at("c_square", [P, 4, NT], qld_off)
        rtmp = at("rope_tmp", [P, 5, NT], qld_off + 6144)
        crs = at("c_rstd", [P, NT], qld_off + 13824)
        heads_off = top[0]
        pp = region("probs", [P, NT])
        ptt = region("probs_t", [P, 3, P])
        ol = region("o_latent", [P, 4, NP_])
        qlp = at("q_latent", [P, 4, NP_], top[0] - 4096)
        assert top[0] <= 229368, top[0]
        top[0] = heads_off
        lpt = region("past_latent_t", [P, 4, P])
        kpt = region("past_krope_t", [P, P])
        qb = region("q_sequence", [P, 5, P])
        pd = region("probs_sample", [P, 144])
        pdt = region("probs_sample_t", [P, P])
        pdn = region("probs_new_t", [16, P])
        dsum = region("softmax_stats_sample", [P, 4])
        assert top[0] <= 229368, top[0]
        ga = at("branch_a_gated", [P, KD, NT], area)

        obh = at("mla_out_hi", [P, FT, NT], oah_off, F32R)
        obl = at("mla_out_lo", [P, FT, NT], oah_off + 12288, F32R)
        mh = at("mix_hi", [P, KD, NT], area, F32R)
        top[0] = after_ob
        ml = region("mix_lo", [P, KD, NT], F32R)
        gab = region("gates", [P, 2, NT])
        mm = region("mixed", [P, 2, NT])
        assert top[0] <= 229368
        ht = at("h_rows", [P, 3, D], phase)
        hn = at("h_normed", [P, 3, D], phase + 24576)
        ach = at("act_hi", [P, HJ, NT], phase + 24576, F32R)
        acl = at("act_lo", [P, HJ, NT], phase + 24576 + 33792, F32R)
        gp = at("gate_pad", [P, 2 + NP_ + NB * 18], area)
        cv = at("conv", [P, 402], area + 2048)
        sg = at("silu", [P, 402], area + 4096)
        rowt = at("proj_rows", [72, 4, P], area + 20992)
        af = at("act", [P, NT], area + 6144)
        ctr = at("conv_rows", [88, 9, P], area + 8192)
        gf = at("g_final_all", [P, D], area)
        jk2 = at("square_junk2", [P, 1024], area + 12800)

        ps = ctx.enter_context(nc.psum_tensor("banks", [P, 8, 512], F32))
        pair = lambda b: ps[:, b:b + 2, :].rearrange("p a n -> p (a n)")[:, 0:6 * P]
        unit = lambda b, u: ps[:, b + u // 4, (u % 4) * P:(u % 4 + 1) * P]
        PARAM_ROWS = [(120, prm[:, :]), (88, cprm[:, 0:2, :]), (88, cprm[:, 2:4, :])]
        PARAM_ROWS += [(88, cprev[:, b]) for b in range(NB)]
        PARAM_ROWS += [(96, shm[:, 0:4, :]), (96, shm[:, 4:8, :]), (32, shl[:, :, :])]
        n_params = {}
        seq18 = lambda t: t.rearrange("p (b t) -> p b t", t=18)
        BON, M_I, M_S = cm["bones"], {0: cm["in64"], 1: cm["in16"]}, {0: cm["st64"], 1: cm["st16"]}
        
        raw_full = [sem("weights_loaded_0"), sem("weights_loaded_1")]
        hi_done, lo_done, blk_used = sem("hi_done"), sem("lo_done"), sem("blocks_used")
        proj_taken, stores = sem("proj_taken"), sem("stores")
        n_stores = [0]

        def store(eng, dst, src):
            eng.dma_start(dst, src).then_inc(stores, 16)
            n_stores[0] += 16

        def transpose(out, in_):
            n = in_.shape[0]
            return nc.tensor.transpose(out, in_, ident[0:n, 0:n])

        w_in = a["w_in"][0].rearrange("(h k p) c -> h p k c", h=2, p=P)
        w_ffn = a["w_ffn_in"][0].rearrange("(h k p) c -> h p k c", h=2, p=P)
        w_oab = [a["w_o_a"][0].rearrange("(k p) c -> p k c", p=P), a["w_o_b"][0].rearrange("(k p) c -> p k c", p=P)]
        w_out = a["w_out"][0].rearrange("(k p) (h c) -> k p h c", p=P, h=2)
        w_dn = a["w_ffn_down"][0].rearrange("(k p) (h c) -> k p h c", p=P, h=2)
        xp = a["x_prompt"][0].rearrange("(t p) c -> p t c", p=P)
        xs = a["x_sample"].rearrange("b s c -> (b s) c")
        vec = lambda n, lo_=0, n_=None: a[n][0][lo_:(lo_ + n_ if n_ else a[n].shape[1])].rearrange("(t p) -> t p", p=P)

        block = ctx.enter_context(nc.Block())

        OPEN = 1
        OPENED = ["y_out_done", "ol_done", "b_taken", "acc_part0", "acc_part1", "acc_taken", "ohd_done",
                  "gate_taken", "up_taken", "states_stored", "s_ps", "conv_done", "a_gated0", "a_gated1",
                  "silu_done", "act_hi"]

        E = sem
        LEVELS = ("lv2", "lv4", "lv8", "lv16", "lv32")
        units = lambda lv: range(6) if lv < 3 else range(4)
        unit_tok = lambda u: slice(256, 384) if u >= 4 else slice(128 * (u % 2), 128 * (u % 2) + 128)
        unit_head = lambda u: u - 4 if u >= 4 else u // 2
        g_bank = lambda lv: 6 if lv == 0 else 4
        heads = lambda i: slice(64 * i, 64 * i + 64)
        seq17 = lambda t: t.rearrange("p (b t) -> p b t", t=17)
        seq16 = lambda t: t.rearrange("p (b t) -> p b t", t=TS)
        bc = lambda m, n: m.unsqueeze(1).to_broadcast([P, n, P])

        def pe_rwkv(f, pieces):
            pe, mm_ = nc.tensor, nc.tensor.matmul
            pieces(1)
            pe.wait_ge(E("lora_w_in"), f * 48 + 48)
            mm_(ps[:, 2, 0:NT], wl[0:96, 0, :], za[0:96, 0, :], start=True, stop=True)
            mm_(ps[:, 3, 0:NT], wl[0:96, 1, :], za[0:96, 1, :], start=True, stop=True)
            for k in range(2):
                last = mm_(ps[:, 5, 0:NT], wg[:, k, :], za[:, 2 + k, :], start=k == 0, stop=k == 1)
            last.then_inc(E("lora_ps"), 1)
            pieces(1)
            pe.wait_ge(E("kk_sq_done"), f + 1)
            mm_(ps[:, 4, 0:NT], BON, sq[:, :], start=True, stop=True).then_inc(E("kk_sum_ps"), 1)
            pieces(2)
            pe.wait_ge(E("s0_in"), f * 32 + 32)
            pe.wait_ge(E("rk_done"), f + 1)
            mm_(ps[:, 6, 0:NT], BON, rk[:, :], start=True, stop=True).then_inc(E("rk_sum_ps"), 1)
            for b in range(NB):
                last = transpose(ps[:, 7, 64 * b:64 * b + 64], s0l[:, b, :])
            last.then_inc(E("s0_ps"), 1)
            pieces(4)
            pe.wait_ge(E("gates_done"), f + 1)
            pe.wait_ge(E("abkr_done"), f + 1)
            for i, src in enumerate((kp_, be)):
                for t in range(3):
                    transpose(ps[:, 2 + i, t * P:t * P + P], src[:, t * P:t * P + P])
            for t in range(3):
                last = transpose(ps[:, 4, t * P:t * P + P], z[:, 2, t * P:t * P + P])
            last.then_inc(E("tok_ps"), 1)
            pe.wait_ge(E("s0_done"), f + 1)
            for i in range(2):
                for b in range(NB):
                    last = mm_(ps[heads(i), 5, 16 * b:16 * b + 16], s0t[:, b, :],
                               al[:, i, 256 + 16 * b:272 + 16 * b], start=True, stop=True)
            last.then_inc(E("as_ps"), 1)
            pieces(1)
            pe.wait_ge(E("bonus_done"), f + 1)
            for u in range(6):
                last = mm_(unit(6, u), be[:, unit_tok(u)], al[:, unit_head(u), unit_tok(u)], start=True, stop=True)
            last.then_inc(E("nt_ps"), 1)
            pe.wait_ge(E("tok_done"), f + 1)
            pe.wait_ge(E("as_done"), f + 1)
            for u in range(6):
                last = mm_(unit(4, u), kp_[:, unit_tok(u)], al[:, unit_head(u), unit_tok(u)], start=True, stop=True)
            last.then_inc(E("mt_ps"), 1)
            pieces(1)
            pe.wait_ge(E("nt_done"), f + 1)
            for u in range(6):
                last = transpose(unit(2, u), n_t[:, u, :])
            last.then_inc(E("n_ps"), 1)
            pieces(3)
            for lv in range(5):
                pe.wait_ge(E("n_level_done"), f * 5 + (lv + 1))
                if lv == 0:
                    pe.wait_ge(E("t_first_done"), f + 1)
                else:
                    pe.wait_ge(E("t_done"), f * 5 + lv)
                for u in units(lv):
                    last = mm_(unit(g_bank(lv), u), (c_k, c_b)[lv % 2][:, u, :], t_x[:, u, :], start=True, stop=True)
                last.then_inc(E("g_ps"), 1)
                pieces(1)
                pe.wait_ge(E("g_done"), f * 5 + (lv + 1))
                if lv == 0:
                    pe.wait_ge(E("mt_done"), f + 1)
                if lv < 4:
                    for u in units(lv):
                        last = mm_(unit(10 - g_bank(lv), u), t_y[:, u, :], t_g[:, u, :], start=True, stop=True)
                for u in units(lv):
                    last = mm_(unit(2, u), t_g[:, u, :], t_y[:, u, :], start=True, stop=True)
                last.then_inc(E("dt_ps"), 1)
                pieces((2, 2, 2, 1, 1)[lv])
            pe.wait_ge(E("t_done"), f * 5 + 5)
            for b, src in ((4, kp_), (6, be)):
                for u in range(6):
                    last = mm_(unit(b, u), src[:, unit_tok(u)], rh[:, unit_head(u), unit_tok(u)],
                               start=True, stop=True)
                last.then_inc(E("c_ps"), 1)
            pieces(1)
            pe.wait_ge(E("c_done"), f * 2 + 2)

            v = tok[:, 2]
            for c in range(4):
                t, r0, cs = c // 2, 64 * (c % 2), slice(64 * (c % 2), 64 * (c % 2) + 64)
                cols = slice(64 * c, 64 * c + 64)
                if c:
                    pe.wait_ge(E("state_done"), f * 4 + c)
                for i in range(2):
                    last = mm_(ps[r0:r0 + 64, 2, heads(i)], m_t[:, 2 * i + t, cs], v[:, t, heads(i)],
                               start=True, stop=c == 0)
                    if c:
                        last = mm_(ps[r0:r0 + 64, 2, heads(i)], al[:, i, cols], st[:, 1, :], start=False, stop=True)
                last.then_inc(E("r_ps"), 1)
                if c == 0:
                    for i in range(2):
                        mm_(ps[:, 6, heads(i)], m_t[:, 4 + i, :], v[:, 2, heads(i)], start=True, stop=False)
                        last = mm_(ps[:, 6, heads(i)], asd[:, :], ident[:, heads(i)], start=False, stop=True)
                    last.then_inc(E("rd_ps"), 1)
                pieces(1)
                pe.wait_ge(E("r_done"), f * 4 + (c + 1))
                for i in range(2):
                    last = mm_(ps[r0:r0 + 64, 3, heads(i)], t_y[:, 2 * i + t, cs], rr[:, 0, heads(i)],
                               start=True, stop=True)
                last.then_inc(E("u_ps"), 1)
                if c == 0:
                    pe.wait_ge(E("rd_done"), f + 1)
                    for i in range(2):
                        last = mm_(ps[:, 7, heads(i)], t_y[:, 4 + i, :], rr[:, 1, heads(i)], start=True, stop=True)
                    last.then_inc(E("ud_ps"), 1)
                gain = [ps[heads(i), 4, 0:64] for i in range(2)]
                yo = [ps[heads(i), 5, cols] for i in range(2)]
                for i in range(2):
                    mm_(gain[i], tok[r0:r0 + 64, 0, t, heads(i)], v[r0:r0 + 64, t, heads(i)], start=True, stop=False)
                    mm_(yo[i], v[:, t, heads(i)], c_k[:, 2 * i + t, cs], start=True, stop=False)
                    if c:
                        mm_(yo[i], st[:, 1, :], rh[:, i, cols], start=False, stop=False)
                pe.wait_ge(E("u_done"), f * 4 + (c + 1))
                mm_(yo[0], un[:, 0, heads(0)], c_b[:, t, cs], start=False, stop=True)
                for i in range(2):
                    last = mm_(gain[i], tok[r0:r0 + 64, 1, t, heads(i)], un[r0:r0 + 64, 0, heads(i)],
                               start=False, stop=True)
                last.then_inc(E("state_ps"), 1)
                mm_(yo[1], un[:, 0, heads(1)], c_b[:, 2 + t, cs], start=False, stop=True).then_inc(E("y_ps"), 1)
                if c == 0:
                    pe.wait_ge(E("ud_done"), f + 1)
                    for i in range(2):
                        o = ps[heads(i), 5, 256:384]
                        mm_(o, v[:, 2, heads(i)], c_k[:, 4 + i, :], start=True, stop=False, skip_group_check=True)
                        mm_(o, un[:, 1, heads(i)], c_b[:, 4 + i, :], start=False, stop=False, skip_group_check=True)
                        for b in range(NB):
                            last = mm_(ps[heads(i), 5, 256 + 16 * b:272 + 16 * b], s0t[:, b, :],
                                       rh[:, i, 256 + 16 * b:272 + 16 * b], start=False, stop=b == NB - 1,
                                       skip_group_check=True)
                    last.then_inc(E("yd_ps"), 1)
                if c in (1, 2):
                    pe.wait_ge(E("vx_done"), f * 2 + c)
                    for i in range(2):
                        last = mm_(ps[heads(i), 6 + (c - 1), :], tok[:, c - 1, 2, heads(i)],
                                   vx[:, i].rearrange("p b v -> p (b v)"), start=True, stop=True)
                    last.then_inc(E("sd_ps"), 1)
            pe.wait_ge(E("state_done"), f * 4 + 4)
            pe.wait_ge(E("y_raw_done"), f + 1)
            mm_(ps[:, 3, 0:NT], BON, yb[:, :], start=True, stop=True).then_inc(E("mean_ps"), 1)
            transpose(ps[0:64, 2, 0:P], st[:, 0, :]).then_inc(E("sp_t_ps"), 1)
            pieces(1)
            pe.wait_ge(E("sd_done"), f + 1)
            pe.wait_ge(E("y_sq_done"), f + 1)
            mm_(ps[:, 4, 0:NT], BON, sq[:, :], start=True, stop=True).then_inc(E("var_ps"), 1)
            for b in range(NB):
                last = transpose(ps[0:64, 6 + b // 4, (b % 4) * P:(b % 4 + 1) * P], s0t[:, b, :])
            last.then_inc(E("sd_t_ps"), 1)

        def act_rwkv(f, cut, ch):
            act, fn = nc.scalar, nc.scalar.activation
            cut(0)
            act.wait_ge(E("lora_ps"), f + 1)
            act.wait_ge(E("pf_done"), f + 1)
            fn(sw[:, :], ps[:, 2, 0:NT], ACT.Sigmoid, bias=pf[:, 3:4])
            fn(aa[:, :], ps[:, 3, 0:NT], ACT.Sigmoid, bias=pf[:, 4:5])
            act.wait_ge(E("kk_raw_done"), f + 1)
            fn(sq[:, :], kk0[:, :], ACT.Square).then_inc(E("kk_sq_done"), 1)
            act.wait_ge(E("y_out_done"), OPEN + f)
            fn(gg[:, :], ps[:, 5, 0:NT], ACT.Copy).then_inc(E("gates_done"), 1)
            act.wait_ge(E("kk_clamped"), f + 1)
            ch.link(fn(rn[:, :], rn[:, :], ACT.Ln))
            ch.link(fn(rn[:, :], rn[:, :], ACT.Exp, scale=-0.5))
            act.wait_ge(E("decay_sums_done"), f + 1)
            fn(e1[:, :], cu[:, :], ACT.Exp, scale=-CDEC)
            fn(e2[:, :], cu[:, :], ACT.Exp, scale=CDEC)
            fn(e3[:, :], dx[:, :], ACT.Exp, scale=-CDEC)
            fn(emid[:, :, :], mid[:, :, :], ACT.Exp, scale=-CDEC).then_inc(E("exps_done"), 1)
            act.wait_ge(E("s0_ps"), f + 1)
            fn(s0t[:, :, :], ps[:, 7, :].rearrange("p (b v) -> p b v", b=NB), ACT.Copy).then_inc(E("s0_done"), 1)
            cut(1)
            act.wait_ge(E("tok_ps"), f + 1)
            fn(tok[:, :, :, :].rearrange("p a t c -> p a (t c)"), ps[:, 2:5, 0:NT], ACT.Copy)\
                .then_inc(E("tok_done"), 1)
            act.wait_ge(E("as_ps"), f + 1)
            fn(asd[:, :], ps[:, 5, 0:P], ACT.Copy).then_inc(E("as_done"), 1)
            cut(2)
            for lv in range(5):
                act.wait_ge(E("g_ps"), f * 5 + (lv + 1))
                n = len(units(lv))
                fn(t_g[:, 0:n, :], pair(g_bank(lv)).rearrange("p (u c) -> p u c", u=6)[:, 0:n, :], ACT.Copy)\
                    .then_inc(E("g_done"), 1)
                if lv != 3:
                    cut((3, 4, 5, 0, 6)[lv])
            act.wait_ge(E("rd_ps"), f + 1)
            fn(rr[:, 1, :], ps[:, 6, 0:P], ACT.Copy).then_inc(E("rd_done"), 1)
            cut(7)
            act.wait_ge(E("ud_ps"), f + 1)
            fn(un[:, 1, :], ps[:, 7, 0:P], ACT.Copy, scale=-1.0).then_inc(E("ud_done"), 1)
            act.wait_ge(E("yd_ps"), f + 1)
            act.wait_ge(E("y_ps"), f * 4 + 4)
            fn(yb[:, :], ps[:, 5, 0:NT], ACT.Copy).then_inc(E("y_raw_done"), 1)
            act.wait_ge(E("sp_t_ps"), f + 1)
            act.wait_ge(E("states_stored"), OPEN + f)
            fn(sto[:, :], ps[0:64, 2, 0:P], ACT.Copy).then_inc(E("s_out"), 1)
            act.wait_ge(E("y_centred"), f + 1)
            fn(sq[:, :], yc[:, :], ACT.Square).then_inc(E("y_sq_done"), 1)
            act.wait_ge(E("var_ps"), f + 1)
            ch.link(fn(rn[:, :], ps[:, 4, 0:NT], ACT.Ln, scale=1.0 / 64, bias=gneps))
            fn(rn[:, :], rn[:, :], ACT.Exp, scale=-0.5).then_inc(E("y_rstd_done"), 1)
            act.wait_ge(E("sd_t_ps"), f + 1)
            fn(so[:, :, :].rearrange("v (h b) c -> v h (b c)", h=2), ps[0:64, 6:8, :], ACT.Copy)\
                .then_inc(E("so_done"), 1)

        def dve_shift(f, ch):
            dve = nc.vector
            tt, stt3, cp = nc.vector.tensor_tensor, nc.vector.scalar_tensor_tensor, nc.vector.tensor_copy
            M, A, S = ALU.mult, ALU.add, ALU.subtract
            cp(pf[:, :], prm[:, 0:80].rearrange("p (g f) -> p g f", f=FT)[:, :, bass.ds(f, 1)].squeeze(2))\
                .then_inc(E("pf_done"), 1)
            ch.link(cp(pb[:, :, 257:PAD:17],
                    shm[:, :, :].rearrange("p b (i f) -> p i f b", f=FT)[:, :, bass.ds(f, 1), :].squeeze(2)))
            dve.wait_ge(E("pf_done"), f + 1)
            dve.wait_ge(proj_taken, f * 4 + (T_FT + 3))
            ch.link(tt(db[:, :, 0:PAD - 1], pb[:, :, 0:PAD - 1], pb[:, :, 1:PAD], S))
            for i in range(3):
                stt3(z[:, i, 0:NP_], db[:, i, 0:NP_], pf[:, i:i + 1], pb[:, i, 1:257], M, A)
                stt3(seq16(z[:, i, NP_:NT]), seq17(db[:, i, 257:PAD])[:, :, 0:TS], pf[:, i:i + 1],
                     seq17(pb[:, i, 257:PAD])[:, :, 1:17], M, A)
            col = lambda q, n: tail[:, q:q + n, :].rearrange("p q (i f) -> p q i f", f=FT)[:, :, :, bass.ds(f, 1)]
            cp(col(0, 1).squeeze(3).squeeze(1), pb[:, :, 256])
            cp(col(1, 8).squeeze(3), pb[:, :, 273:PAD:17].rearrange("p i b -> p b i")).then_inc(E("z_done"), 1)
            dve.wait_ge(E("z_done"), f + 1)
            nc.vector.tensor_scalar(kk0[:, :], z[:, 1, :], pf[:, 5:6], None, M).then_inc(E("kk_raw_done"), 1)

        def dve_rwkv(f, cut, ch, shift_next=True):
            dve = nc.vector
            tt, stt3, cp = nc.vector.tensor_tensor, nc.vector.scalar_tensor_tensor, nc.vector.tensor_copy
            M, A, S = ALU.mult, ALU.add, ALU.subtract
            link = ch.link
            zk, zv, zr = z[:, 1, :], z[:, 2, :], z[:, 0, :]
            cut(0)
            dve.wait_ge(E("gates_done"), f + 1)
            cp(pfl[:, :], pf[:, 8:10])
            link(nc.vector.tensor_tensor_scan(cu[:, :], reset, sw[:, :], 0.0, M, A))
            c4 = cu[:, 0:NP_].rearrange("p (c t) -> p c t", c=4)
            link(cp(mid[:, :, :], c4[:, :, 31:64:32]))
            link(tt(c4, c4, mid[:, :, 0:1].to_broadcast([P, 4, 64]), S))
            tt(dx[:, :], cu[:, :], sw[:, :], S).then_inc(E("decay_sums_done"), 1)
            dve.wait_ge(E("kk_sum_ps"), f + 1)
            nc.vector.tensor_scalar(rn[:, :], ps[:, 4, 0:NT], 1e-12, None, ALU.max).then_inc(E("kk_clamped"), 1)
            link(nc.vector.tensor_scalar(t1[:, :], aa[:, :], -1.0, pf[:, 6:7], A, M))
            link(stt3(k2[:, :], t1[:, :], 1.0, zk, A, M))
            stt3(rk[:, :], zr, pf[:, 7:8], k2[:, :], M, M).then_inc(E("rk_done"), 1)
            dve.wait_ge(E("exps_done"), f + 1)
            tt(kp_[:, :], k2[:, :], e2[:, :], M)
            link(tt(rn[:, :], kk0[:, :], rn[:, :], M))
            for i in range(2):
                h = heads(i)
                tt(al[h, i, :], rn[h, :], e3[h, :], M)
            link(tt(kka[:, :], rn[:, :], aa[:, :], M))
            tt(be[:, :], kka[:, :], e2[:, :], M).then_inc(E("abkr_done"), 1)
            cut(1)
            dve.wait_ge(E("rk_sum_ps"), f + 1)
            tt(rk[:, :], ps[:, 6, 0:NT], zv, M).then_inc(E("bonus_done"), 1)
            for i in range(2):
                tt(rh[heads(i), i, :], z[heads(i), 0, :], e1[heads(i), :], M)
            cut(2)
            u6 = lambda b, lo_, n: ps[:, b + lo_ // 4, 0:n * P].rearrange("p (u c) -> p u c", u=n)

            def masked(dst, b, masks):
                tt(dst[:, 0:4, :], u6(b, 0, 4), bc(masks[0], 4), M)
                return tt(dst[:, 4:6, :], u6(b, 4, 2), bc(masks[1], 2), M)
            dve.wait_ge(E("nt_ps"), f + 1)
            masked(n_t, 6, M_S).then_inc(E("nt_done"), 1)
            dve.wait_ge(E("nt_done"), f + 1)
            link(tt(t_y[:, :, :], n_t[:, :, :], bc(cm["nl1"], 6), M))
            link(tt(t_y[:, :, :], t_y[:, :, :], bc(ident, 6), A))
            dve.wait_ge(E("n_ps"), f + 1)
            link(masked(t_x, 2, (cm["nl1t"], cm["nl1t"])))
            tt(t_x[:, :, :], t_x[:, :, :], bc(ident, 6), A).then_inc(E("t_first_done"), 1)
            dve.wait_ge(E("t_first_done"), f + 1)
            dve.wait_ge(E("mt_ps"), f + 1)
            masked(m_t, 4, M_S).then_inc(E("mt_done"), 1)
            for lv in range(5):
                if lv in (0, 1, 3):
                    cut((3, 4, 0, 5)[lv])
                dve.wait_ge(E("dt_ps"), f * 5 + (lv + 1))
                for lo_, n in ((0, 4), (4, 2)) if lv < 3 else ((0, 4),):
                    if lv < 4:
                        tt(t_x[:, lo_:lo_ + n, :], t_x[:, lo_:lo_ + n, :], u6(10 - g_bank(lv), lo_, n), S)
                    last = tt(t_y[:, lo_:lo_ + n, :], t_y[:, lo_:lo_ + n, :], u6(2, lo_, n), S)
                last.then_inc(E("t_done"), 1)
                dve.wait_ge(E("t_done"), f * 5 + (lv + 1))
            cut(6)
            for j, (dst, b) in enumerate(((c_k, 4), (c_b, 6))):
                dve.wait_ge(E("c_ps"), f * 2 + (j + 1))
                masked(dst, b, M_I).then_inc(E("c_done"), 1)
            for c in range(4):
                r = slice(64 * (c % 2), 64 * (c % 2) + 64)
                dve.wait_ge(E("r_ps"), f * 4 + (c + 1))
                cp(rr[r, 0, :], ps[r, 2, 0:P]).then_inc(E("r_done"), 1)
                dve.wait_ge(E("u_ps"), f * 4 + (c + 1))
                nc.vector.tensor_scalar(un[r, 0, :], ps[r, 3, 0:P], -1.0, None, M).then_inc(E("u_done"), 1)
                dve.wait_ge(E("state_ps"), f * 4 + (c + 1))
                e_last = e1[:, 64 * c + 63:64 * c + 64]
                if c == 0:
                    link(nc.vector.tensor_scalar(st[:, 0, :], ps[:, 4, 0:64], e_last, None, M))
                elif c < 3:
                    link(stt3(st[:, 0, :], ps[:, 4, 0:64], e_last, st[:, 2, :], M, A))
                else:
                    stt3(st[:, 0, :], ps[:, 4, 0:64], e_last, st[:, 2, :], M, A).then_inc(E("state_done"), 1)
                if c < 3:
                    dve.wait_ge(E("y_ps"), f * 4 + (c + 1))
                    nc.vector.tensor_scalar(st[:, 2, :], st[:, 0, :], emid_tot(c + 1), None, M)
                    nc.vector.tensor_scalar(st[:, 1, :], st[:, 0, :], emid[:, c + 1, 0:1], None, M)\
                        .then_inc(E("state_done"), 1)
                    dve.wait_ge(E("state_done"), f * 4 + (c + 1))
                if c == 0:
                    cut(7)
                if c < 2:
                    if c == 0:
                        dve.wait_ge(E("tok_done"), f + 1)
                    else:
                        dve.wait_ge(E("ud_done"), f + 1)
                        dve.wait_ge(E("sd_ps"), f * 2 + 1)
                    src = tok[:, 2, 2, :] if c == 0 else un[:, 1, :]
                    for i in range(2):
                        last = tt(vx[:, i], src[:, heads(i)].unsqueeze(1).to_broadcast([P, NB, 64]),
                                  bmask.unsqueeze(2).to_broadcast([P, NB, 64]), M)
                    last.then_inc(E("vx_done"), 1)
            dve.wait_ge(E("yd_ps"), f + 1)
            dve.wait_ge(E("sd_ps"), f * 2 + 2)
            p3 = lambda b: ps[:, b, :].rearrange("p (b v) -> p b v", b=NB)
            link(tt(s0t[:, :, :], s0t[:, :, :], p3(6), A))
            link(tt(s0t[:, :, :], s0t[:, :, :], p3(7), A))
            tt(s0t[:, :, :], s0t[:, :, :],
               e1[:, 256 + TS - 1:NT:TS].unsqueeze(2).to_broadcast([P, NB, 64]), M).then_inc(E("sd_done"), 1)
            dve.wait_ge(E("mean_ps"), f + 1)
            stt3(yc[:, :], ps[:, 3, 0:NT], -1.0 / 64, yb[:, :], M, A).then_inc(E("y_centred"), 1)
            if shift_next:
                dve_shift(f + 1, ch)
            dve.wait_ge(E("y_rstd_done"), f + 1)
            dve.wait_ge(E("y_centred"), f + 1)
            link(tt(yc[:, :], yc[:, :], rn[:, :], M))
            link(nc.vector.tensor_scalar(yc[:, :], yc[:, :], pfl[:, 0:1], pfl[:, 1:2], M, A))
            link(tt(yc[:, :], yc[:, :], rk[:, :], A))
            tt(oa[:, bass.ds(f, 1), :].squeeze(1), yc[:, :], gg[:, :], M).then_inc(E("y_out_done"), 1)
            dve.wait_ge(E("y_out_done"), OPEN + f + 1)

        emid_tot = lambda c: emid[:, c, 1:2]
        def full(t):
            return 16 * t + 16 + 16 * min(max(t - (T_MLA + 3), 0), 5)

        def act_hi(t, s, cnt=None):
            nc.scalar.wait_ge(raw_full[s], full(t) if cnt is None else cnt)
            if not (isinstance(t, int) and t == 0):
                nc.scalar.wait_ge(blk_used, t * 2 + (s - 1))
            nc.scalar.activation(hi[:, s], raw[:, s], ACT.Copy).then_inc(hi_done, 1)

        def dve_lo(t, s):
            nc.vector.wait_ge(hi_done, t * 2 + (s + 1))
            nc.vector.tensor_tensor(lo[:, s], raw[:, s], hi[:, s].bitcast(F32), ALU.subtract).then_inc(lo_done, 1)

        def pe_block(t, s, out, ks=range(8), beside_norm=False):
            if ks[0] == 0:
                nc.tensor.wait_ge(lo_done, t * 2 + (s + 1))
            for k in ks:
                kt = 8 * s + k
                if beside_norm:
                    nc.tensor.wait_ge(E("xt_lo"), kt + 1)
                nc.tensor.matmul(out, hi[:, s, k, :], xh[:, kt, :], start=kt == 0, stop=False)
                nc.tensor.matmul(out, hi[:, s, k, :], xl[:, kt, :], start=False, stop=False)
                last = nc.tensor.matmul(out, lo[:, s, k, :], xh[:, kt, :], start=False, stop=kt == 15)
            if ks[-1] == 7:
                last.then_inc(blk_used, 1)

        def pe_half(t, s, xh_, xl_, out, ks=range(8)):
            if ks[0] == 0:
                nc.tensor.wait_ge(lo_done, t * 2 + (s + 1))
            for k in ks:
                nc.tensor.matmul(out, hi[:, s, k, :], xh_[:, k, :], start=k == 0, stop=False)
                nc.tensor.matmul(out, hi[:, s, k, :], xl_[:, k, :], start=False, stop=False)
                last = nc.tensor.matmul(out, lo[:, s, k, :], xh_[:, k, :], start=False, stop=k == 7)
            if ks[-1] == 7:
                last.then_inc(blk_used, 1)

        def pe_proj(t, p):
            if p >= 2:
                nc.tensor.wait_ge(proj_taken, p - 1)
            for s in range(2):
                pe_block(t, s, ps[:, p % 2, 0:NT])

        def act_next(t, end=False):
            static = isinstance(t, int)
            act_hi(t, 1, full(t) if static else t * 16 + 96)
            if not end:
                act_hi(t + 1, 0, full(t + 1) if static else t * 16 + 112)

        def dve_next(t, end=False):
            dve_lo(t, 1)
            if not end:
                dve_lo(t + 1, 0)

        def pe_norm(src, first, ready, taken):
            for kt in range(KD):
                bank = 2 + kt % 6
                if kt == 0:
                    nc.tensor.wait_ge(ready, 3)
                if kt >= 6:
                    nc.tensor.wait_ge(taken, first * KD + kt - 5)
                for t in range(3):
                    last = transpose(ps[:, bank, t * P:t * P + P], src[:, t, kt * P:kt * P + P])
                last.then_inc(E("norm_ps"), 1)

        def act_norm_stats(src, sq_out, arrived, ch):
            for t in range(3):
                arrived(t)
                nc.scalar.activation(sq_out, src[:, t, :], ACT.Square, accum_out=stat[:, t:t + 1])\
                    .then_inc(E("sum_sq"), 1)
                nc.scalar.wait_ge(E("sum_sq"), sumsq[0] + t + 1)
            sumsq[0] += 3
            ch.link(nc.scalar.activation(stat[:, 3:6], stat[:, 0:3], ACT.Ln, scale=1.0 / D, bias=epsb))
            nc.scalar.activation(stat[:, 0:3], stat[:, 3:6], ACT.Exp, scale=-0.5).then_inc(E("rstd_done"), 1)
        sumsq = [0]
        epsb, gneps = EPS, GN_EPS

        def act_norm(first, gcol):
            for kt in range(KD):
                nc.scalar.wait_ge(E("norm_ps"), first * KD + kt + 1)
                nc.scalar.activation(xh[:, kt, :], ps[:, 2 + kt % 6, 0:NT], ACT.Identity,
                                     scale=prm[:, gcol + kt:gcol + kt + 1]).then_inc(E("xh_done"), 1)

        def dve_norm(first, gcol):
            for kt in range(KD):
                nc.vector.wait_ge(E("xh_done"), first * KD + kt + 1)
                nc.vector.scalar_tensor_tensor(xl[:, kt, :], ps[:, 2 + kt % 6, 0:NT], prm[:, gcol + kt:gcol + kt + 1],
                                               xh[:, kt, :].bitcast(F32), ALU.mult, ALU.subtract)\
                    .then_inc(E("xt_lo"), 1)

        @block.sync
        def _(sp):
            def block_in(t, s, dst, src):
                sp.dma_start(dst, src).then_inc(raw_full[s], 16)

            def free(t, s):
                if not (isinstance(t, int) and t == 0):
                    sp.wait_ge(lo_done, t * 2 + (s - 1))

            def tile_in(t, src):
                for s in range(2):
                    free(t, s)
                    block_in(t, s, raw[:, s], src(s))

            sp.dma_start(c1[:, :], consts[:, 0:NC1]).then_inc(sem("c1_in"), 16)
            for t in range(3):
                sp.dma_start(xt[:, t, :], xp[:, t, :] if t < 2 else xs).then_inc(sem(f"x_in{t}"), 16)
            for j, c in enumerate((3072, 3168, 3264, 3392)):
                tile_in(T_LORA + j, lambda s: w_in[s][:, :, c:c + P])
            with sp.Fori(0, FT) as f:
                for q, (c, w) in enumerate(((0, P), (W, P), (2 * W, P), (Q0, 192))):
                    tile_in(T_FT + q + f * 4, lambda s: w_in[s][:, :, bass.ds(f * w + c, P)])
            for j in range(9):
                t = T_MLA + j
                for s in range(2):
                    free(t, s)
                    if j < 4:
                        c = CKV0 + j * P
                        block_in(t, s, raw[:, s], w_in[s][:, :, c:c + P])
                    else:
                        g0 = Q0 + 384 * (j - 4)
                        cols = (g0 + 128, g0 + 320) if j < 8 else (KR0, KR0)
                        for g, c in enumerate(cols):
                            block_in(t, s, raw[:, s, :, 64 * g:64 * g + 64], w_in[s][:, :, c:c + 64])
            for t0, g, w, j0, pairs in ((T_MIX, 0, 0, KD // 2, 4), (T_MIX + 12, 0, 0, 0, 4), (T_MIX_B, D, 1, 0, 8)):
                with sp.Fori(1, pairs + 1) as i1:
                    for q in range(2):
                        tile_in(i1 * 3 + (t0 + q - 3),
                                lambda s: w_in[s][:, :, bass.ds(i1 * (2 * P) + (G0 + g + (j0 + q - 2) * P), P)])
                    tile_in(i1 * 3 + (t0 - 1),
                            lambda s: w_oab[w][:, :, bass.ds(i1 * (2 * P) + (j0 + s - 2) * P, P)])

            def wide_tiles(t0, ch, count, w, row0):
                with sp.Fori(0, count) as i:
                    t = i + t0
                    for s in range(2):
                        free(t, s)
                        src = w[bass.ds(i * 2 + (row0 + s), 1), :, bass.ds(ch, 1), :].squeeze(2).squeeze(0)
                        sp.dma_start(raw[:, s].rearrange("p k c -> p (k c)"), src).then_inc(raw_full[s], 16)

            with sp.Fori(0, 2) as ch:
                wide_tiles(ch * 8 + T_OUT, ch, 8, w_out, 0)
            with sp.Fori(0, 2) as hf:
                with sp.Fori(0, HJ) as j:
                    for q in range(2):
                        tile_in(hf * T_HALF + j * 2 + (T_FFN + q),
                                lambda s: w_ffn[s][:, :, bass.ds(hf * (HJ * P) + j * P + q * DFF, P)])
                with sp.Fori(0, 2) as ch:
                    wide_tiles(hf * T_HALF + ch * 11 + (T_FFN + 2 * HJ), ch, 11, w_dn, hf * HJ)
            for t in range(3):
                sp.wait_ge(sem("y_ready"), t + 1)
                sp.dma_start(y_prompt[0].rearrange("(t p) c -> p t c", p=P)[:, t, :] if t < 2
                             else y_sample.rearrange("b s c -> (b s) c"), hn[:, t, :]).then_inc(sem("y_stored"), 16)
            sp.wait_ge(sem("y_stored"), 48)

        @block.gpsimd
        def _(pool):
            for name in OPENED:
                pool.sem_inc(sem(name), OPEN)
            n = {"norm_params_in": 0, "params_in": 0}

            def load(dst, src, seen="norm_params_in"):
                pool.dma_start(dst, src).then_inc(sem(seen), 16)
                n[seen] += 16
            load(rows[0:24, 0, :], vec("mu_shift", 0, 3072))
            for i, nm in enumerate(("w0", "a0", "k_k", "k_a")):
                load(rows[24 + 8 * i:32 + 8 * i, 0, :], vec(nm))
            load(rows[56:64, 0, :], a["r_k"][0].rearrange("(t h) n -> t (h n)", h=2))
            load(rows[64:72, 0, :], vec("lnx_g"))
            load(rows[72:80, 0, :], vec("lnx_b"))
            load(rows[80:96, 0, :], vec("g_mix"))
            load(rows[96:112, 0, :], vec("g_ffn"))
            for i, c in enumerate((3072, 3168, 3264, 3392)):
                load(rows[112 + i:113 + i, 0, :], vec("mu_shift", c, P))
            load(rows[116:120, 0, :], vec("g_kv"))
            for i, c in enumerate((3072, 3168, 3264, 3392)):
                load(rows[8 * i:8 * i + 8, 13, :], a["state_rwkv_shift"][0, :, 0, c:c + P], "params_in")
            load(rows[0:88, 1, :], a["conv_w"][0, 0:2, :].rearrange("j (t p) -> (j t) p", p=P), "params_in")
            load(rows[0:44, 2, :], a["conv_w"][0, 2, :].rearrange("(t p) -> t p", p=P), "params_in")
            load(rows[44:88, 2, :], vec("conv_b"), "params_in")
            for b in range(NB):
                load(rows[0:88, 3 + b, :], a["state_ffn_conv"][0, b].rearrange("r (t p) -> (r t) p", p=P),
                     "params_in")
                load(rows[24 * (b % 4):24 * (b % 4) + 24, 11 + b // 4, :],
                     a["state_rwkv_shift"][0, b, 0, 0:3072].rearrange("(t p) -> t p", p=P), "params_in")
            n_params.update(n)
            pool.dma_start(c2[:, :], consts[:, NC1:NC1 + NC2]).then_inc(sem("tables_in"), 16)

            def lora_in(f):
                for i, nm in enumerate(("w2", "a2")):
                    pool.dma_start(wl[0:96, i, :], a[nm][0][:, bass.ds(f * P, P)]).then_inc(sem("lora_w_in"), 16)
                pool.dma_start(wg[:, :, :], a["g2"][0].rearrange("(k p) c -> p k c", p=P)[:, :, bass.ds(f * P, P)])\
                    .then_inc(sem("lora_w_in"), 16)

            def s0_in(f):
                for i in range(2):
                    src = a["state_rwkv_wkv"][0].rearrange("b (f i) v k -> i f v b k", i=2)[i][bass.ds(f, 1)]
                    pool.dma_start(s0l[:, :, 64 * i:64 * i + 64], src.squeeze(0)).then_inc(sem("s0_in"), 16)

            pool.wait_ge(sem("xt_lo"), KD)
            lora_in(0)
            s0_in(0)

            def rwkv(f, last):
                pool.wait_ge(sem("nt_done"), f + 1)
                for lv, name in enumerate(LEVELS):
                    if lv >= 2:
                        pool.wait_ge(sem("g_ps"), f * 5 + (lv - 1))
                    n_u = len(units(lv))
                    nc.gpsimd.tensor_tensor((c_k, c_b)[lv % 2][:, 0:n_u, :], n_t[:, 0:n_u, :], bc(cm[name], n_u),
                                            ALU.mult).then_inc(sem("n_level_done"), 1)
                if not last:
                    pool.wait_ge(sem("gates_done"), f + 1)
                    lora_in(f + 1)
                    pool.wait_ge(sem("s0_done"), f + 1)
                    s0_in(f + 1)
                pool.wait_ge(sem("s_out"), f + 1)
                pool.wait_ge(sem("so_done"), f + 1)
                dst = wkv_s[0].rearrange("b (f i) v k -> i f v b k", i=2)
                dp = wkv_p[0, 0].rearrange("(f i) v k -> f v i k", i=2)
                one = lambda ap: ap[f] if last else ap[bass.ds(f, 1)].squeeze(0)
                for i in range(2):
                    pool.dma_start(one(dst[i]), so[:, :, 64 * i:64 * i + 64]).then_inc(sem("state_stores"), 16)
                pool.dma_start(one(dp), sto[:, :].rearrange("v (i k) -> v i k", i=2))\
                    .then_inc(sem("state_stores"), 16)
                pool.wait_ge(sem("state_stores"), f * 48 + 48)
                pool.sem_inc(sem("states_stored"), 1)

            pool.wait_ge(sem("tables_in"), 16)
            with pool.Fori(0, FT - 1) as f:
                rwkv(f, False)
            rwkv(FT - 1, True)

            pool.wait_ge(sem("y_out_done"), OPEN + FT)
            pool.dma_start(c3[:, :], consts[:, NC1 + NC2:NC1 + NC2 + NC3]).then_inc(sem("tables_in"), 16)
            w_ukv = a["w_ukv"][0].rearrange("(k p) c -> p k c", p=P)

            def head_in(i, hh):
                pool.dma_start(wuk[:, hh], w_ukv[:, :, bass.ds(i * 512 + 256 * hh, 256)])\
                    .then_inc(sem(f"wuk_in{hh}"), 16)

            def past_in(i, bb):
                b = i * 2 + bb
                one = lambda ap: ap[bass.ds(b, 1)].squeeze(0)
                pool.dma_start(lp[:, bb, :], one(a["cache_mla_latent"][0])).then_inc(sem(f"past_in{bb}"), 16)
                pool.dma_start(kpast[:, bb], one(a["cache_mla_krope"][0]).unsqueeze(1).to_broadcast([P, 2, 64]))\
                    .then_inc(sem(f"past_in{bb}"), 16)
                pool.dma_start(lnew[0:TS, bb, :], one(lat_s[0])).then_inc(sem(f"past_in{bb}"), 16)

            for hh in range(2):
                head_in(0, hh)
            pool.wait_ge(sem("latent_rows_done"), 1)
            store(pool, lat_p[0, 0].rearrange("(t p) c -> p t c", p=P), ltok[:, 0:2, :])
            pool.dma_start(lat_s[0].rearrange("b s c -> (b s) c"), ltok[:, 2, :]).then_inc(sem("new_latent_stored"), 16)
            store(pool, kr_p[0, 0].rearrange("(t p) c -> p t c", p=P), krt[:, 0:2, :])
            store(pool, kr_s[0].rearrange("b s c -> (b s) c"), krt[:, 2, :])
            pool.wait_ge(sem("new_latent_stored"), 16)
            pool.wait_ge(sem("latent_done"), 1)
            for bb in range(2):
                past_in(0, bb)
            with pool.Fori(0, 3) as i:
                for hh in range(2):
                    pool.wait_ge(sem("oh_ps"), i * 2 + (hh + 1))
                    head_in(i + 1, hh)
            def values_in(i, hh, half):
                pool.dma_start(wuk[:, hh, :, half * P:half * P + P],
                               w_ukv[:, :, bass.ds(i * 1024 + (512 * half + 256 * hh + P), P)])\
                    .then_inc(sem(f"wuk_in{hh}"), 16)

            for hh in range(2):
                pool.wait_ge(sem("oh_ps"), 7 + hh)
                for half in range(2):
                    values_in(0, hh, half)
            with pool.Fori(0, 3) as i:
                for bb in range(2):
                    pool.wait_ge(sem("old_ps"), i * 2 + (bb + 1))
                    past_in(i + 1, bb)
            for half in range(2):
                for hh in range(2):
                    pool.wait_ge(sem("ohd_ps"), 2 * half + hh + 1)
                    values_in(1, hh, half)
            pool.wait_ge(blk_used, 2 * T_OUT)
            for t in range(3):
                pool.dma_start(ht[:, t, :], xp[:, t, :] if t < 2 else xs).then_inc(sem("h_in"), 16)
            pool.wait_ge(sem("act_done"), 2 * HJ)
            pool.dma_start(gf[:, :], a["g_final"].partition_broadcast(P)).then_inc(sem("h_in"), 16)
            for q in range(9):
                if q in (0, 8):
                    pool.wait_ge(sem("tails_taken"), q // 8 + 1)
                dst = conv_p[0, 0] if q == 0 else conv_s[0, q - 1]
                store(pool, dst.rearrange("r (t p) -> (r t) p", p=P), ctr[:, q, :])
            shp, shs = shift_p[0, 0], shift_s[0, :, 0]
            for q in range(9):
                dst = (shp[0] if q == 0 else shs[q - 1])[0:3072].rearrange("(t p) -> t p", p=P)
                store(pool, dst, rowt[24 * (q % 3):24 * (q % 3) + 24, q // 3, :])
            for l, (c, w) in enumerate(((3072, 96), (3168, 96), (3264, P), (3392, P))):
                store(pool, shp[:, c:c + w], rowt[9 * l:9 * l + 1, 3, 0:w])
                store(pool, shs[:, c:c + w], rowt[9 * l + 1:9 * l + 9, 3, 0:w])
            pool.wait_ge(stores, n_stores[0])

        @block.tensor
        def _(pe):
            mm_ = nc.tensor.matmul
            def params_to_columns(which):
                for i in which:
                    r = PARAM_ROWS[i][0]
                    last = transpose(ps[:, 2 + i // 4, (i % 4) * P:(i % 4) * P + r], rows[0:r, i, :])
                last.then_inc(E("params_ps"), 1)

            pe.wait_ge(E("c1_in"), 16)
            pe.wait_ge(E("norm_params_in"), n_params["norm_params_in"])
            params_to_columns(range(1))
            pe.wait_ge(E("params_done"), 1)
            pe_norm(xt, 0, E("x_scaled"), E("xt_lo"))
            for s in range(2):
                pe_block(T_LORA, s, ps[:, 0, 0:NT], beside_norm=True)
            pe.wait_ge(E("params_in"), n_params["params_in"])
            params_to_columns(range(1, len(PARAM_ROWS)))
            for t in range(1, 4):
                pe_proj(T_LORA + t, t)
            pe.wait_ge(E("tables_in"), 16)
            for q in range(4):
                pe_proj(T_FT + q, 4 + q)
            pe.wait_ge(E("z_lora_done"), 4)
            pe.wait_ge(E("zeroed"), 1)

            with pe.Fori(0, FT - 1) as f:
                done = 0

                def pieces(n):
                    nonlocal done
                    for piece in range(done, done + n):
                        q, s, part = piece // 8, piece // 4 % 2, piece % 4
                        if piece % 8 == 0:
                            pe.wait_ge(proj_taken, f * 4 + (8 + q - 1))
                        pe_block(f * 4 + (T_FT + 4 + q), s, ps[:, q % 2, 0:NT], range(2 * part, 2 * part + 2))
                    done += n
                pe_rwkv(f, pieces)
                assert done == 32
            done = 0

            def last_pieces(n):
                nonlocal done
                for piece in range(done, done + n):
                    q, s, part = piece // 8, piece // 4 % 2, piece % 4
                    if piece % 8 == 0:
                        pe.wait_ge(proj_taken, T_MLA + q - 1)
                    pe_block(T_MLA + q, s, ps[:, (T_MLA + q) % 2, 0:NT], range(2 * part, 2 * part + 2))
                done += n
            pe_rwkv(FT - 1, last_pieces)

            def rotate(k):
                if k == 1:
                    pe.wait_ge(E("c_rstd_done"), 1)
                elif k > 1:
                    pe.wait_ge(E("rope_done"), k - 1)
                pe.wait_ge(proj_taken, T_MLA + 5 + k)
                mm_(ps[:, 6 + k % 2, 0:NT], rot, (kr2 if k == 4 else qrp[:, k])[:, :], start=True, stop=True)\
                    .then_inc(E("rot_ps"), 1)

            for j in range(4, 9):
                pe_proj(T_MLA + j, T_MLA + j)
                if j == 4:
                    pe.wait_ge(E("tables_in"), 32)
                    pe.wait_ge(E("y_out_done"), OPEN + FT)
                    pe.wait_ge(E("c_sq_done"), 1)
                    for k in range(4):
                        last = mm_(ps[:, 7, 0:NT], ones, csq[:, k, :], start=k == 0, stop=k == 3)
                    last.then_inc(E("c_sum_ps"), 1)
                else:
                    rotate(j - 5)
            pe.wait_ge(E("latent_done"), 1)
            for t in range(3):
                for j in range(4):
                    transpose(ps[:, 2 + t, j * P:j * P + P], latt[:, j, t * P:t * P + P])
            rotate(4)
            pe.wait_ge(E("rope_done"), 5)
            for t in range(3):
                last = transpose(ps[:, 5, t * P:t * P + P], kr2[:, t * P:t * P + P])
            last.then_inc(E("latent_rows_ps"), 1)

            def side(pair_no):
                done = 0

                def pieces(n):
                    nonlocal done
                    for piece in range(done, done + n):
                        b, part = piece // 4, piece % 4
                        t, q, s = pair_no * 3 + (T_MIX + b // 2), b // 2, b % 2
                        ks = range(2 * part, 2 * part + 2)
                        if q < 2:
                            if piece % 8 == 0:
                                pe.wait_ge(E(f"a_gated{q}"), OPEN + pair_no)
                            pe_block(t, s, ps[:, q, 0:NT], ks)
                        else:
                            if part == 0:
                                pe.wait_ge(proj_taken, pair_no * 2 + (T_MIX + s + 1))
                            pe_half(t, s, oah, oal, ps[:, s, 0:NT], ks)
                    done += n
                return pieces

            def prompt_head(i, hh, pieces):
                e = i * 2 + hh
                w = wuk[:, hh]
                pe.wait_ge(E(f"wuk_in{hh}"), i * 16 + 16)
                for kc in range(4):
                    last = transpose(ps[:, 2, kc * P:kc * P + P], w[:, kc, 0:P])
                last.then_inc(E("wk_ps"), 1)
                pieces(1)
                pe.wait_ge(E("wk_done"), e + 1)
                pe.wait_ge(E("ol_done"), OPEN + e)
                for kc in range(4):
                    last = mm_(ps[:, 3 + kc, 0:NT], wkt[:, kc * P:kc * P + P],
                               qn[:, bass.ds(e, 1), :].squeeze(1), start=True, stop=True)
                last.then_inc(E("ql_ps"), 1)
                pieces(2)
                pe.wait_ge(E("ql_done"), e + 1)
                h = heads(hh)
                for t, (c0, n) in enumerate(((0, P), (P, 2 * P))):
                    for kc in range(4):
                        mm_(ps[:, 7, c0:c0 + n], qlp[:, kc, t * P:t * P + P], latt[:, kc, 0:n],
                            start=kc == 0, stop=False)
                    last = mm_(ps[:, 7, c0:c0 + n], qrs[h, t * P:t * P + P], kr2[h, 0:n], start=False, stop=True)
                last.then_inc(E("s_ps"), 1)
                pieces(4)
                pe.wait_ge(E("p_done"), e + 1)
                for j in range(3):
                    last = transpose(ps[:, 2, j * P:j * P + P], pp[:, j * P:j * P + P])
                last.then_inc(E("pt_ps"), 1)
                pieces(1)
                pe.wait_ge(E("pt_done"), e + 1)
                o = ps[:, 3:5, :].rearrange("p a (k t) -> p (a k) t", k=2)
                for kc in range(4):
                    mm_(o[:, kc, 0:P], ltok[:, 0, kc * P:kc * P + P], ptt[:, 0, :], start=True, stop=True)
                    mm_(o[:, kc, P:2 * P], ltok[:, 0, kc * P:kc * P + P], ptt[:, 1, :], start=True, stop=False)
                    last = mm_(o[:, kc, P:2 * P], ltok[:, 1, kc * P:kc * P + P], ptt[:, 2, :], start=False, stop=True)
                last.then_inc(E("ol_ps"), 1)
                pieces(2)
                pe.wait_ge(E("ol_done"), OPEN + e + 1)
                for kc in range(4):
                    last = mm_(ps[:, 5, 0:NP_], w[:, kc, P:2 * P], ol[:, kc, :], start=kc == 0, stop=kc == 3)
                last.then_inc(E("oh_ps"), 1)
                pieces(2)
                pe.wait_ge(E("oh_done"), e + 1)

            pe.wait_ge(E("latent_rows_done"), 1)
            pe.wait_ge(E("oa_split"), FT)
            with pe.Fori(0, 4) as i:
                pieces = side(i)
                for hh in range(2):
                    prompt_head(i, hh, pieces)

            with pe.Fori(0, 4) as i:
                pieces = side(i + 4)
                for bb in range(2):
                    b = i * 2 + bb
                    pe.wait_ge(E(f"past_in{bb}"), i * 48 + 48)
                    for kc in range(4):
                        transpose(ps[:, 2, kc * P:kc * P + P], lp[:, bb, kc * P:kc * P + P])
                    transpose(ps[:, 3, 0:P], kpast[:, bb].rearrange("p r c -> p (r c)")).then_inc(E("lpt_ps"), 1)
                    pieces(3)
                    pe.wait_ge(E("lpt_done"), b + 1)
                    for kc in range(5):
                        k_ = lpt[:, kc, :] if kc < 4 else kpt[:, :]
                        mm_(ps[:, 4, 0:P], qb[:, kc, :], k_, start=kc == 0, stop=kc == 4)
                    for kc in range(5):
                        k_ = (latt[:, kc, :] if kc < 4 else kr2[:, :])[:, bass.ds(b * TS + NP_, TS)]
                        last = mm_(ps[:, 4, P:P + TS], qb[:, kc, :], k_, start=kc == 0, stop=kc == 4)
                    last.then_inc(E("sd_scores_ps"), 1)
                    pieces(4)
                    pe.wait_ge(E("pd_done"), b + 1)
                    transpose(ps[:, 5, 0:P], pd[:, 0:P])
                    transpose(ps[0:TS, 5, P:2 * P], pd[:, P:P + TS]).then_inc(E("pdt_ps"), 1)
                    pieces(2)
                    pe.wait_ge(E("pdt_done"), b + 1)
                    for kc in range(4):
                        mm_(ps[:, 6, kc * P:kc * P + P], lp[:, bb, kc * P:kc * P + P], pdt[:, :],
                            start=True, stop=False)
                        last = mm_(ps[:, 6, kc * P:kc * P + P], lnew[0:TS, bb, kc * P:kc * P + P], pdn[0:TS, :],
                                   start=False, stop=True)
                    last.then_inc(E("old_ps"), 1)
                    pieces(3)
                    pe.wait_ge(E("old_done"), b + 1)
            with pe.Fori(0, 2) as i:
                for half in range(2):
                    for hh in range(2):
                        e = i * 4 + (2 * half + hh)
                        if half == 0:
                            pe.wait_ge(E(f"wuk_in{hh}"), i * 32 + 96)
                        pe.wait_ge(E("ohd_done"), OPEN + e)
                        for kc in range(4):
                            last = mm_(ps[:, 7, 0:P], wuk[:, hh, kc, half * P:half * P + P],
                                       qld[:, kc, bass.ds(e, 1), :].squeeze(1), start=kc == 0, stop=kc == 3)
                        last.then_inc(E("ohd_ps"), 1)

            pe.wait_ge(E("a_gated0"), OPEN + KD // 2)
            pe.wait_ge(E("a_gated1"), OPEN + KD // 2)
            with pe.Fori(0, KD // 2) as i:
                for q in range(2):
                    pe.wait_ge(proj_taken, i * 2 + (T_MIX + KD + q - 1))
                    for s in range(2):
                        pe_block(i * 3 + (T_MIX_B + q), s, ps[:, q, 0:NT])
                pe.wait_ge(E("ob_split"), FT)
                for s in range(2):
                    pe.wait_ge(E("b_taken"), OPEN + i * 2)
                    pe_half(i * 3 + (T_MIX_B + 2), s, obh, obl, ps[:, 2 + s, 0:NT])

            def wide(t0, ch_no, kts, lh, ll):
                for kt in range(kts):
                    s = kt % 2
                    pe.wait_ge(lo_done, t0 * 2 + (kt + 1))
                    wh, wlo = (x[:, s].rearrange("p k c -> p (k c)") for x in (hi, lo))
                    for t in range(3):
                        if kt == 0:
                            pe.wait_ge(E(("acc_part0", "acc_part1", "acc_taken")[t]), OPEN + ch_no)
                        l_h, l_l = lh[:, kt, t * P:t * P + P], ll[:, kt, t * P:t * P + P]
                        for n, (l_, w_) in enumerate(((l_h, wh), (l_h, wlo), (l_l, wh))):
                            for cb in range(2):
                                last = mm_(ps[:, 2 + 2 * t + cb, :], l_, w_[:, 512 * cb:512 * cb + 512],
                                           start=kt == 0 and n == 0, stop=kt == kts - 1 and n == 2)
                    last.then_inc(blk_used, 1)

            pe.wait_ge(E("mix_done"), KD)
            with pe.Fori(0, 2) as ch:
                wide(ch * 8 + T_OUT, ch, 16, mh, ml)
            pe.wait_ge(E("acc_taken"), OPEN + 2)
            pe_norm(hn, 1, E("h_scaled"), E("xt_lo"))
            pe.wait_ge(E("xt_lo"), 2 * KD)
            for hf in range(2):
                with pe.Fori(0, HJ) as j:
                    for q in range(2):
                        t = j * 2 + (hf * T_HALF + T_FFN + q)
                        pe.wait_ge(E(("gate_taken", "up_taken")[q]), OPEN + j + hf * HJ)
                        for s in range(2):
                            pe_block(t, s, ps[:, q, 0:NT])
                pe.wait_ge(E("act_done"), hf * HJ + HJ)
                if hf == 0:
                    with pe.Fori(0, 2) as ch:
                        wide(ch * 11 + (T_FFN + 2 * HJ), ch + 2, HJ, ach, acl)
                    continue
                for q in range(8):
                    last = transpose(ps[0:88, q // 4, (q % 4) * P:(q % 4 + 1) * P],
                                     ctail[:, q].rearrange("p r j -> p (r j)"))
                last.then_inc(E("tails_ps"), 1)
                wide(T_HALF + T_FFN + 2 * HJ, 4, HJ, ach, acl)
                pe.wait_ge(E("tails_taken"), 1)
                transpose(ps[0:88, 0, 0:P], ctail[:, 8].rearrange("p r j -> p (r j)"))
                for g in range(3):
                    transpose(ps[0:72, 1, g * P:g * P + P], tail[:, 3 * g:3 * g + 3, :].rearrange("p q t -> p (q t)"))
                transpose(ps[0:36, 1, 3 * P:4 * P], taill[:, :, :].rearrange("p l q -> p (l q)"))\
                    .then_inc(E("tails_ps"), 1)
                wide(T_HALF + 11 + T_FFN + 2 * HJ, 5, HJ, ach, acl)

        @block.scalar
        def _(act):
            fn = nc.scalar.activation
            ch = Chain(nc.scalar, E("act_chain"))
            act_norm_stats(xt, junk[:, :], lambda t: act.wait_ge(E(f"x_in{t}"), 16), ch)
            def params_taken(which):
                for i in which:
                    r, dst = PARAM_ROWS[i]
                    src = ps[:, 2 + i // 4, (i % 4) * P:(i % 4) * P + r]
                    if len(dst.shape) == 3:
                        src = src.rearrange("p (a c) -> p a c", a=dst.shape[1])
                    last = fn(dst, src, ACT.Copy)
                last.then_inc(E("params_done"), 1)

            act.wait_ge(E("params_ps"), 1)
            params_taken(range(1))
            act.wait_ge(E("params_done"), 1)
            act_hi(0, 0)
            act_norm(0, 80)

            def taken(t, p, dst, sem_=proj_taken):
                act.wait_ge(blk_used, t * 2 + 2)
                fn(dst, ps[:, p % 2, 0:NT], ACT.Copy).then_inc(sem_, 1)

            def taken_pad(t, p, i):
                act.wait_ge(blk_used, t * 2 + 2)
                fn(pb[:, i, 1:257], ps[:, p % 2, 0:NP_], ACT.Copy)
                fn(seq17(pb[:, i, 257:PAD])[:, :, 1:17], seq16(ps[:, p % 2, NP_:NT]), ACT.Copy)\
                    .then_inc(proj_taken, 1)

            for t in range(4):
                act_next(t)
                if t == 0:
                    act.wait_ge(E("params_ps"), 2)
                    params_taken(range(1, len(PARAM_ROWS)))
                if t >= 2:
                    act.wait_ge(E("z_lora_done"), t - 1)
                taken_pad(t, t, t % 2)
                if t == 2:
                    act.wait_ge(E("z_lora_done"), 1)
                    fn(za[0:96, 0, :], za[0:96, 0, :], ACT.Tanh)
            act.wait_ge(E("z_lora_done"), 4)
            ch.link(fn(za[:, 2:4, :], za[:, 2:4, :], ACT.Sigmoid))
            for q in range(4):
                act_next(T_FT + q)
                if q < 3:
                    taken_pad(T_FT + q, q, q)

            def act_cut(f):
                def cut(k):
                    q, s = divmod(k, 2)
                    t = f * 4 + (T_FT + 4 + q)
                    if s == 0:
                        if q == 0:
                            taken(t - 1, 1, qn[:, bass.ds(f, 1), :].squeeze(1))
                        else:
                            if q == 1:
                                act.wait_ge(E("z_done"), f + 1)
                            taken_pad(t - 1, q - 1, q - 1)
                    if s == 0:
                        act_hi(t, 1, t * 16 + 16)
                    else:
                        act_hi(t + 1, 0, t * 16 + 32)
                return cut
            act.wait_ge(E("zeroed"), 1)
            with ch.loop(FT - 1, LINKS["act_rwkv"]) as f:
                act_rwkv(f, act_cut(f), ch)

            def last_cut(k):
                q, s = divmod(k, 2)
                t = T_MLA + q
                if k == 0:
                    taken(t - 1, 1, qn[:, FT - 1, :])
                elif s == 0:
                    if q == 1:
                        act.wait_ge(E("z_done"), FT)
                    taken(t - 1, t - 1, cc[:, q - 1])
                act_hi(t + s, 1 - s)
            act_rwkv(FT - 1, last_cut, ch)

            act_next(T_MLA + 4)
            act.wait_ge(E("y_out_done"), OPEN + FT)
            act.wait_ge(E("states_stored"), OPEN + FT)
            taken(T_MLA + 3, T_MLA + 3, cc[:, 3])
            act.wait_ge(proj_taken, T_MLA + 4)
            fn(csq[:, :, :], cc[:, :, :], ACT.Square).then_inc(E("c_sq_done"), 1)
            for j in range(4, 9):
                t = T_MLA + j
                if j > 4:
                    act_next(t)
                if j == 5:
                    act.wait_ge(E("c_sum_ps"), 1)
                    ch.link(fn(crs[:, :], ps[:, 7, 0:NT], ACT.Ln, scale=1.0 / LAT, bias=epsb))
                    fn(crs[:, :], crs[:, :], ACT.Exp, scale=-0.5).then_inc(E("c_rstd_done"), 1)
                for k in range((j - 4) * 2, (j - 3) * 2 if j < 8 else 8):
                    fn(oah[:, k, :], oa[:, k, :], ACT.Copy).then_inc(E("oah_done"), 1)
                taken(t, t, qrp[:, j - 4] if j < 8 else kr2[:, :])
            act.wait_ge(E("oa_split"), FT)
            act.wait_ge(E("latent_rows_ps"), 1)
            fn(ltok[:, :, :], ps[:, 2:5, :], ACT.Copy)
            fn(krt[:, :, :], ps[:, 5, 0:NT].rearrange("p (t c) -> p t c", t=3)[:, :, 0:64], ACT.Copy)\
                .then_inc(E("latent_rows_done"), 1)

            def side_cut(pair_no, k):
                b, s = divmod(k, 2)
                t = pair_no * 3 + (T_MIX + b)
                if s == 0:
                    act_hi(t, 1, t * 16 + 96)
                else:
                    act_hi(t + 1, 0, t * 16 + 112)

            def side_gate(pair_no, q, j):
                t = pair_no * 3 + (T_MIX + q)
                act.wait_ge(blk_used, t * 2 + 2)
                fn(ga[:, bass.ds(j, 1), :].squeeze(1), ps[:, q, 0:NT], ACT.Sigmoid).then_inc(proj_taken, 1)

            with ch.loop(4, 0) as i:
                for hh in range(2):
                    e = i * 2 + hh
                    act.wait_ge(E("wk_ps"), e + 1)
                    fn(wkt[:, :], ps[:, 2, :], ACT.Copy).then_inc(E("wk_done"), 1)
                    side_cut(i, 3 * hh)
                    if hh == 0:
                        act.wait_ge(E("s_ps"), OPEN + e)
                        fn(qrs[:, :], qrp[:, bass.ds(i, 1), 0:NP_].squeeze(1), ACT.Copy)
                    act.wait_ge(E("ql_ps"), e + 1)
                    act.wait_ge(E("qlp_done"), e + 1)
                    fn(qld[:, :, bass.ds(e, 1), :].squeeze(2), ps[:, 3:7, NP_:NT], ACT.Copy).then_inc(E("ql_done"), 1)
                    act.wait_ge(E("mx_done"), e + 1)
                    for t, (c0, n) in enumerate(((0, P), (P, 2 * P))):
                        last = fn(pp[:, c0:c0 + n], pp[:, c0:c0 + n], ACT.Exp, bias=msum[:, 2 + t:3 + t],
                                  accum_out=msum[:, 4 + t:5 + t])
                    last.then_inc(E("ex_done"), 1)
                    side_cut(i, 3 * hh + 1)
                    if hh == 1:
                        side_gate(i, 1, i * 2 + (KD // 2 + 1))
                    act.wait_ge(E("pt_ps"), e + 1)
                    fn(ptt[:, :, :], ps[:, 2, 0:NT].rearrange("p (j c) -> p j c", j=3), ACT.Copy)\
                        .then_inc(E("pt_done"), 1)
                    side_cut(i, 3 * hh + 2)
                    if hh == 0:
                        side_gate(i, 0, i * 2 + KD // 2)
                    act.wait_ge(E("oh_ps"), e + 1)
                    fn(ob[:, bass.ds(e, 1), 0:NP_].squeeze(1), ps[:, 5, 0:NP_], ACT.Copy).then_inc(E("oh_done"), 1)
            with ch.loop(4, 0) as i:
                for bb in range(2):
                    b = i * 2 + bb
                    act.wait_ge(E("lpt_ps"), b + 1)
                    fn(lpt[:, :, :].rearrange("p k c -> p (k c)"), ps[:, 2, :], ACT.Copy)
                    act.wait_ge(E("kpt_done"), b + 1)
                    fn(qb[:, 0:4, :].rearrange("p k (h t) -> p (k h) t", h=8),
                       qld[:, :, :, bass.ds(b * TS, TS)].rearrange("p k h t -> p (k h) t"), ACT.Copy)\
                        .then_inc(E("lpt_done"), 1)
                    side_cut(i + 4, 3 * bb)
                    act.wait_ge(E("mxd_done"), b + 1)
                    fn(pd[:, :], ps[:, 4, 0:P + TS], ACT.Exp, scale=SCALE, bias=dsum[:, 1:2], accum_out=dsum[:, 2:3])\
                        .then_inc(E("exd_done"), 1)
                    side_cut(i + 4, 3 * bb + 1)
                    if bb == 1:
                        side_gate(i + 4, 1, i * 2 + 1)
                    act.wait_ge(E("pdt_ps"), b + 1)
                    fn(pdt[:, :], ps[:, 5, 0:P], ACT.Copy)
                    fn(pdn[0:TS, :], ps[0:TS, 5, P:2 * P], ACT.Copy).then_inc(E("pdt_done"), 1)
                    side_cut(i + 4, 3 * bb + 2)
                    if bb == 0:
                        side_gate(i + 4, 0, i * 2)
            with ch.loop(4, 0) as i:
                for hh in range(2):
                    e = i * 2 + hh
                    act.wait_ge(E("ohd_ps"), e + 1)
                    fn(ob[:, bass.ds(e, 1), NP_:NT].squeeze(1), ps[:, 7, 0:P], ACT.Copy).then_inc(E("ohd_done"), 1)
            act_hi(T_MIX_B, 1)
            act.wait_ge(E("old_done"), NB)
            act.wait_ge(E("ohd_done"), OPEN + FT)
            for k in range(FT):
                fn(obh[:, k, :], ob[:, k, :], ACT.Copy).then_inc(E("obh_done"), 1)

            def mix_pair(i, last):
                t = i * 3 + T_MIX_B
                count = lambda blk: t * 16 + (96 + 16 * (blk // 2))
                for q in range(2):
                    for blk in (2 * q + 2, 2 * q + 3):
                        act_hi(t + blk // 2, blk % 2, count(blk))
                    act.wait_ge(blk_used, t * 2 + (2 * q + 2))
                    act.wait_ge(E("b_taken"), OPEN + i * 2)
                    fn(gab[:, q, :], ps[:, q, 0:NT], ACT.Sigmoid).then_inc(proj_taken, 1)
                for q in range(2):
                    if not (last and q == 1):
                        act_hi(t + 3, q, count(6))
                    act.wait_ge(E("mixed"), i * 2 + (q + 1))
                    dst = mh[:, i * 2 + q, :] if last else mh[:, bass.ds(i * 2 + q, 1), :].squeeze(1)
                    fn(dst, mm[:, q, :], ACT.Copy).then_inc(E("mix_hi"), 1)

            with ch.loop(KD // 2 - 1, 0) as i:
                mix_pair(i, False)
            mix_pair(KD // 2 - 1, True)

            def half_squares(n, c, t):
                passes = (0, 4)[n] + c
                act.wait_ge(E(("acc_part0", "acc_part1", "acc_taken")[t]), OPEN + passes + 1)
                act.wait_ge(E("sum_sq"), 3 + 6 * n + 3 * c + t)
                fn((hn[:, 0, 0:1024], jk2[:, :])[n], ht[:, t, 1024 * c:1024 * c + 1024], ACT.Square,
                   accum_out=hsum[:, 3 * c + t:3 * c + t + 1]).then_inc(E("sum_sq"), 1)

            def act_rstd(n):
                for t in range(3):
                    half_squares(n, 1, t)
                act.wait_ge(E("sum_sq_h"), n + 1)
                ch.link(fn(stat[:, 3:6], stat[:, 0:3], ACT.Ln, scale=1.0 / D, bias=epsb))
                fn(stat[:, 0:3], stat[:, 3:6], ACT.Exp, scale=-0.5).then_inc(E("rstd_done"), 1)

            with ch.loop(8, 0) as i:
                act_next(i + T_OUT)
            for i in range(3):
                act_next(T_OUT + 8 + i)
                half_squares(0, 0, i)
            with ch.loop(5, 0) as i:
                act_next(i + (T_OUT + 11))
            act_rstd(0)
            act_norm(1, 96)
            def act_leading(j, n):
                act.wait_ge(E("up_taken"), OPEN + n + 1)
                dst = ach[:, j, :] if isinstance(j, int) else ach[:, bass.ds(j, 1), :].squeeze(1)
                fn(dst, af[:, :], ACT.Copy).then_inc(E("act_hi"), 1)

            def ffn_act(hf, j, before):
                t, n = j * 2 + (hf * T_HALF + T_FFN), j + hf * HJ
                act_hi(t, 1, t * 16 + 96)
                if before:
                    act_leading(j - 1, n - 1)
                act_hi(t + 1, 0, t * 16 + 112)
                act_hi(t + 1, 1, t * 16 + 112)
                act.wait_ge(blk_used, t * 2 + 2)
                act.wait_ge(E("conv_done"), OPEN + n)
                fn(gp[:, 2:2 + NP_], ps[:, 0, 0:NP_], ACT.Copy)
                fn(seq18(gp[:, 2 + NP_:])[:, :, 2:18], seq16(ps[:, 0, NP_:NT]), ACT.Copy)\
                    .then_inc(E("gate_taken"), 1)
                act_hi(t + 2, 0, t * 16 + 128)
                act.wait_ge(E("conv_done"), OPEN + n + 1)
                act.wait_ge(E("up_taken"), OPEN + n)
                fn(sg[:, 0:400], cv[:, 0:400], ACT.Silu).then_inc(E("silu_done"), 1)

            for hf in range(2):
                ffn_act(hf, 0, False)
                with ch.loop(HJ - 1, 0) as i:
                    ffn_act(hf, i + 1, True)
                act_leading(HJ - 1, hf * HJ + HJ - 1)
                t0 = hf * T_HALF + T_FFN + 2 * HJ
                if hf == 0:
                    with ch.loop(22, 0) as i:
                        act_next(i + t0)
                    continue
                act_next(t0)
                act.wait_ge(E("tails_ps"), 1)
                fn(ctr[:, 0:8, :].rearrange("p (a q) c -> p a (q c)", a=2), ps[0:88, 0:2, :], ACT.Copy)\
                    .then_inc(E("tails_taken"), 1)
                with ch.loop(10, 0) as i:
                    act_next(i + (t0 + 1))
                for i in range(3):
                    act_next(t0 + 11 + i)
                    half_squares(1, 0, i)
                act.wait_ge(E("tails_ps"), 2)
                fn(ctr[:, 8, :], ps[0:88, 0, 0:P], ACT.Copy)
                fn(rowt[0:72, 0:3, :].rearrange("p g c -> p (g c)"), ps[0:72, 1, 0:3 * P], ACT.Copy)
                fn(rowt[0:36, 3, :], ps[0:36, 1, 3 * P:4 * P], ACT.Copy).then_inc(E("tails_taken"), 1)
                with ch.loop(7, 0) as i:
                    act_next(i + (t0 + 14))
                act_next(t0 + 21, end=True)
            act_rstd(1)

        @block.vector
        def _(dve):
            tt, stt3, cp, ts = (nc.vector.tensor_tensor, nc.vector.scalar_tensor_tensor, nc.vector.tensor_copy,
                                nc.vector.tensor_scalar)
            M, A, S = ALU.mult, ALU.add, ALU.subtract
            ch = Chain(nc.vector, E("dve_chain"))
            dve.wait_ge(E("rstd_done"), 1)
            for t in range(3):
                ts(xt[:, t, :], xt[:, t, :], stat[:, t:t + 1], None, M).then_inc(E("x_scaled"), 1)
            dve.wait_ge(E("params_done"), 1)
            dve_lo(0, 0)
            dve_norm(0, 80)
            dve.wait_ge(E("norm_ps"), KD)
            nc.vector.memset(pb[:, :, 0:1], 0.0)
            nc.vector.memset(rr[:, :, :], 0.0)
            nc.vector.memset(un[:, :, :], 0.0)
            nc.vector.memset(al[:, :, :], 0.0)
            nc.vector.memset(db[:, :, PAD - 1:PAD], 0.0)
            nc.vector.memset(rh[:, :, :], 0.0).then_inc(E("zeroed"), 1)
            dve.wait_ge(E("zeroed"), 1)
            for t in range(4):
                dve_next(t)
                if t == 0:
                    dve.wait_ge(E("params_done"), 2)
                i = t % 2
                ch.link(cp(pb[:, i, 257:PAD:17], shl[:, t, :]))
                dve.wait_ge(proj_taken, t + 1)
                ch.link(tt(db[:, i, 0:PAD - 1], pb[:, i, 0:PAD - 1], pb[:, i, 1:PAD], S))
                mu = prm[:, 112 + t:113 + t]
                stt3(za[:, t, 0:NP_], db[:, i, 0:NP_], mu, pb[:, i, 1:257], M, A)
                stt3(seq16(za[:, t, NP_:NT]), seq17(db[:, i, 257:PAD])[:, :, 0:TS], mu,
                     seq17(pb[:, i, 257:PAD])[:, :, 1:17], M, A)
                cp(taill[:, t, 0:1], pb[:, i, 256:257])
                cp(taill[:, t, 1:9], pb[:, i, 273:PAD:17]).then_inc(E("z_lora_done"), 1)
                dve.wait_ge(E("z_lora_done"), t + 1)
            for q in range(4):
                dve_next(T_FT + q)

            def dve_cut(f):
                def cut(k):
                    q, s = divmod(k, 2)
                    t = f * 4 + (T_FT + 4 + q)
                    dve_lo(t, 1) if s == 0 else dve_lo(t + 1, 0)
                return cut
            dve.wait_ge(E("tables_in"), 16)
            dve_shift(0, ch)
            with ch.loop(FT - 1, LINKS["dve_rwkv"]) as f:
                dve_rwkv(f, dve_cut(f), ch)
            dve_rwkv(FT - 1, dve_cut(FT - 1), ch, shift_next=False)

            def rope(k):
                x = kr2[:, :] if k == 4 else qrp[:, k]
                dve.wait_ge(E("rot_ps"), k + 1)
                tt(rtmp[:, k, :], ps[:, 6 + k % 2, 0:NT], sin, M)
                ch.link(tt(x, x, cos, M))
                tt(x, x, rtmp[:, k, :], A).then_inc(E("rope_done"), 1)

            for j in range(4, 9):
                dve_next(T_MLA + j)
                for k in range((j - 4) * 2, (j - 3) * 2 if j < 8 else 8):
                    dve.wait_ge(E("oah_done"), k + 1)
                    tt(oal[:, k, :], oa[:, k, :], oah[:, k, :].bitcast(F32), S).then_inc(E("oa_split"), 1)
                if j == 5:
                    dve.wait_ge(E("c_rstd_done"), 1)
                    for k in range(4):
                        last = stt3(latt[:, k, :], cc[:, k, :], prm[:, 116 + k:117 + k], crs[:, :], M, M)
                    last.then_inc(E("latent_done"), 1)
                    dve.wait_ge(E("tables_in"), 32)
                if j > 5:
                    rope(j - 6)
            rope(3)
            rope(4)

            def side_lo(pair_no, k):
                b, s = divmod(k, 2)
                t = pair_no * 3 + (T_MIX + b)
                dve_lo(t, 1) if s == 0 else dve_lo(t + 1, 0)

            def side_product(pair_no, q, j):
                dve.wait_ge(blk_used, pair_no * 6 + (2 * T_MIX + 4 + q + 1))
                g = ga[:, bass.ds(j, 1), :].squeeze(1)
                tt(g, ps[:, q, 0:NT], g, M).then_inc(E(f"a_gated{q}"), 1)

            with ch.loop(4, LINKS["dve_head"]) as i:
                for hh in range(2):
                    e = i * 2 + hh
                    dve.wait_ge(E("ql_ps"), e + 1)
                    cp(qlp[:, :, :], ps[:, 3:7, 0:NP_]).then_inc(E("qlp_done"), 1)
                    side_lo(i, 3 * hh)
                    dve.wait_ge(E("s_ps"), OPEN + e + 1)
                    ch.link(stt3(pp[:, :], ps[:, 7, 0:NT], SCALE, amask, M, A))
                    nc.vector.reduce_max(msum[:, 0:1], pp[:, 0:P], AX)
                    ch.link(nc.vector.reduce_max(msum[:, 1:2], pp[:, P:NT], AX))
                    ts(msum[:, 2:4], msum[:, 0:2], -1.0, None, M).then_inc(E("mx_done"), 1)
                    dve.wait_ge(E("ex_done"), e + 1)
                    ch.link(nc.vector.reciprocal(msum[:, 6:8], msum[:, 4:6]))
                    ts(pp[:, 0:P], pp[:, 0:P], msum[:, 6:7], None, M)
                    ts(pp[:, P:NT], pp[:, P:NT], msum[:, 7:8], None, M).then_inc(E("p_done"), 1)
                    side_lo(i, 3 * hh + 1)
                    dve.wait_ge(E("ol_ps"), e + 1)
                    cp(ol[:, :, :].rearrange("p (a k) t -> p a (k t)", a=2), ps[:, 3:5, :]).then_inc(E("ol_done"), 1)
                    if hh == 1:
                        side_product(i, 0, i * 2 + KD // 2)
                    side_lo(i, 3 * hh + 2)
                side_product(i, 1, i * 2 + (KD // 2 + 1))
            dve.wait_ge(E("oh_ps"), FT)
            ch.link(nc.vector.memset(qb[:, 4, :], 0.0))
            with ch.loop(4, LINKS["dve_seq"]) as i:
                for bb in range(2):
                    b = i * 2 + bb
                    dve.wait_ge(E("lpt_ps"), b + 1)
                    cp(kpt[:, :], ps[:, 3, 0:P])
                    for hh in range(2):
                        last = cp(qb[heads(hh), 4, :].rearrange("p (h t) -> p h t", h=8)[:, hh:8:2, :],
                                  qrp[heads(hh), :, bass.ds(b * TS + NP_, TS)])
                    last.then_inc(E("kpt_done"), 1)
                    side_lo(i + 4, 3 * bb)
                    dve.wait_ge(E("sd_scores_ps"), b + 1)
                    ch.link(nc.vector.reduce_max(dsum[:, 0:1], ps[:, 4, 0:P + TS], AX))
                    ts(dsum[:, 1:2], dsum[:, 0:1], -SCALE, None, M).then_inc(E("mxd_done"), 1)
                    dve.wait_ge(E("exd_done"), b + 1)
                    ch.link(nc.vector.reciprocal(dsum[:, 3:4], dsum[:, 2:3]))
                    ts(pd[:, :], pd[:, :], dsum[:, 3:4], None, M).then_inc(E("pd_done"), 1)
                    side_lo(i + 4, 3 * bb + 1)
                    dve.wait_ge(E("old_ps"), b + 1)
                    cp(qld[:, :, :, bass.ds(b * TS, TS)].rearrange("p k h t -> p (k h) t"),
                       ps[:, 6, :].rearrange("p (k t) -> p k t", t=TS)).then_inc(E("old_done"), 1)
                    if bb == 1:
                        side_product(i + 4, 0, i * 2)
                    side_lo(i + 4, 3 * bb + 2)
                side_product(i + 4, 1, i * 2 + 1)
            dve_lo(T_MIX_B, 1)
            for k in range(FT):
                dve.wait_ge(E("obh_done"), k + 1)
                tt(obl[:, k, :], ob[:, k, :], obh[:, k, :].bitcast(F32), S).then_inc(E("ob_split"), 1)

            def mix_pair(i, last):
                t = i * 3 + T_MIX_B
                tile_of = lambda x, j: x[:, j, :] if last else x[:, bass.ds(j, 1), :].squeeze(1)
                for blk in range(2, 6):
                    dve_lo(t + blk // 2, blk % 2)
                for q in range(2):
                    if not (last and q == 1):
                        dve_lo(t + 3, q)
                    j = i * 2 + q
                    dve.wait_ge(proj_taken, j + (T_MIX + KD + 1))
                    dve.wait_ge(blk_used, t * 2 + (5 + q))
                    tt(mm[:, q, :], ps[:, 2 + q, 0:NT], gab[:, q, :], M).then_inc(E("b_taken"), 1)
                    dve.wait_ge(E("b_taken"), OPEN + j + 1)
                    tt(mm[:, q, :], mm[:, q, :], tile_of(ga, j), A).then_inc(E("mixed"), 1)
                    dve.wait_ge(E("mix_hi"), j + 1)
                    tt(tile_of(ml, j), mm[:, q, :], tile_of(mh, j).bitcast(F32), S).then_inc(E("mix_done"), 1)

            with ch.loop(KD // 2 - 1, 0) as i:
                mix_pair(i, False)
            mix_pair(KD // 2 - 1, True)

            def add_acc(c, need, done):
                dve.wait_ge(E("acc_taken"), OPEN + done)
                dve.wait_ge(blk_used, need)
                for t in range(3):
                    for cb in range(2):
                        dst = ht[:, t, bass.ds(c * 1024 + 512 * cb, 512)]
                        last = tt(dst, dst, ps[:, 2 + 2 * t + cb, :], A)
                    last.then_inc(E(("acc_part0", "acc_part1", "acc_taken")[t]), 1)

            def add_half_sums(n):
                dve.wait_ge(E("sum_sq"), 3 + 6 * n + 6)
                tt(stat[:, 0:3], hsum[:, 0:3], hsum[:, 3:6], A).then_inc(E("sum_sq_h"), 1)

            with ch.loop(2, 0) as c:
                with ch.loop(8, 0) as i:
                    dve_next(c * 8 + i + T_OUT)
                dve.wait_ge(E("h_in"), 48)
                add_acc(c, c * 16 + (2 * T_OUT + 16), c)
            dve.wait_ge(E("acc_taken"), OPEN + 2)
            add_half_sums(0)
            dve.wait_ge(E("rstd_done"), 2)
            for t in range(3):
                ts(hn[:, t, :], ht[:, t, :], stat[:, t:t + 1], None, M).then_inc(E("h_scaled"), 1)
            dve_norm(1, 96)
            dve.wait_ge(E("xt_lo"), 2 * KD)
            ch.link(nc.vector.memset(gp[:, 0:2], 0.0))
            def gated(j, n, t):
                dve.wait_ge(E("silu_done"), OPEN + n + 1)
                dve.wait_ge(blk_used, t * 2 + 4)
                dve.wait_ge(E("act_hi"), OPEN + n)
                tt(af[:, 0:NP_], sg[:, 0:NP_], ps[:, 1, 0:NP_], M)
                tt(seq16(af[:, NP_:NT]), seq18(sg[:, 2 + NP_:])[:, :, 0:TS], seq16(ps[:, 1, NP_:NT]), M)\
                    .then_inc(E("up_taken"), 1)

            def act_rest(j, n):
                tile = lambda x: x[:, j, :] if isinstance(j, int) else x[:, bass.ds(j, 1), :].squeeze(1)
                dve.wait_ge(E("act_hi"), OPEN + n + 1)
                dve.wait_ge(E("up_taken"), OPEN + n + 1)
                tt(tile(acl), af[:, :], tile(ach).bitcast(F32), S).then_inc(E("act_done"), 1)

            def ffn_dve(hf, j, before):
                t, n = j * 2 + (hf * T_HALF + T_FFN), j + hf * HJ
                tap = lambda q: cprm[:, q, n:n + 1] if isinstance(n, int) else cprm[:, q, bass.ds(n, 1)]
                dve_lo(t, 1)
                if before:
                    gated(j - 1, n - 1, t - 2)
                dve_lo(t + 1, 0)
                if before:
                    act_rest(j - 1, n - 1)
                ch.link(cp(seq18(gp[:, 2 + NP_:])[:, :, 0:2], cprev[:, :, :, bass.ds(n, 1)].squeeze(3)))
                dve_lo(t + 1, 1)
                dve.wait_ge(E("gate_taken"), OPEN + n + 1)
                dve.wait_ge(E("silu_done"), OPEN + n)
                ch.link(ts(cv[:, 0:400], gp[:, 2:402], tap(2), tap(3), M, A))
                ch.link(stt3(cv[:, 0:400], gp[:, 1:401], tap(1), cv[:, 0:400], M, A))
                cp(ctail[:, 0, :, bass.ds(n, 1)].squeeze(2), gp[:, NP_:NP_ + 2])
                cp(ctail[:, 1:9, :, bass.ds(n, 1)].squeeze(3), seq18(gp[:, 2 + NP_:])[:, :, 16:18])
                stt3(cv[:, 0:400], gp[:, 0:400], tap(0), cv[:, 0:400], M, A).then_inc(E("conv_done"), 1)
                dve_lo(t + 2, 0)

            for hf in range(2):
                ffn_dve(hf, 0, False)
                with ch.loop(HJ - 1, LINKS["dve_ffn"]) as i:
                    ffn_dve(hf, i + 1, True)
                gated(HJ - 1, hf * HJ + HJ - 1, hf * T_HALF + T_FFN + 2 * HJ - 2)
                act_rest(HJ - 1, hf * HJ + HJ - 1)
                for c in range(2):
                    t0 = hf * T_HALF + c * 11 + T_FFN + 2 * HJ
                    end = hf == 1 and c == 1
                    with ch.loop(10 if end else 11, 0) as i:
                        dve_next(i + t0)
                    if end:
                        dve_next(t0 + 10, end=True)
                    add_acc(c, (t0 + 11) * 2, 2 * hf + c + 2)
            dve.wait_ge(E("acc_taken"), OPEN + 6)
            add_half_sums(1)
            dve.wait_ge(E("rstd_done"), 3)
            dve.wait_ge(E("h_in"), 64)
            for t in range(3):
                stt3(hn[:, t, :], ht[:, t, :], stat[:, t:t + 1], gf[:, :], M, M).then_inc(E("y_ready"), 1)


LINKS = {"act_rwkv": 3, "dve_rwkv": 20, "dve_head": 6, "dve_seq": 4, "dve_ffn": 3}

_INS = ["x_prompt", "x_sample", "cache_mla_latent", "cache_mla_krope", "state_rwkv_wkv", "state_rwkv_shift",
        "state_ffn_conv", "g_mix", "w_in", "mu_shift", "w0", "w2", "a0", "a2", "g2", "k_k", "k_a", "r_k", "lnx_g",
        "lnx_b", "w_o_a", "g_kv", "w_ukv", "w_o_b", "w_out", "g_ffn", "w_ffn_in", "conv_w", "conv_b", "w_ffn_down",
        "g_final"]
_OUTS = [(1, 256, D), (8, 16, D), (1, 1, 256, LAT), (1, 1, 256, 64), (1, 1, 16, 64, 64), (1, 1, 1, RW),
         (1, 1, 2, DFF), (1, 8, 16, LAT), (1, 8, 16, 64), (1, 8, 16, 64, 64), (1, 8, 1, RW), (1, 8, 2, DFF)]


def kernel(**inputs):
    import numpy as _np
    import concourse.bacc as _bacc
    from concourse.bass_utils import run_bass_kernel_spmd as _run

    nc = _bacc.Bacc("TRN2", target_bir_lowering=False, num_devices=1)
    arrays, aps = {}, {}
    for name in _INS:
        x = _np.ascontiguousarray(inputs[name])
        arrays[f"in_{name}"] = x
        aps[name] = nc.dram_tensor(f"in_{name}", x.shape, mybir.dt.from_np(x.dtype), kind="ExternalInput").ap()
    arrays["shape_consts"] = constants()
    consts = nc.dram_tensor("shape_consts", arrays["shape_consts"].shape, F32, kind="ExternalInput").ap()
    outs = [nc.dram_tensor(f"out_{i}", s, F32, kind="ExternalOutput").ap() for i, s in enumerate(_OUTS)]
    build(nc, aps, consts, outs)
    r = _run(nc, [arrays], core_ids=[0])
    return tuple(r.results[0][f"out_{i}"] for i in range(len(_OUTS)))
```
